# Optimizing a Trainium2 kernel written in Bass

```python
import math
import jax, jax.numpy as jnp
from jax import lax
import numpy as np

D_MODEL = 1024
BATCH = 1
SEQ = 1024
DEPTH = 1

N_MEM = 256
CONV_WIDTH = D_MODEL // 2
CONV_KSIZE = 31
ATT_PATTERNS = ((128, 1), (512, 4), (2048, 16))
N_GROUPS = len(ATT_PATTERNS)
HEADS_PER_GROUP = 4
ATT_HEAD_DIM = D_MODEL // 16
N_ATT_HEADS = N_GROUPS * HEADS_PER_GROUP
ATT_WIDTH = N_ATT_HEADS * ATT_HEAD_DIM
ATT_OUT_WIDTH = HEADS_PER_GROUP * ATT_HEAD_DIM
MEM_HEADS = 4
MEM_HEAD_DIM = D_MODEL // 8
MEM_WIDTH = MEM_HEADS * MEM_HEAD_DIM
N_BRANCHES = 3
IN_WIDTH = 2 * CONV_WIDTH + 3 * ATT_WIDTH + MEM_WIDTH + N_BRANCHES * D_MODEL
FFN_HIDDEN = -(-(8 * D_MODEL) // (3 * 256)) * 256
NUM_BUCKETS = 32
MAX_DISTANCE = 1024
RMS_EPS = 1e-6
LN_EPS = 1e-5
NEG_INF = -1e30

kernel_name = "hybrid_gated_conv_dilated_memory_encoder"

def _rms_norm(x, g):
    xf = x.astype(jnp.float32)
    y = xf * lax.rsqrt(jnp.mean(xf * xf, axis=-1, keepdims=True) + RMS_EPS)
    return (y * g.astype(jnp.float32)).astype(x.dtype)

def _layer_norm(x, g, b):
    xf = x.astype(jnp.float32)
    mu = jnp.mean(xf, axis=-1, keepdims=True)
    xc = xf - mu
    y = xc * lax.rsqrt(jnp.mean(xc * xc, axis=-1, keepdims=True) + LN_EPS)
    return (y * g.astype(jnp.float32) + b.astype(jnp.float32)).astype(x.dtype)

def _t5_bucket(rel):
    nb = NUM_BUCKETS // 2
    max_exact = nb // 2
    ret = jnp.where(rel > 0, nb, 0)
    n = jnp.abs(rel)
    nf = jnp.maximum(n, 1).astype(jnp.float32)
    large = max_exact + (jnp.log(nf / max_exact) / math.log(MAX_DISTANCE / max_exact)
                         * (nb - max_exact)).astype(jnp.int32)
    large = jnp.minimum(large, nb - 1)
    return ret + jnp.where(n < max_exact, n, large)

def _dilated_group(q, k, v, bias_tab, dilation, radius):
    B, S, H, E = q.shape
    blk = radius
    unit = dilation * blk
    sp = -(-S // unit) * unit
    L = sp // dilation
    nb = L // blk

    def to_blocks(t):
        t = jnp.pad(t, ((0, 0), (0, sp - S), (0, 0), (0, 0)))
        t = t.reshape(B, L, dilation, H, E).transpose(0, 2, 1, 3, 4)
        return t.reshape(B, dilation, nb, blk, H, E)

    def band_keys(t):
        tp = jnp.pad(t, ((0, 0), (0, 0), (1, 1), (0, 0), (0, 0), (0, 0)))
        return jnp.concatenate([tp[:, :, :-2], tp[:, :, 1:-1], tp[:, :, 2:]], axis=3)

    qb = to_blocks(q)
    kb = band_keys(to_blocks(k))
    vb = band_keys(to_blocks(v))
    valid = (jnp.arange(sp) < S).reshape(L, dilation).T.reshape(dilation, nb, blk)
    vp = jnp.pad(valid, ((0, 0), (1, 1), (0, 0)))
    kvalid = jnp.concatenate([vp[:, :-2], vp[:, 1:-1], vp[:, 2:]], axis=2)

    s = jnp.einsum('brnqhe,brnkhe->brnhqk', qb, kb).astype(jnp.float32) * (E ** -0.5)
    off = jnp.arange(3 * blk)[None, :] - blk - jnp.arange(blk)[:, None]
    band = jnp.abs(off) <= radius
    bias = bias_tab[_t5_bucket(off * dilation)].transpose(2, 0, 1).astype(jnp.float32)
    mask = band & kvalid[:, :, None, None, :]
    s = jnp.where(mask, s + bias, NEG_INF)
    m = jnp.max(s, axis=-1, keepdims=True)
    e = jnp.exp(s - m)
    den = jnp.sum(e, axis=-1, keepdims=True)
    lse = (m + jnp.log(den))[..., 0]
    o = jnp.einsum('brnhqk,brnkhe->brnqhe', (e / den).astype(v.dtype), vb)

    def from_blocks(t):
        tail = t.shape[4:]
        t = t.reshape(B, dilation, L, *tail).swapaxes(1, 2).reshape(B, sp, *tail)
        return t[:, :S]

    return from_blocks(o), from_blocks(lse.transpose(0, 1, 2, 4, 3))

def _dilated_attention(att_in, rel_bias):
    B, S, _ = att_in.shape
    qkv = att_in.reshape(B, S, 3, N_GROUPS, HEADS_PER_GROUP, ATT_HEAD_DIM)
    outs, lses = [], []
    for g, (window, dilation) in enumerate(ATT_PATTERNS):
        radius = window // (2 * dilation)
        tab = rel_bias[:, g * HEADS_PER_GROUP:(g + 1) * HEADS_PER_GROUP]
        o, l = _dilated_group(qkv[:, :, 0, g], qkv[:, :, 1, g], qkv[:, :, 2, g], tab, dilation, radius)
        outs.append(o)
        lses.append(l)
    w = jax.nn.softmax(jnp.stack(lses, axis=0), axis=0)
    o = jnp.sum(w[..., None].astype(outs[0].dtype) * jnp.stack(outs, axis=0), axis=0)
    return o.reshape(B, S, ATT_OUT_WIDTH)

def _conv_module(u, w_dw, b_dw, ln_g, ln_b, w_o):
    a, gt = jnp.split(u, 2, axis=-1)
    u = a * jax.nn.sigmoid(gt)
    pad = CONV_KSIZE // 2
    y = lax.conv_general_dilated(u, w_dw[:, None, :], window_strides=(1,), padding=((pad, pad),),
                                 dimension_numbers=('NWC', 'WIO', 'NWC'),
                                 feature_group_count=CONV_WIDTH) + b_dw
    y = jax.nn.silu(_layer_norm(y, ln_g, ln_b))
    return y @ w_o

def _memory_attention(q_in, mem, g_mem, w_kv, w_o):
    B, S, _ = q_in.shape
    M = mem.shape[1]
    q = q_in.reshape(B, S, MEM_HEADS, MEM_HEAD_DIM)
    kv = (_rms_norm(mem, g_mem) @ w_kv).reshape(B, M, 2, MEM_HEADS, MEM_HEAD_DIM)
    k, v = kv[:, :, 0], kv[:, :, 1]
    s = jnp.einsum('bshe,bmhe->bhsm', q, k).astype(jnp.float32) * (MEM_HEAD_DIM ** -0.5)
    p = jax.nn.softmax(s, axis=-1).astype(v.dtype)
    o = jnp.einsum('bhsm,bmhe->bshe', p, v).reshape(B, S, MEM_WIDTH)
    return o @ w_o

def setup_inputs(seed: int = 0) -> dict:
    key = jax.random.key(seed)
    ks = jax.random.split(key, 24)
    f32 = jnp.float32

    def nrm(k, shape, scale):
        return jax.random.normal(k, shape, f32) * scale

    def gain(k, shape):
        return 1.0 + 0.05 * jax.random.normal(k, shape, f32)

    return {
        "x": jax.random.normal(ks[0], (BATCH, SEQ, D_MODEL), f32),
        "mem": jax.random.normal(ks[1], (BATCH, N_MEM, D_MODEL), f32),
        "rel_bias": nrm(ks[2], (NUM_BUCKETS, N_ATT_HEADS), 0.5),
        "norm_mix_pre": gain(ks[3], (DEPTH, D_MODEL)),
        "w_in": nrm(ks[4], (DEPTH, D_MODEL, IN_WIDTH), D_MODEL ** -0.5),
        "b_gate": nrm(ks[5], (DEPTH, N_BRANCHES * D_MODEL), 0.01),
        "conv_dw": nrm(ks[6], (DEPTH, CONV_KSIZE, CONV_WIDTH), CONV_KSIZE ** -0.5),
        "conv_dw_bias": nrm(ks[7], (DEPTH, CONV_WIDTH), 0.02),
        "conv_ln_g": gain(ks[8], (DEPTH, CONV_WIDTH)),
        "conv_ln_b": nrm(ks[9], (DEPTH, CONV_WIDTH), 0.02),
        "w_conv_out": nrm(ks[10], (DEPTH, CONV_WIDTH, D_MODEL), CONV_WIDTH ** -0.5),
        "w_att_out": nrm(ks[11], (DEPTH, ATT_OUT_WIDTH, D_MODEL), ATT_OUT_WIDTH ** -0.5),
        "norm_mem": gain(ks[12], (DEPTH, D_MODEL)),
        "w_mem_kv": nrm(ks[13], (DEPTH, D_MODEL, 2 * MEM_WIDTH), D_MODEL ** -0.5),
        "w_mem_out": nrm(ks[14], (DEPTH, MEM_WIDTH, D_MODEL), MEM_WIDTH ** -0.5),
        "w_out": nrm(ks[15], (DEPTH, D_MODEL, D_MODEL), D_MODEL ** -0.5),
        "norm_mix_post": gain(ks[16], (DEPTH, D_MODEL)),
        "norm_ffn_pre": gain(ks[17], (DEPTH, D_MODEL)),
        "w_ffn_in": nrm(ks[18], (DEPTH, D_MODEL, 2 * FFN_HIDDEN), D_MODEL ** -0.5),
        "w_ffn_out": nrm(ks[19], (DEPTH, FFN_HIDDEN, D_MODEL), FFN_HIDDEN ** -0.5),
        "norm_ffn_post": gain(ks[20], (DEPTH, D_MODEL)),
    }

def reference(x, mem, rel_bias, norm_mix_pre, w_in, b_gate, conv_dw, conv_dw_bias, conv_ln_g,
              conv_ln_b, w_conv_out, w_att_out, norm_mem, w_mem_kv, w_mem_out, w_out,
              norm_mix_post, norm_ffn_pre, w_ffn_in, w_ffn_out, norm_ffn_post):
    B, S, _ = x.shape
    c1 = 2 * CONV_WIDTH
    c2 = c1 + 3 * ATT_WIDTH
    c3 = c2 + MEM_WIDTH
    for l in range(DEPTH):
        h = _rms_norm(x, norm_mix_pre[l])
        z = h @ w_in[l]
        y_conv = _conv_module(z[..., :c1], conv_dw[l], conv_dw_bias[l], conv_ln_g[l],
                              conv_ln_b[l], w_conv_out[l])
        y_att = _dilated_attention(z[..., c1:c2], rel_bias) @ w_att_out[l]
        y_mem = _memory_attention(z[..., c2:c3], mem, norm_mem[l], w_mem_kv[l], w_mem_out[l])
        gates = jax.nn.sigmoid(z[..., c3:] + b_gate[l]).reshape(B, S, N_BRANCHES, D_MODEL)
        merged = gates[:, :, 0] * y_conv + gates[:, :, 1] * y_att + gates[:, :, 2] * y_mem
        x = x + _rms_norm(merged @ w_out[l], norm_mix_post[l])
        h = _rms_norm(x, norm_ffn_pre[l])
        gu = h @ w_ffn_in[l]
        g_ff, u_ff = gu[..., :FFN_HIDDEN], gu[..., FFN_HIDDEN:]
        x = x + _rms_norm((jax.nn.silu(g_ff) * u_ff) @ w_ffn_out[l], norm_ffn_post[l])
    return x


_drawn_inputs = setup_inputs


def setup_inputs(seed=0):
    import zlib

    import numpy as np

    out = dict(_drawn_inputs(seed))
    spreads = {}
    factors = {'b_gate': 8.0,
     'conv_ln_b': 21.787,
     'norm_mem': 5.568,
     'rel_bias': 5.513,
     'conv_dw_bias': 8.0,
     'conv_ln_g': 7.764}
    for name, (base, spread) in spreads.items():
        noise = np.random.default_rng([zlib.crc32(name.encode()), seed]).standard_normal(out[name].shape)
        drawn = base * np.exp(spread * noise) if base else spread * noise
        out[name] = __import__('jax').numpy.asarray(drawn.astype(out[name].dtype))
    for name, factor in factors.items():
        out[name] = (out[name] * factor).astype(out[name].dtype)
    return out
```

```python
import concourse.bass as bass
from concourse import mybir
from contextlib import ExitStack

P = 128
D = 1024
T = 1024
NT = T // P
KD = D // P
HALF = 512
N_MEM = 256
MEM_HEADS = 4
CONV_W = 512
CT = CONV_W // P
TAPS = 31
PAD = TAPS // 2
ATT_W = 768
ATT_E = 64
SLOTS_H = 4
HIDDEN = 2816
CHUNKS = HIDDEN // 256
DILATIONS = (1, 4, 16)
RADIUS = 64
REL = 512
NEG = -1e30
C_ATT = 2 * CONV_W
C_MEM = C_ATT + 3 * ATT_W
C_GATE = C_MEM + MEM_HEADS * P
ROW = ATT_E + 2

V_MIX, V_MEM, V_FFN, V_GATE, V_DWB, V_LNG, V_LNB = 0, 8, 16, 24, 48, 52, 56
N_VEC = 60

U_KV, U_MQ, U_CONV, U_QKV, U_BR, U_OUT, U_FFN = 0, 8, 12, 20, 56, 92, 100
N_UNITS = U_FFN + 6 * CHUNKS
CREDIT = 2


def window(g, t):
    if g == 0:
        start = min(max(P * t - RADIUS, 0), T - 2 * P)
        return start, P * t - start
    if g == 1:
        return 2 * P * (t // 2), P * (t % 2)
    return P * t, 0


V_CHUNKS = ([0, P] + [RADIUS + P * k for k in range(7)] + [T - 2 * P, T - P],
            [P * k for k in range(NT)], [P * k for k in range(NT)])
V_BATCHES = (3, 2, 2)


def v_batches_before(pair):
    return sum(2 * V_BATCHES[g] for g in range(pair // 2)) + (pair % 2) * V_BATCHES[pair // 2]


def hybrid_layer(nc, x, mem, rel_bias, norm_mix_pre, w_in, b_gate, conv_dw, conv_dw_bias, conv_ln_g,
                 conv_ln_b, w_conv_out, w_att_out, norm_mem, w_mem_kv, w_mem_out, w_out,
                 norm_mix_post, norm_ffn_pre, w_ffn_in, w_ffn_out, norm_ffn_post,
                 identity, bucket_hot, out):
    f32 = mybir.dt.float32
    f32r = mybir.dt.float32r
    u8 = mybir.dt.uint8
    ALU = mybir.AluOpType
    ACT = mybir.ActivationFunctionType
    X = mybir.AxisListType.X
    ctx = ExitStack()

    BASE = 16512

    def sb(name, shape, offset, dt=f32):
        return nc.alloc_sbuf_tensor_at(name, shape, dt, offset=BASE + offset)

    KB = 1024
    h_hi = sb("h_hi", [P, KD, T], 0, f32r)
    h_lo = sb("h_lo", [P, KD, T], 32 * KB, f32r)
    raw = sb("raw", [P, 2, 1024], 64 * KB)
    w_hi = sb("w_hi", [P, 2, 1024], 72 * KB, f32r)
    w_lo = sb("w_lo", [P, 2, 1024], 80 * KB, f32r)
    o = 88 * KB
    ident = sb("ident", [P, P], o)
    ones = sb("ones", [P, P], o + 512)
    zeros = sb("zeros", [P, P], o + 1024)
    vcols = sb("vcols", [P, N_VEC], o + 1536)
    taps = sb("taps", [P, TAPS, CT], o + 2048)
    sumsq = sb("sumsq", [P, 40], o + 2560)
    std = sb("std", [P, 40], o + 2720)
    rstd = sb("rstd", [P, 40], o + 2880)
    eps_rms = sb("eps_rms", [P, 8], o + 3040)
    eps_ln = sb("eps_ln", [P, 8], o + 3072)
    post_gain = sb("post_gain", [P, D], o + 3104)
    R = o + 3104 + 4096
    U_W = T + 2 * PAD
    u = sb("u", [P, CT, U_W], R)
    ATT = R + CT * U_W * 4
    MEM = ATT + 16 * KB
    ACC = MEM + 32 * KB
    SG = ACC + 32 * KB
    TMP = SG + 8 * KB
    x_tok = sb("x_tok", [P, NT, D], R)
    mem_hi_t = sb("mem_hi_t", [P, KD, N_MEM], MEM, f32r)
    mem_lo_t = sb("mem_lo_t", [P, KD, N_MEM], MEM + 8 * KB, f32r)
    mem_tok = sb("mem_tok", [P, 2, D], MEM + 16 * KB)
    xs0 = sb("xs0", [P, 2, D], MEM + 24 * KB)
    f0 = [sb("f0a", [P, D], o + 3104), sb("f0b", [P, D], ACC + 8 * KB)]
    bhot = sb("bhot", [33, 3, REL], ACC + 12 * KB)
    rel = sb("rel", [33, 12], ACC + 18 * KB)
    e_rows = sb("e_rows", [SLOTS_H, 3, REL], ACC + 20 * KB)
    junk0 = sb("junk0", [P, D], ACC + 28 * KB)
    vec_rows = sb("vec_rows", [N_VEC, P], ACC + 26 * KB)
    tap_rows = sb("tap_rows", [TAPS * CT, P], ACC + 26 * KB + 512)
    q_mem = sb("q_mem", [P, MEM_HEADS, T], ATT)
    kv_t = sb("kv_t", [P, 2 * MEM_HEADS, N_MEM], ACC)
    v_mem = sb("v_mem", [P, 2, MEM_HEADS, P], ACC + 8 * KB)
    q_cur = sb("q_cur", [P, T], ACC + 12 * KB)
    k_cur = sb("k_cur", [P, N_MEM], ACC + 16 * KB)
    v_cur = sb("v_cur", [P, 2, P], ACC + 17 * KB)
    p_mem = sb("p_mem", [P, 2, N_MEM], ACC + 18 * KB)
    pt_mem = sb("pt_mem", [P, 2, 2, HALF], ACC + 20 * KB)
    sg_conv = sb("sg_conv", [P, T], ACC + 28 * KB)
    mstat = sb("mstat", [P, 2, 4], ACC + 46 * KB)
    m_hi = sb("m_hi", [P, MEM_HEADS, T], MEM, f32r)
    m_lo = sb("m_lo", [P, MEM_HEADS, T], MEM + 16 * KB, f32r)
    nxt = sb("nxt", [P, 3, T], ATT)
    prob = sb("prob", [P, 2, 2, 256], ATT + 12 * KB)
    cur = sb("cur", [P, 3, T], ACC)
    v_tok = sb("v_tok", [P, 12, P], ACC + 12 * KB)
    sbias = sb("sbias", [P, 2, 2, 256], ACC + 18 * KB)
    p_t = sb("p_t", [P, 2, 4, P], ACC + 22 * KB)
    heads_out = sb("heads_out", [P, NT, 2, ROW], ACC + 26 * KB)
    bias01 = sb("bias01", [P, 2 * SLOTS_H, 384], ACC + 32 * KB)
    bias2 = sb("bias2", [P, SLOTS_H, P], ACC + 44 * KB)
    parts = sb("parts", [P, 3, NT * SLOTS_H, ROW], ACC)
    a_tok = sb("a_tok", [P, NT, SLOTS_H * ATT_E], ATT)
    cmb = sb("cmb", [P, 10, NT * SLOTS_H], ACC + 26 * KB)
    wsum = sb("wsum", [P, NT * SLOTS_H, ATT_E], SG)
    a_hi = sb("a_hi", [P, 2, T], ATT, f32r)
    a_lo = sb("a_lo", [P, 2, T], ATT + 8 * KB, f32r)
    acc = sb("acc", [P, KD, T], ACC)
    sg = sb("sg", [P, 2, T], SG)
    tmp = sb("tmp", [P, 2, T], TMP)
    c_hi = sb("c_hi", [P, CT, T], ATT, f32r)
    c_lo = sb("c_lo", [P, CT, T], R, f32r)
    merged_hi = sb("merged_hi", [P, KD, T], MEM, f32r)
    merged_lo = sb("merged_lo", [P, KD, T], ACC, f32r)
    y_t = sb("y_t", [P, KD, T], R)
    x1 = sb("x1", [P, NT, D], MEM)
    x_again = sb("x_again", [P, NT, D], ACC)
    act_hi = sb("act_hi", [P, 2, 2, T], ACC, f32r)
    act_lo = sb("act_lo", [P, 2, 2, T], ACC + 16 * KB, f32r)

    rel_scratch = nc.dram_tensor("rel_scratch", (3 * SLOTS_H, P, REL), f32)
    att_scratch = nc.dram_tensor("att_scratch", (3, T, SLOTS_H * ROW), f32).ap()

    with ctx:
        z = [ctx.enter_context(nc.psum_tensor(f"z{k}", [P, 1024], f32)) for k in range(4)]
        s_bank = z[2][:].rearrange("p (b n) -> p b n", b=2)
        t_bank = z[3][:, 0:512]
        o_bank = z[3][:, 512:1024]

        def sem(name):
            return ctx.enter_context(nc.semaphore(name))

        raw_ready = [sem("raw_ready0"), sem("raw_ready1")]
        hi_done = sem("hi_done")
        split_done = sem("split_done")
        unit_done = sem("unit_done")
        z_free = [sem(f"z{k}_free") for k in range(4)]
        consts_in, rel_in, mem_in, tables_in = (sem(n) for n in ("consts_in", "rel_in", "mem_in", "tables_in"))
        x_in = [sem(f"x_in{t}") for t in range(NT)]
        rel_ones, rel_mm, rel_rows, rel_out = (sem(n) for n in ("rel_ones", "rel_mm", "rel_rows", "rel_out"))
        consts_set, vec_mm, vec_set = (sem(n) for n in ("consts_set", "vec_mm", "vec_set"))
        sq_done, std_done, rstd_done, xs_done = (sem(n) for n in ("sq_done", "std_done", "rstd_done", "xs_done"))
        xt_mm, f_done, fhi_done, flo_done = (sem(n) for n in ("xt_mm", "f_done", "fhi_done", "flo_done"))
        vmem_mm, vmem_set = sem("vmem_mm"), sem("vmem_set")
        m_cur, m_qk, m_max, m_exp, m_rden, m_pn, m_t, m_pt, m_pv, m_ohi, m_olo = (sem(n) for n in (
            "m_cur", "m_qk", "m_max", "m_exp", "m_rden", "m_pn", "m_t", "m_pt", "m_pv", "m_ohi", "m_olo"))
        u_pad = sem("u_pad")
        c_cur, c_qk, c_add, c_max, c_exp, c_t, c_pt, c_pv, c_oev, c_vt, c_vset = (sem(n) for n in (
            "c_cur", "c_qk", "c_add", "c_max", "c_exp", "c_t", "c_pt", "c_pv", "c_oev", "c_vt",
            "c_vset"))
        heads_sent = [sem("heads_sent0"), sem("heads_sent1")]
        bias_cut = sem("bias_cut")
        parts_in, cmb_step, cmb_exp, a_tok_set, at_mm, ahi_set, a_set = (sem(n) for n in (
            "parts_in", "cmb_step", "cmb_exp", "a_tok_set", "at_mm", "ahi_set", "a_set"))
        br_tmp, br_f, br_hi, br_lo, tap_done = (sem(n) for n in ("br_tmp", "br_f", "br_hi", "br_lo", "tap_done"))
        ln_mean, ln_xc, ln_sq, ln_var, ln_std, ln_rstd, ln_xn, ln_f, ln_hi, ln_lo = (sem(n) for n in (
            "ln_mean", "ln_xc", "ln_sq", "ln_var", "ln_std", "ln_rstd", "ln_xn", "ln_f", "ln_hi", "ln_lo"))
        y_set, n_yt, n_sq, n_std, n_rstd, n_t1, n_x1, n_xs, n_xt, n_f, n_hi, n_lo, x_again_in, gain_in = (
            sem(n) for n in ("y_set", "n_yt", "n_sq", "n_std", "n_rstd", "n_t1", "n_x1", "n_xs", "n_xt", "n_f",
                             "n_hi", "n_lo", "x_again_in", "gain_in"))
        x_again_t = [sem(f"x_again{t}") for t in range(NT)]
        y_zero, ff_f, ff_hi, ff_lo, ff_y = (sem(n) for n in ("y_zero", "ff_f", "ff_hi", "ff_lo", "ff_y"))
        t_sq, t_std, t_rstd, t_t1, t_out, t_yt, stored = (sem(n) for n in (
            "t_sq", "t_std", "t_rstd", "t_t1", "t_out", "t_yt", "stored"))

        Z0_QKV = Z1_QKV = 4 + 2 + MEM_HEADS
        Z01_BR = (Z0_QKV + 12, Z1_QKV + 6)
        Z01_B1 = tuple(n + 5 for n in Z01_BR)
        Z01_B2 = tuple(n + 4 for n in Z01_B1)
        Z01_OUT = tuple(n + 4 for n in Z01_B2)
        Z01_N = tuple(n + 4 for n in Z01_OUT)
        Z01_F = tuple(n + 4 for n in Z01_N)
        Z23_N = 3 * 4
        Z23_F = Z23_N + 4
        Z23_T = Z23_F + 4 * CHUNKS

        block = ctx.enter_context(nc.Block())

        def unit_ready(pe, r):
            pe.wait_ge(split_done, r + CREDIT + 1)

        kv_v = w_mem_kv.rearrange("o (k p) n -> p (o k) n", p=P)
        in_v = w_in.rearrange("o (k p) n -> p (o k) n", p=P)
        conv_v = w_conv_out.rearrange("o (k p) n -> p (o k) n", p=P)
        att_v = w_att_out.rearrange("o (k p) n -> p (o k) n", p=P)
        memo_v = w_mem_out.rearrange("o (k p) n -> p (o k) n", p=P)
        out_v = w_out.rearrange("o (k p) n -> p (o k) n", p=P)
        ffi_v = w_ffn_in.rearrange("o (k p) n -> p (o k) n", p=P)
        ffo_v = w_ffn_out.rearrange("o (k p) n -> p (o k) n", p=P)

        @block.sync
        def _(sp):
            def load(r, slot, src, row, k, col, n, free=True):
                src = src.bitcast(u8)
                (row_step, _), (tile_step, _), _ = src.ap
                at = tile_step * row + 4 * col
                src = bass.AP(src.tensor, at if isinstance(at, int) else sp.snap(sp.to_reg(at)),
                              [[row_step, P], [tile_step, k], [1, 4 * n]])
                if free:
                    sp.wait_ge(split_done, r + 1)
                sp.dma_start(raw[:, slot, 0:k * n].rearrange("p (k n) -> p k n", k=k).bitcast(u8), src)\
                    .then_inc(raw_ready[slot], 16)

            sp.dma_start(mem_tok[:], mem.rearrange("o (t p) d -> p (o t) d", p=P)).then_inc(mem_in, 16)
            sp.dma_start(ident[:], identity).then_inc(consts_in, 16)
            for slot in range(2):
                load(slot, slot, kv_v, 0, KD, P * slot, P, free=False)
            sp.dma_start(bhot[:], bucket_hot.rearrange("g b n -> b g n")).then_inc(rel_in, 16)
            for row, v, n in ((V_MIX, norm_mix_pre, 8), (V_MEM, norm_mem, 8), (V_FFN, norm_ffn_pre, 8),
                              (V_GATE, b_gate, 24), (V_DWB, conv_dw_bias, 4), (V_LNG, conv_ln_g, 4),
                              (V_LNB, conv_ln_b, 4)):
                sp.dma_start(vec_rows[row:row + n, :], v.rearrange("o (k p) -> (o k) p", p=P))\
                    .then_inc(consts_in, 16)
            sp.dma_start(tap_rows[:], conv_dw.rearrange("o j (c p) -> (o j c) p", p=P)).then_inc(consts_in, 16)
            with sp.Fori(1, 4) as i:
                for slot in range(2):
                    load(U_KV + 2 * i + slot, slot, kv_v, 0, KD, 2 * P * i + P * slot, P)
            with sp.Fori(0, 2) as i:
                for slot in range(2):
                    load(U_MQ + 2 * i + slot, slot, in_v, 0, KD, C_MEM + 2 * P * i + P * slot, P)
            with sp.Fori(0, CT) as i:
                load(U_CONV + 2 * i, 0, in_v, 0, KD, CONV_W + P * i, P)
                load(U_CONV + 2 * i + 1, 1, in_v, 0, KD, P * i, P)
            sp.wait_ge(rel_out, 48)
            with nc.allow_non_contiguous_dma(reason="Toeplitz rows"):
                sp.dma_start(bias01[:], bass.AP(rel_scratch, P, [[REL - 1, P], [P * REL, 8], [1, 384]]))\
                    .then_inc(tables_in, 16)
                sp.dma_start(bias2[:], bass.AP(rel_scratch, 8 * P * REL + 2 * P,
                                               [[REL - 1, P], [P * REL, 4], [1, P]])).then_inc(tables_in, 16)
            with sp.Fori(0, 6) as i:
                for j in range(6):
                    load(U_QKV + 6 * i + j, j % 2,
                         in_v, 4 * (j % 2), 4, C_ATT + ATT_W * (j // 2) + P * i, P)
            for b, (proj, k) in enumerate(((memo_v, 4), (att_v, 2), (conv_v, 4))):
                branch = (2, 1, 0)[b]
                with sp.Fori(0, 2) as i:
                    for j in range(2):
                        for q in range(2):
                            r = U_BR + 12 * b + 6 * i + 3 * j + q
                            load(r, (3 * j + q) % 2,
                                 in_v, 0, KD, C_GATE + D * branch + HALF * i + P * (2 * j + q), P)
                        load(U_BR + 12 * b + 6 * i + 3 * j + 2, (3 * j + 2) % 2,
                             proj, 0, k, HALF * i + 256 * j, 256)
            with sp.Fori(0, 4) as i:
                for slot in range(2):
                    load(U_OUT + 2 * i + slot, slot, out_v, 0, KD, 2 * P * i + P * slot, P)
            sp.dma_start(post_gain[:], norm_mix_post.to_broadcast([P, D])).then_inc(gain_in, 16)

            def load_ffn_in(r, slot, tile, gate):
                load(r, slot, ffi_v, 0, KD, (0 if gate else HIDDEN) + P * tile, P)

            def load_ffn_out(r, slot, chunk, half):
                load(r, slot, ffo_v, 2 * chunk, 2, HALF * half, HALF)

            load_ffn_in(U_FFN, 0, 0, True)
            load_ffn_in(U_FFN + 1, 1, 0, False)
            sp.wait_ge(unit_done, U_FFN + CREDIT)
            for t in range(NT):
                sp.dma_start(x_again[:, t, :], x[0, P * t:P * (t + 1), :]).then_inc(x_again_t[t], 16)
            load_ffn_in(U_FFN + 2, 0, 1, True)
            load_ffn_in(U_FFN + 3, 1, 1, False)
            sp.wait_ge(n_x1, NT)
            sp.dma_start(post_gain[:], norm_ffn_post.to_broadcast([P, D])).then_inc(gain_in, 16)
            with sp.Fori(1, CHUNKS) as c:
                r = U_FFN - 2 + 6 * c
                for j in range(2):
                    load_ffn_in(r + 3 * j, (3 * j) % 2, 2 * c + j, True)
                    load_ffn_in(r + 3 * j + 1, (3 * j + 1) % 2, 2 * c + j, False)
                    load_ffn_out(r + 3 * j + 2, (3 * j + 2) % 2, c - 1, j)
            for half in range(2):
                load_ffn_out(N_UNITS - 2 + half, half, CHUNKS - 1, half)
            for t in range(NT):
                sp.wait_ge(t_out, t + 1)
                sp.dma_start(out[0, P * t:P * (t + 1), :], x1[:, t, :]).then_inc(stored, 16)
            sp.wait_ge(stored, 16 * NT)

        @block.gpsimd
        def _(pool):
            pool.sem_inc(split_done, CREDIT)
            nc.gpsimd.memset(zeros[:], 0.0).then_inc(consts_set, 1)
            nc.gpsimd.memset(eps_rms[:], 1e-6).then_inc(consts_set, 1)
            nc.gpsimd.memset(eps_ln[:], 1e-5).then_inc(consts_set, 1)
            nc.gpsimd.memset(ones[:], 1.0 / CONV_W).then_inc(consts_set, 1)
            nc.gpsimd.memset(rel[:], 1.0).then_inc(rel_ones, 1)
            pool.wait_ge(consts_set, 4)

            def split(r, n, slot, width=1024, free=True):
                pool.wait_ge(raw_ready[slot], 16 * (n + 1))
                if free:
                    pool.wait_ge(unit_done, r + 1)
                a = width // P
                view = [w[:, slot, 0:width].rearrange("p (a b) -> p a b", a=a) for w in (raw, w_hi, w_lo)]
                nc.gpsimd.tensor_tensor(view[1], view[0], zeros[:].unsqueeze(1).to_broadcast([P, a, P]),
                                        ALU.add).then_inc(hi_done, 1)
                pool.wait_ge(hi_done, r + 1)
                nc.gpsimd.tensor_tensor(view[2], view[0], view[1], ALU.subtract).then_inc(split_done, 1)

            def split_run(first, last, widths=(1024, 1024)):
                per = len(widths)
                with pool.Fori(0, (last - first) // per) as i:
                    for j, width in enumerate(widths):
                        split(first + per * i + j, first // 2 + per // 2 * i + j // 2, j % 2, width)

            for slot in range(2):
                split(slot, 0, slot, free=False)
            split_run(2, U_QKV)
            split_run(U_QKV, U_BR, (512, 512))
            split_run(U_BR, U_BR + 12)
            split_run(U_BR + 12, U_BR + 24, (1024, 1024, 512, 1024, 1024, 512))
            split_run(U_BR + 24, U_FFN + 2)
            pool.wait_ge(n_yt, NT)
            nc.gpsimd.memset(y_t[:], 0.0).then_inc(y_zero, 1)
            split_run(U_FFN + 2, N_UNITS)

        SPLIT_PRODUCTS = ("hh", "hl", "lh")

        def products(slot, k_tiles, pick, cols, rhs_hi, rhs_lo, dst, rhs_n, first=0, last=None):
            todo = []
            halves = (rhs_n + HALF - 1) // HALF
            n = min(rhs_n, HALF)
            for h in range(halves):
                for k in range(k_tiles):
                    for what in SPLIT_PRODUCTS:
                        w = w_hi if what[0] == "h" else w_lo
                        m = rhs_hi if what[1] == "h" else rhs_lo
                        todo.append((dst[:, h * HALF:h * HALF + n], w[:, slot, pick(k) + cols:pick(k) + cols + P],
                                     m(k, h * HALF, n), first == 0 and k == 0 and what == "hh",
                                     last is None and k == k_tiles - 1 and what == "lh"))
            return todo

        def issue(todo):
            for dst, w, m, start, stop in todo:
                mm = nc.tensor.matmul(dst, w, m, start=start, stop=stop)
            return mm

        def h_rhs(t):
            return lambda k, at, n: t[:, k, at:at + n]

        def unit_todo(slot, dst):
            return products(slot, KD, lambda k: P * k, 0, h_rhs(h_hi), h_rhs(h_lo), dst, T)

        @block.tensor
        def _(pe):
            pe.sem_inc(unit_done, CREDIT)
            for s in (m_t, m_pv, c_t, c_pv):
                pe.sem_inc(s, 2)

            def transposes(dst, src, n, done):
                for k in range(n):
                    mm = nc.tensor.transpose(dst[:, P * k:P * (k + 1)], src[:, P * k:P * (k + 1)], ident[:])
                mm.then_inc(done, 1)

            pe.wait_ge(consts_in, 16 * 9)
            nc.tensor.transpose(z[0][:, 0:N_VEC], vec_rows[:], ident[0:N_VEC, 0:N_VEC])
            nc.tensor.transpose(z[0][:, P:P + TAPS * CT], tap_rows[:], ident[0:TAPS * CT, 0:TAPS * CT])\
                .then_inc(vec_mm, 1)
            pe.wait_ge(rel_in, 32)
            for g in range(3):
                dst = z[1][0:SLOTS_H, HALF * g:HALF * (g + 1)] if g < 2 else z[0][0:SLOTS_H, HALF:2 * HALF]
                mm = nc.tensor.matmul(dst, rel[:, SLOTS_H * g:SLOTS_H * (g + 1)], bhot[:, g, :], start=True, stop=True)
            mm.then_inc(rel_mm, 1)
            for t in range(2):
                pe.wait_ge(xs_done, t + 1)
                transposes(z[2 + t], xs0[:, t], KD, xt_mm)
            pe.wait_ge(flo_done, 2)
            with pe.Fori(0, 4) as i:
                for s in range(2):
                    n = 2 * i + s
                    unit_ready(pe, U_KV + n)
                    pe.wait_ge(z_free[s], i + 1)
                    issue(products(s, KD, lambda k: P * k, 0, h_rhs(mem_hi_t), h_rhs(mem_lo_t), z[s], N_MEM))\
                        .then_inc(unit_done, 1)
                    pe.wait_ge(xs_done, n + 3)
                    pe.wait_ge(f_done, n + 1)
                    transposes(z[2 + s], xs0[:, s], KD, xt_mm)
            for k in range(2):
                pe.wait_ge(z_free[k], 4 + 1)
            pe.wait_ge(f_done, 9)
            for c in range(2):
                for h in range(MEM_HEADS):
                    mm = nc.tensor.transpose(z[2][:, P * (4 * c + h):P * (4 * c + h + 1)],
                                             kv_t[:, MEM_HEADS + h, P * c:P * (c + 1)], ident[:])
            mm.then_inc(vmem_mm, 1)
            pe.wait_ge(flo_done, 10)
            with pe.Fori(0, 2) as i:
                for s in range(2):
                    unit_ready(pe, U_MQ + 2 * i + s)
                    pe.wait_ge(z_free[s], 4 + i + 1)
                    issue(unit_todo(s, z[s])).then_inc(unit_done, 1)

            pe.wait_ge(vmem_set, 1)
            pe.wait_ge(f_done, 10)
            with pe.Fori(0, MEM_HEADS) as h:
                conv = [unit_todo(0, z[0]), unit_todo(1, z[1])]
                flat = [(j, n) for j in range(2) for n in range(len(conv[j]))]
                share = -(-len(flat) // 10)
                for step in range(10):
                    if step in (5, 9):
                        half = (step - 5) // 4
                        pe.wait_ge(m_pt, 8 * h + 4 * half + 4 + 1)
                        pe.wait_ge(m_olo, 2 * h + half + 1)
                        for c in range(2):
                            mm = nc.tensor.matmul(o_bank, v_cur[:, c, :], pt_mem[:, half, c, :], start=c == 0, stop=c == 1)
                        mm.then_inc(m_pv, 1)
                    if 1 <= step <= 8:
                        t = step - 1
                        pe.wait_ge(m_pn, 8 * h + t + 1)
                        pe.wait_ge(m_pt, 8 * h + t + 1)
                        for c in range(2):
                            at = P * c
                            mm = nc.tensor.transpose(t_bank[:, at:at + P], p_mem[:, t % 2, P * c:P * (c + 1)], ident[:])
                        mm.then_inc(m_t, 1)
                    if step < 8:
                        t = step
                        if t == 0:
                            pe.wait_ge(m_cur, h + 1)
                        pe.wait_ge(m_exp, 8 * h + t + 1)
                        nc.tensor.matmul(s_bank[:, t % 2, 0:N_MEM], q_cur[:, P * t:P * (t + 1)], k_cur[:],
                                         start=True, stop=True).then_inc(m_qk, 1)
                    for j, n in flat[share * step:share * (step + 1)]:
                        if n == 0:
                            unit_ready(pe, U_CONV + 2 * h + j)
                            pe.wait_ge(z_free[j], 6 + h + 1)
                        mm = issue([conv[j][n]])
                        if n == len(conv[j]) - 1:
                            mm.then_inc(unit_done, 1)

            def qkv_todo():
                todo = []
                for j in range(6):
                    dst = z[(j // 2) % 2]
                    half_k = j % 2
                    part = []
                    for hh in range(2):
                        for k in range(4):
                            for what in SPLIT_PRODUCTS:
                                w = w_hi if what[0] == "h" else w_lo
                                m = h_hi if what[1] == "h" else h_lo
                                part.append((dst[:, hh * HALF:(hh + 1) * HALF], w[:, j % 2, P * k:P * (k + 1)],
                                             m[:, 4 * half_k + k, hh * HALF:(hh + 1) * HALF],
                                             half_k == 0 and k == 0 and what == "hh",
                                             half_k == 1 and k == 3 and what == "lh"))
                    todo += [(j, n, len(part), mm) for n, mm in enumerate(part)]
                return todo


            def qkv_issue(share, pair):
                for j, n, size, mm in share:
                    if n == 0:
                        unit_ready(pe, U_QKV + 6 * pair + j)
                        if j == 0:
                            pe.wait_ge(z_free[0], Z0_QKV + 2 * pair + 1)
                        if j == 2:
                            pe.wait_ge(z_free[1], Z1_QKV + pair + 1)
                        if j == 4:
                            pe.wait_ge(z_free[0], Z0_QKV + 2 * pair + 2)
                    m = issue([mm])
                    if n == size - 1:
                        m.then_inc(unit_done, 1)

            def dilated_pair(g, pair, vb, more):
                todo = qkv_todo() if more else []
                share = -(-len(todo) // 10)
                tile = 8 * pair
                chunks = V_CHUNKS[g]
                pe.wait_ge(c_cur, 3 * pair + 3)
                for step in range(10):
                    if step == 0:
                        pe.wait_ge(c_oev, tile + 1)
                        pe.wait_ge(c_pt, tile + 1)
                    for b in ((0, 1) if step == 0 else (2,) if step == 1 and V_BATCHES[g] == 3 else ()):
                        if b == 2:
                            pe.wait_ge(c_vset, vb + 1)
                        dst = t_bank if b == 1 else o_bank
                        for j, start in enumerate(chunks[4 * b:4 * b + 4]):
                            mm = nc.tensor.transpose(dst[:, P * j:P * (j + 1)], cur[:, 2, start:start + P], ident[:])
                        mm.then_inc(c_vt, 1)
                    if step >= 2:
                        t = step - 2
                        if t == 0:
                            pe.wait_ge(c_vset, vb + V_BATCHES[g])
                        pe.wait_ge(c_pt, tile + t + 2)
                        pe.wait_ge(c_oev, tile + t + 1)
                        start = window(g, t)[0]
                        keys = 1 if g == 2 else 2
                        for hd in range(2):
                            for c in range(keys):
                                mm = nc.tensor.matmul(o_bank[:, ATT_E * hd:ATT_E * (hd + 1)], p_t[:, t % 2, 2 * hd + c, :],
                                                      v_tok[:, chunks.index(start + P * c), ATT_E * hd:ATT_E * (hd + 1)],
                                                      start=c == 0, stop=c == keys - 1)
                        mm.then_inc(c_pv, 1)
                    if 1 <= step <= 8:
                        t = step - 1
                        if t == 0:
                            pe.wait_ge(c_vset, vb + 2)
                        pe.wait_ge(c_exp, tile + t + 3)
                        pe.wait_ge(c_pt, tile + t + 1)
                        for hd in range(2):
                            for c in range(1 if g == 2 else 2):
                                mm = nc.tensor.transpose(t_bank[:, P * (2 * hd + c):P * (2 * hd + c + 1)],
                                                         prob[:, t % 2, hd, P * c:P * (c + 1)], ident[:])
                        mm.then_inc(c_t, 1)
                    if step < 8:
                        t = step
                        pe.wait_ge(c_add, tile + t + 1)
                        start = window(g, t)[0]
                        n = P if g == 2 else 2 * P
                        for hd in range(2):
                            rows = slice(ATT_E * hd, ATT_E * (hd + 1))
                            mm = nc.tensor.matmul(s_bank[:, hd, 0:n], cur[rows, 0, P * t:P * (t + 1)],
                                                  cur[rows, 1, start:start + n], start=True, stop=True)
                        mm.then_inc(c_qk, 1)
                    qkv_issue(todo[share * step:share * (step + 1)], pair + 1)

            qkv_issue(qkv_todo(), 0)
            pe.wait_ge(m_exp, 8 * MEM_HEADS + 2)
            pe.wait_ge(m_pt, 8 * MEM_HEADS + 1)
            pe.wait_ge(m_olo, 2 * MEM_HEADS + 1)
            for g in range(2):
                with pe.Fori(0, 2) as i:
                    dilated_pair(g, 2 * g + i, v_batches_before(2 * g) + V_BATCHES[g] * i, True)
            dilated_pair(2, 4, v_batches_before(4), True)
            dilated_pair(2, 5, v_batches_before(5), False)
            pe.wait_ge(c_add, 8 * 6 + 1)
            pe.wait_ge(c_oev, 8 * 6 + 1)


            def branch(b, k_tiles, rhs_hi, rhs_lo, z01, z23, ready=None):
                with pe.Fori(0, 2) as i:
                    r = U_BR + 12 * b + 6 * i
                    for j in range(2):
                        for q in range(2):
                            unit_ready(pe, r + 3 * j + q)
                            pe.wait_ge(z_free[q], z01[q] + 2 * i + j + 1)
                            issue(unit_todo((3 * j + q) % 2, z[q])).then_inc(unit_done, 1)
                        unit_ready(pe, r + 3 * j + 2)
                        if ready:
                            pe.wait_ge(*ready)
                        for q in range(2):
                            pe.wait_ge(z_free[2 + q], z23 + 2 * i + j + 1)
                            mm = issue(products((3 * j + 2) % 2, k_tiles, lambda k: 256 * k, P * q,
                                                rhs_hi, rhs_lo, z[2 + q], T))
                        mm.then_inc(unit_done, 1)

            branch(0, 4, h_rhs(m_hi), h_rhs(m_lo), Z01_BR, 0)
            pe.wait_ge(a_tok_set, 1)
            for c in range(2):
                pe.wait_ge(z_free[c], Z01_BR[c] + 4 + 1)
                for t in range(NT):
                    mm = nc.tensor.transpose(z[c][:, P * t:P * (t + 1)], a_tok[:, t, P * c:P * (c + 1)], ident[:])
                mm.then_inc(at_mm, 1)
            branch(1, 2, h_rhs(a_hi), h_rhs(a_lo), Z01_B1, 4)
            pe.wait_ge(tap_done, TAPS * CT + 1)
            pe.wait_ge(z_free[2], 8 + 1)
            pe.wait_ge(z_free[3], 8 + 1)
            for hh in range(2):
                for c in range(CT):
                    mm = nc.tensor.matmul(z[2][:, HALF * hh:HALF * (hh + 1)], ones[:],
                                          u[:, c, PAD + HALF * hh:PAD + HALF * (hh + 1)], start=c == 0, stop=c == CT - 1)
            mm.then_inc(ln_mean, 1)
            for c in range(CT):
                pe.wait_ge(ln_sq, c + 1)
                for hh in range(2):
                    mm = nc.tensor.matmul(z[3][:, HALF * hh:HALF * (hh + 1)], ones[:],
                                          tmp[:, c % 2, HALF * hh:HALF * (hh + 1)], start=c == 0, stop=c == CT - 1)
                mm.then_inc(ln_var, 1)
            branch(2, 4, h_rhs(c_hi), h_rhs(c_lo), Z01_B2, 8, (ln_lo, CT))

            pe.wait_ge(br_lo, KD)
            with pe.Fori(0, 4) as i:
                for s in range(2):
                    unit_ready(pe, U_OUT + 2 * i + s)
                    pe.wait_ge(z_free[s], Z01_OUT[s] + i + 1)
                    issue(products(s, KD, lambda k: P * k, 0, h_rhs(merged_hi), h_rhs(merged_lo), z[s], T))\
                        .then_inc(unit_done, 1)
            for k in range(2):
                pe.wait_ge(z_free[k], Z01_N[k] + 1)

            def y_tile(t, slot, wait, done):
                pe.wait_ge(z_free[2 + slot], wait)
                for k in range(KD):
                    mm = nc.tensor.transpose(z[2 + slot][:, P * k:P * (k + 1)], y_t[:, k, P * t:P * (t + 1)], ident[:])
                mm.then_inc(done, 1)

            y_tile(0, 0, Z23_N + 1, n_yt)
            for t in range(NT):
                if t + 1 < NT:
                    y_tile(t + 1, (t + 1) % 2, Z23_N + (t + 1) // 2 + 1, n_yt)
                pe.wait_ge(n_xs, t + 1)
                pe.wait_ge(z_free[t % 2], Z01_N[t % 2] + t // 2 + 1)
                transposes(z[t % 2], sg[:, t % 2], KD, n_xt)

            pe.wait_ge(n_lo, NT)

            def hidden(r, slot0, z01):
                for s in range(2):
                    slot = (slot0 + s) % 2
                    unit_ready(pe, r + s)
                    pe.wait_ge(z_free[s], z01[s] + 1)
                    issue(unit_todo(slot, z[s])).then_inc(unit_done, 1)

            def ffn_out(r, slot, act_slot, z23):
                unit_ready(pe, r)
                for q in range(4):
                    pe.wait_ge(z_free[2 + q % 2], z23 + q // 2 + 1)
                    mm = issue(products(slot, 2, lambda k: HALF * k, P * q,
                                        lambda k, at, n: act_hi[:, act_slot, k, at:at + n],
                                        lambda k, at, n: act_lo[:, act_slot, k, at:at + n], z[2 + q % 2], T))
                    if q < 3:
                        mm.then_inc(ff_y, 1)
                mm.then_inc(unit_done, 1)

            def chunk(c, act_slot):
                for j in range(2):
                    r = U_FFN - 2 + 6 * c + 3 * j
                    hidden(r, (3 * j) % 2, (Z01_F[0] + 2 * c + j, Z01_F[1] + 2 * c + j))
                    if j == 0:
                        pe.wait_ge(ff_lo, 2 * c)
                    ffn_out(r + 2, (3 * j + 2) % 2, act_slot, Z23_F + 4 * (c - 1) + 2 * j)

            for j in range(2):
                hidden(U_FFN + 2 * j, 0, (Z01_F[0] + j, Z01_F[1] + j))
            with pe.Fori(0, (CHUNKS - 1) // 2) as i:
                for s in range(2):
                    chunk(2 * i + 1 + s, s)
            pe.wait_ge(ff_lo, 2 * CHUNKS)
            for half in range(2):
                ffn_out(N_UNITS - 2 + half, half, (CHUNKS - 1) % 2, Z23_F + 4 * (CHUNKS - 1) + 2 * half)
            for k in (0, 1):
                pe.wait_ge(z_free[2 + k], Z23_T + 1)
            for t in range(NT):
                y_tile(t, t % 2, Z23_T + t // 2 + 1, t_yt)

        @block.scalar
        def _(act):
            for s, credit in ((m_exp, 2), (m_pt, 1), (c_exp, 2), (c_pt, 1), (heads_sent[0], 16),
                              (heads_sent[1], 16), (z_free[0], 1)):
                act.sem_inc(s, credit)
            a = nc.scalar.activation
            act.wait_ge(rel_ones, 1)
            act.dma_start(rel[0:32, :], rel_bias).then_inc(rel_in, 16)
            for t in range(NT):
                act.dma_start(x_tok[:, t, :], x[0, P * t:P * (t + 1), :]).then_inc(x_in[t], 16)
            act.wait_ge(consts_set, 4)

            def token_stats(j):
                if j == 0:
                    act.wait_ge(mem_in, 16)
                if j >= 2:
                    act.wait_ge(x_in[j - 2], 16)
                src = mem_tok[:, j, :] if j < 2 else x_tok[:, j - 2, :]
                if j:
                    act.wait_ge(sq_done, j)
                a(junk0[:], src, ACT.Square, accum_out=sumsq[:, j:j + 1]).then_inc(sq_done, 1)
                act.wait_ge(sq_done, j + 1)
                a(std[:, j:j + 1], sumsq[:, j:j + 1], ACT.Sqrt, bias=eps_rms[:, 0:1], scale=1.0 / D)\
                    .then_inc(std_done, 1)

            def token_hi(j):
                act.wait_ge(f_done, j + 1)
                dst = mem_hi_t[:, :, P * j:P * (j + 1)] if j < 2 else h_hi[:, :, P * (j - 2):P * (j - 1)]
                a(dst, f0[j % 2][:].rearrange("p (k n) -> p k n", k=KD), ACT.Copy).then_inc(fhi_done, 1)

            token_stats(0)
            token_stats(1)
            act.wait_ge(vec_mm, 1)
            a(vcols[:], z[0][:, 0:N_VEC], ACT.Copy).then_inc(vec_set, 1)
            a(taps[:].rearrange("p j c -> p (j c)"), z[0][:, P:P + TAPS * CT], ACT.Copy).then_inc(vec_set, 1)
            token_hi(0)
            token_hi(1)
            act.wait_ge(rel_rows, 3)
            for g in range(3):
                src = e_rows[:, g, :].unsqueeze(1).to_broadcast([SLOTS_H, P, REL])
                act.dma_start(rel_scratch.ap()[SLOTS_H * g:SLOTS_H * (g + 1), :, :], src).then_inc(rel_out, 16)
            token_stats(2)
            for n in range(8):
                act.wait_ge(unit_done, U_KV + n + 1 + CREDIT)
                a(kv_t[:, n, :], z[n % 2][:, 0:N_MEM], ACT.Copy).then_inc(z_free[n % 2], 1)
                if n + 3 < 10:
                    token_stats(n + 3)
                token_hi(n + 2)
            act.wait_ge(vmem_mm, 1)
            act.wait_ge(flo_done, 10)
            a(v_mem[:].rearrange("p c h n -> p (c h n)"), z[2][:], ACT.Copy).then_inc(vmem_set, 1)
            for h in range(MEM_HEADS):
                act.wait_ge(unit_done, U_MQ + h + 1 + CREDIT)
                a(q_mem[:, h, :], z[h % 2][:], ACT.Copy, scale=P ** -0.5).then_inc(z_free[h % 2], 1)

            act.wait_ge(rel_out, 48)
            with act.Fori(0, MEM_HEADS) as h:
                for step in range(10):
                    if step < 8:
                        t = step
                        act.wait_ge(m_max, 8 * h + t + 1)
                        act.wait_ge(m_t, 8 * h + t + 1)
                        a(p_mem[:, t % 2, :], s_bank[:, t % 2, 0:N_MEM], ACT.Exp, bias=mstat[:, t % 2, 0:1],
                          accum_out=mstat[:, t % 2, 1:2]).then_inc(m_exp, 1)
                    if 1 <= step <= 8:
                        t = step - 1
                        act.wait_ge(m_t, 8 * h + t + 3)
                        act.wait_ge(m_pv, 2 * h + t // 4 + 1)
                        a(pt_mem[:, t // 4, :, P * (t % 4):P * (t % 4 + 1)],
                          t_bank[:, 0:256].rearrange("p (c n) -> p c n", c=2), ACT.Copy)\
                            .then_inc(m_pt, 1)
                    if step == 6:
                        act.wait_ge(unit_done, U_CONV + 2 * h + 1 + CREDIT)
                        act.wait_ge(z_free[1], 6 + h + 1)
                        a(sg_conv[:], z[0][:], ACT.Sigmoid).then_inc(z_free[0], 1)

            def next_evac(j, pair, first=False):
                act.wait_ge(unit_done, U_QKV + 6 * pair + 2 * j + 2 + CREDIT)
                if not first:
                    act.wait_ge(c_cur, 3 * pair)
                a(nxt[:, j, :], z[j % 2][:], ACT.Copy, scale=ATT_E ** -0.5 if j == 0 else 1.0)\
                    .then_inc(z_free[j % 2], 1)

            def dilated_pair(g, pair, vb, more):
                tile = 8 * pair
                n = P if g == 2 else 2 * P
                for step in range(10):
                    for b in ((0, 1) if step == 0 else (2,) if step == 1 and V_BATCHES[g] == 3 else ()):
                        act.wait_ge(c_vt, vb + b + 1)
                        m = len(V_CHUNKS[g][4 * b:4 * b + 4])
                        a(v_tok[:, 4 * b:4 * b + m, :].rearrange("p j n -> p (j n)"),
                          (t_bank if b == 1 else o_bank)[:, 0:P * m], ACT.Copy).then_inc(c_vset, 1)
                    if step < 8:
                        t = step
                        act.wait_ge(c_max, tile + t + 1)
                        act.wait_ge(c_t, tile + t + 1)
                        for hd in range(2):
                            i = a(prob[:, t % 2, hd, 0:n], sbias[:, t % 2, hd, 0:n], ACT.Exp,
                                  bias=heads_out[:, t, hd, ATT_E + 1:ATT_E + 2],
                                  accum_out=heads_out[:, t, hd, ATT_E:ATT_E + 1])
                        i.then_inc(c_exp, 1)
                    if 1 <= step <= 8:
                        t = step - 1
                        act.wait_ge(c_t, tile + t + 3)
                        act.wait_ge(c_pv, tile + t + 1)
                        if g == 2:
                            a(p_t[:, t % 2, 0:4:2, :], t_bank.rearrange("p (b n) -> p b n", b=4)[:, 0:4:2, :],
                              ACT.Copy).then_inc(c_pt, 1)
                        else:
                            a(p_t[:, t % 2, :, :].rearrange("p b n -> p (b n)"), t_bank, ACT.Copy).then_inc(c_pt, 1)
                    if more and step in (4, 7):
                        next_evac((step - 4) // 3, pair + 1)
                    if step in (6, 9):
                        half = (step - 6) // 3
                        act.wait_ge(c_oev, tile + 4 * half + 4 + 1)
                        send(g, pair, half)
                if more:
                    next_evac(2, pair + 1)

            def send(g, pair, half):
                col = 2 * ROW * (pair - 2 * g)
                rows = att_scratch[g, :, bass.ds(col, 2 * ROW)]
                ts = slice(4 * half, 4 * half + 4)
                src = heads_out[:, ts].rearrange("p t h n -> p t (h n)")
                if g == 0:
                    act.dma_start(rows.rearrange("(t p) n -> p t n", p=P)[:, ts], src).then_inc(heads_sent[half], 16)
                elif g == 1:
                    for r in range(2):
                        act.dma_start(rows.rearrange("(c p r) n -> r p c n", p=P, c=2)[2 * half + r],
                                      src[:, 2 * r:2 * r + 2]).then_inc(heads_sent[half], 16)
                else:
                    for b in range(2):
                        act.dma_start(rows.rearrange("(l t a) n -> a l t n", t=8, a=2)[b, :, ts],
                                      src[64 * b:64 * (b + 1)]).then_inc(heads_sent[half], 16)

            act.wait_ge(z_free[1], 6 + MEM_HEADS + 1)
            for j in range(3):
                next_evac(j, 0, first=True)
            for g in range(2):
                with act.Fori(0, 2) as i:
                    dilated_pair(g, 2 * g + i, v_batches_before(2 * g) + V_BATCHES[g] * i, True)
            dilated_pair(2, 4, v_batches_before(4), True)
            dilated_pair(2, 5, v_batches_before(5), False)
            for half in range(2):
                act.wait_ge(heads_sent[half], 16 * (1 + 2 + 4 + 4))
            for g in range(3):
                act.dma_start(parts[:, g].rearrange("p (t h) n -> p t (h n)", t=NT),
                              att_scratch[g].rearrange("(t p) n -> p t n", p=P)).then_inc(parts_in, 16)
            act.wait_ge(cmb_step, 5)
            a(cmb[:, 4:7, :], cmb[:, 1:4, :], ACT.Exp).then_inc(cmb_exp, 1)

            def gate(b, q, d):
                r = U_BR + 12 * b + 6 * (d // 4) + 3 * (d % 4 // 2) + d % 2
                act.wait_ge(unit_done, r + 1 + CREDIT)
                act.wait_ge(z_free[2 + q], 4 * b + d // 2 + 1)
                col = V_GATE + KD * (2, 1, 0)[b] + d
                a(sg[:, q, :], z[q][:], ACT.Sigmoid, bias=vcols[:, col:col + 1]).then_inc(z_free[q], 1)

            act.wait_ge(a_tok_set, 1)
            for d in range(KD):
                gate(0, d % 2, d)
            for c in range(2):
                act.wait_ge(at_mm, 2)
                a(a_hi[:, c, :], z[c][:], ACT.Copy).then_inc(ahi_set, 1)
            for d in range(KD):
                gate(1, d % 2, d)
            for c in range(CT):
                act.wait_ge(ln_xc, c + 1)
                if c >= 2:
                    act.wait_ge(ln_var, c - 1)
                a(tmp[:, c % 2, :], u[:, c, PAD:PAD + T], ACT.Square).then_inc(ln_sq, 1)
            act.wait_ge(ln_var, CT)
            a(sg[:, 0, :], z[3][:], ACT.Sqrt, bias=eps_ln[:, 0:1]).then_inc(ln_std, 1)
            for c in range(CT):
                act.wait_ge(ln_xn, c + 1)
                if c >= 2:
                    act.wait_ge(ln_lo, c - 1)
                a(tmp[:, c % 2, :], u[:, c, PAD:PAD + T], ACT.Silu, bias=vcols[:, V_LNB + c:V_LNB + c + 1],
                  scale=vcols[:, V_LNG + c:V_LNG + c + 1]).then_inc(ln_f, 1)
                act.wait_ge(ln_f, c + 1)
                a(c_hi[:, c, :], tmp[:, c % 2, :], ACT.Copy).then_inc(ln_hi, 1)

            def merged_part(d):
                act.wait_ge(br_f, d + 1)
                a(merged_hi[:, d, :], tmp[:, d % 2, :], ACT.Copy).then_inc(br_hi, 1)

            act.wait_ge(ln_lo, CT)
            for d in range(0, KD, 2):
                gate(2, 0, d)
                gate(2, 1, d + 1)
                merged_part(d)
                merged_part(d + 1)
            for d in range(KD):
                act.wait_ge(unit_done, U_OUT + d + 1 + CREDIT)
                a(y_t[:, d, :], z[d % 2][:], ACT.Copy).then_inc(z_free[d % 2], 1)
            def norm_first(t):
                act.wait_ge(n_yt, t + 1)
                if t >= 2:
                    act.wait_ge(n_xt, t - 1)
                a(sg[:, t % 2, :], z[2 + t % 2][:], ACT.Square, accum_out=sumsq[:, 10 + t:11 + t]).then_inc(n_sq, 1)
                act.wait_ge(n_sq, 2 * t + 1)
                a(std[:, 10 + t:11 + t], sumsq[:, 10 + t:11 + t], ACT.Sqrt, bias=eps_rms[:, 0:1], scale=1.0 / D)\
                    .then_inc(n_std, 1)

            def norm_second(t):
                act.wait_ge(n_x1, t + 1)
                a(sg[:, t % 2, :], x1[:, t, :], ACT.Square, accum_out=sumsq[:, 20 + t:21 + t]).then_inc(n_sq, 1)
                act.wait_ge(n_sq, 2 * t + 2)
                a(std[:, 20 + t:21 + t], sumsq[:, 20 + t:21 + t], ACT.Sqrt, bias=eps_rms[:, 0:1], scale=1.0 / D)\
                    .then_inc(n_std, 1)

            def norm_hi(t):
                act.wait_ge(z_free[t % 2], Z01_N[t % 2] + t // 2 + 2)
                a(h_hi[:, :, P * t:P * (t + 1)], tmp[:, t % 2, :].rearrange("p (k n) -> p k n", k=KD), ACT.Copy)\
                    .then_inc(n_hi, 1)

            for t in range(NT):
                norm_first(t)
                norm_second(t)
                if t:
                    norm_hi(t - 1)
            norm_hi(NT - 1)

            def hidden(r, j, act_slot, n):
                act.wait_ge(unit_done, r + 1 + CREDIT)
                act.wait_ge(z_free[1], Z01_F[1] + n)
                a(sg[:, j, :], z[0][:], ACT.Silu).then_inc(z_free[0], 1)
                act.wait_ge(z_free[1], Z01_F[1] + n + 2)
                a(act_hi[:, act_slot, j, :], tmp[:, j, :], ACT.Copy).then_inc(ff_hi, 1)

            act.wait_ge(n_lo, NT)
            for j in range(2):
                hidden(U_FFN + 2 * j, j, 0, j)
            with act.Fori(0, (CHUNKS - 1) // 2) as i:
                for s in range(2):
                    c = 2 * i + 1 + s
                    for j in range(2):
                        if j == 0:
                            act.wait_ge(unit_done, U_FFN - 2 + 6 * c + CREDIT)
                        hidden(U_FFN - 2 + 6 * c + 3 * j, j, (s + 1) % 2, 2 * c + j)
            for t in range(NT):
                act.wait_ge(t_yt, t + 1)
                a(sg[:, t % 2, :], z[2 + t % 2][:], ACT.Square, accum_out=sumsq[:, 30 + t:31 + t]).then_inc(t_sq, 1)
                act.wait_ge(t_sq, t + 1)
                a(std[:, 30 + t:31 + t], sumsq[:, 30 + t:31 + t], ACT.Sqrt, bias=eps_rms[:, 0:1], scale=1.0 / D)\
                    .then_inc(t_std, 1)

        @block.vector
        def _(dve):
            for s, credit in ((m_olo, 1), (c_add, 1), (c_oev, 1), (tap_done, 1), (z_free[1], 1), (z_free[2], 1), (z_free[3], 1)):
                dve.sem_inc(s, credit)
            v = nc.vector

            def scaled(dst, src, scalar):
                return v.tensor_scalar(dst, src, scalar, None, ALU.mult)

            dve.wait_ge(rel_mm, 1)
            v.tensor_copy(e_rows[:, 0, :], z[1][0:SLOTS_H, 0:HALF]).then_inc(rel_rows, 1)
            v.tensor_copy(e_rows[:, 1, :], z[1][0:SLOTS_H, HALF:2 * HALF]).then_inc(rel_rows, 1)
            v.tensor_copy(e_rows[:, 2, :], z[0][0:SLOTS_H, HALF:2 * HALF]).then_inc(rel_rows, 1)

            def tokens_scaled(j):
                dve.wait_ge(std_done, j + 1)
                v.reciprocal(rstd[:, j:j + 1], std[:, j:j + 1]).then_inc(rstd_done, 1)
                dve.wait_ge(rstd_done, j + 1)
                if j >= 2:
                    dve.wait_ge(xt_mm, j - 1)
                src = mem_tok[:, j, :] if j < 2 else x_tok[:, j - 2, :]
                scaled(xs0[:, j % 2, :], src, rstd[:, j:j + 1]).then_inc(xs_done, 1)

            def tokens_gain(j):
                dve.wait_ge(xt_mm, j + 1)
                if j == 0:
                    dve.wait_ge(vec_set, 2)
                if j >= 2:
                    dve.wait_ge(flo_done, j - 1)
                col = V_MEM if j < 2 else V_MIX
                gain = vcols[:, col:col + KD].unsqueeze(2).to_broadcast([P, KD, P])
                v.tensor_tensor(f0[j % 2][:].rearrange("p (k n) -> p k n", k=KD),
                                z[2 + j % 2][:].rearrange("p (k n) -> p k n", k=KD), gain, ALU.mult).then_inc(f_done, 1)

            def tokens_lo(j):
                dve.wait_ge(fhi_done, j + 1)
                hi, lo = (mem_hi_t, mem_lo_t) if j < 2 else (h_hi, h_lo)
                at = slice(P * (j % 2 if j < 2 else j - 2), P * (j % 2 if j < 2 else j - 2) + P)
                v.tensor_tensor(lo[:, :, at], f0[j % 2][:].rearrange("p (k n) -> p k n", k=KD), hi[:, :, at],
                                ALU.subtract).then_inc(flo_done, 1)

            tokens_scaled(0)
            tokens_scaled(1)
            tokens_gain(0)
            tokens_gain(1)
            tokens_lo(0)
            tokens_lo(1)
            for j in range(2, 10):
                tokens_scaled(j)
                tokens_gain(j)
                if j > 2:
                    tokens_lo(j - 1)
            tokens_lo(9)
            v.memset(u[:, :, 0:PAD], 0.0).then_inc(u_pad, 1)
            v.memset(u[:, :, PAD + T:U_W], 0.0).then_inc(u_pad, 1)

            dve.wait_ge(vmem_set, 1)
            dve.wait_ge(z_free[0], 6 + 1)
            dve.wait_ge(z_free[1], 6 + 1)
            with dve.Fori(0, MEM_HEADS) as h:
                dve.wait_ge(unit_done, U_CONV + 2 * h + CREDIT)
                scaled(q_cur[:], q_mem[:, bass.ds(h, 1), :].rearrange("p a t -> p (a t)"), 1.0)
                scaled(k_cur[:], kv_t[:, bass.ds(h, 1), :].rearrange("p a t -> p (a t)"), 1.0)
                scaled(v_cur[:], v_mem[:, :, bass.ds(h, 1), :].rearrange("p c a n -> p c (a n)"), 1.0)\
                    .then_inc(m_cur, 1)
                for step in range(10):
                    if step < 8:
                        t = step
                        dve.wait_ge(m_qk, 8 * h + t + 1)
                        v.tensor_reduce(mstat[:, t % 2, 0:1], s_bank[:, t % 2, 0:N_MEM], X, ALU.max, negate=True)\
                            .then_inc(m_max, 1)
                        dve.wait_ge(m_exp, 8 * h + t + 3)
                        v.reciprocal(mstat[:, t % 2, 2:3], mstat[:, t % 2, 1:2]).then_inc(m_rden, 1)
                        dve.wait_ge(m_rden, 8 * h + t + 1)
                        scaled(p_mem[:, t % 2, :], p_mem[:, t % 2, :], mstat[:, t % 2, 2:3]).then_inc(m_pn, 1)
                    if step in (6, 9):
                        half = (step - 6) // 3
                        dve.wait_ge(m_pv, 2 * h + half + 3)
                        at = slice(HALF * half, HALF * (half + 1))
                        hi = m_hi[:, bass.ds(h, 1), at].rearrange("p a t -> p (a t)")
                        lo = m_lo[:, bass.ds(h, 1), at].rearrange("p a t -> p (a t)")
                        scaled(hi, o_bank, 1.0).then_inc(m_ohi, 1)
                        dve.wait_ge(m_ohi, 2 * h + half + 1)
                        v.tensor_tensor(lo, o_bank, hi, ALU.subtract).then_inc(m_olo, 1)
                dve.wait_ge(unit_done, U_CONV + 2 * h + 2 + CREDIT)
                dve.wait_ge(z_free[0], 6 + h + 2)
                v.tensor_tensor(u[:, bass.ds(h, 1), PAD:PAD + T].rearrange("p a t -> p (a t)"), z[1][:], sg_conv[:],
                                ALU.mult).then_inc(z_free[1], 1)

            dve.wait_ge(tables_in, 32)
            v.memset(bias2[0:64, :, 64:P], NEG).then_inc(bias_cut, 1)
            v.memset(bias2[64:P, :, 0:64], NEG).then_inc(bias_cut, 1)
            dve.wait_ge(bias_cut, 2)

            def dilated_pair(g, pair, sent_before):
                tile = 8 * pair
                d = DILATIONS[g]
                n = P if g == 2 else 2 * P
                head = 2 * (pair - 2 * g)
                dve.wait_ge(z_free[0], Z0_QKV + 2 * pair + 3)
                dve.wait_ge(z_free[1], Z1_QKV + pair + 2)
                dve.wait_ge(unit_done, U_QKV + 6 * pair + 6 + CREDIT)
                for j in range(3):
                    if d == 1:
                        dst, src = cur[:, j, :], nxt[:, j, :]
                    else:
                        dst = cur[:, j, :].rearrange("p (r l) -> p r l", r=d)
                        src = nxt[:, j, :].rearrange("p (l r) -> p r l", r=d)
                    v.tensor_copy(dst, src).then_inc(c_cur, 1)
                for step in range(10):
                    if step < 8:
                        t = step
                        dve.wait_ge(c_qk, tile + t + 1)
                        dve.wait_ge(c_exp, tile + t + 1)
                        if g == 2:
                            bias = bias2[:, bass.ds(head, 2), :]
                        else:
                            col = P - window(g, t)[1]
                            bias = bias01[:, bass.ds(SLOTS_H * g + head, 2), col:col + n]
                        v.tensor_tensor(sbias[:, t % 2, :, 0:n], s_bank[:, :, 0:n], bias, ALU.add).then_inc(c_add, 1)
                        dve.wait_ge(c_add, tile + t + 2)
                        if t % 4 == 0:
                            dve.wait_ge(heads_sent[t // 4], 16 * (1 + sent_before))
                        v.tensor_reduce(heads_out[:, t, :, ATT_E + 1:ATT_E + 2], sbias[:, t % 2, :, 0:n], X, ALU.max,
                                        negate=True).then_inc(c_max, 1)
                    if step >= 2:
                        t = step - 2
                        dve.wait_ge(c_pv, tile + t + 3)
                        v.tensor_copy(heads_out[:, t, :, 0:ATT_E], o_bank[:, 0:2 * ATT_E].rearrange(
                            "p (h e) -> p h e", h=2)).then_inc(c_oev, 1)

            for g in range(2):
                with dve.Fori(0, 2) as i:
                    dilated_pair(g, 2 * g + i, 2 * g + (1 + g) * i)
            dilated_pair(2, 4, 6)
            dilated_pair(2, 5, 8)

            steps = [0]

            def combine(op, *args):
                op(*args).then_inc(cmb_step, 1)
                steps[0] += 1
                dve.wait_ge(cmb_step, steps[0])

            def col(g, c):
                return parts[:, g, :, c]

            dve.wait_ge(parts_in, 48)
            combine(v.tensor_tensor, cmb[:, 0, :], col(0, ATT_E + 1), col(1, ATT_E + 1), ALU.min)
            combine(v.tensor_tensor, cmb[:, 0, :], cmb[:, 0, :], col(2, ATT_E + 1), ALU.min)
            for g in range(3):
                combine(v.tensor_tensor, cmb[:, 1 + g, :], cmb[:, 0, :], col(g, ATT_E + 1), ALU.subtract)
            dve.wait_ge(cmb_exp, 1)
            for g in range(3):
                combine(v.tensor_tensor, cmb[:, 1 + g, :], cmb[:, 4 + g, :], col(g, ATT_E), ALU.mult)
            combine(v.tensor_tensor, cmb[:, 7, :], cmb[:, 1, :], cmb[:, 2, :], ALU.add)
            combine(v.tensor_tensor, cmb[:, 7, :], cmb[:, 7, :], cmb[:, 3, :], ALU.add)
            combine(v.reciprocal, cmb[:, 8, :], cmb[:, 7, :])
            total = a_tok[:].rearrange("p t (h e) -> p (t h) e", h=SLOTS_H)
            for g in range(3):
                combine(v.tensor_tensor, cmb[:, 1 + g, :], cmb[:, 4 + g, :], cmb[:, 8, :], ALU.mult)
                share = cmb[:, 1 + g, :].unsqueeze(2).to_broadcast([P, NT * SLOTS_H, ATT_E])
                combine(v.tensor_tensor, total if g == 0 else wsum[:], parts[:, g, :, 0:ATT_E], share, ALU.mult)
                if g == 1:
                    combine(v.tensor_tensor, total, total, wsum[:], ALU.add)
            v.tensor_tensor(total, total, wsum[:], ALU.add).then_inc(a_tok_set, 1)

            TAP_ORDER = [k for k in range(TAPS) if k != PAD] + [PAD]

            def conv_taps(c, first, last):
                def row(t, at, n):
                    return t[:, bass.ds(c, 1), at:at + n].rearrange("p a t -> p (a t)")

                for n in range(first, last):
                    k = TAP_ORDER[n]
                    w = taps[:, k, bass.ds(c, 1)]
                    dve.wait_ge(tap_done, TAPS * c + n + 1)
                    if n == 0:
                        op = v.tensor_scalar(tmp[:, 1, :], row(u, k, T), w, vcols[:, bass.ds(V_DWB + c, 1)],
                                             ALU.mult, ALU.add)
                    else:
                        op = v.scalar_tensor_tensor(row(u, PAD, T) if n == TAPS - 1 else tmp[:, 1, :], row(u, k, T), w,
                                                    tmp[:, 1, :], ALU.mult, ALU.add)
                    op.then_inc(tap_done, 1)

            def branch(b, z01, z23):
                with dve.Fori(0, 2) as i:
                    for j in range(2):
                        for q in range(2):
                            n = 2 * j + q
                            dve.wait_ge(unit_done, U_BR + 12 * b + 6 * i + 3 * j + 3 + CREDIT)
                            dve.wait_ge(z_free[q], z01[q] + 2 * i + j + 2)
                            acc_d = acc[:, bass.ds(4 * i + n, 1), :].rearrange("p a t -> p (a t)")
                            if b == 0:
                                v.tensor_tensor(acc_d, z[2 + q][:], sg[:, q, :], ALU.mult).then_inc(z_free[2 + q], 1)
                            else:
                                f = tmp[:, 0 if b == 1 else q, :]
                                v.tensor_tensor(f, z[2 + q][:], sg[:, q, :], ALU.mult).then_inc(z_free[2 + q], 1)
                                dve.wait_ge(z_free[2 + q], z23 + 2 * i + j + 2)
                                v.tensor_tensor(acc_d if b == 1 else f, acc_d, f, ALU.add)\
                                    .then_inc(br_tmp if b == 1 else br_f, 1)
                            if b < 2:
                                conv_taps(2 * b + i, 8 * n, min(8 * n + 8, TAPS))
                            else:
                                dve.wait_ge(br_hi, 4 * i + n + 1)
                                v.tensor_tensor(merged_lo[:, bass.ds(4 * i + n, 1), :].rearrange("p a t -> p (a t)"), f,
                                                merged_hi[:, bass.ds(4 * i + n, 1), :].rearrange("p a t -> p (a t)"),
                                                ALU.subtract).then_inc(br_lo, 1)

            branch(0, Z01_BR, 0)
            for c in range(2):
                dve.wait_ge(ahi_set, c + 1)
                v.tensor_tensor(a_lo[:, c, :], z[c][:], a_hi[:, c, :], ALU.subtract).then_inc(z_free[c], 1)
            branch(1, Z01_B1, 4)
            dve.wait_ge(ln_mean, 1)
            for c in range(CT):
                v.tensor_tensor(u[:, c, PAD:PAD + T], u[:, c, PAD:PAD + T], z[2][:], ALU.subtract).then_inc(ln_xc, 1)
            dve.wait_ge(ln_std, 1)
            v.reciprocal(sg[:, 1, :], sg[:, 0, :]).then_inc(ln_rstd, 1)
            dve.wait_ge(ln_rstd, 1)

            def ln_scale(c):
                v.tensor_tensor(u[:, c, PAD:PAD + T], u[:, c, PAD:PAD + T], sg[:, 1, :], ALU.mult).then_inc(ln_xn, 1)

            def ln_low(c):
                dve.wait_ge(ln_hi, c + 1)
                v.tensor_tensor(c_lo[:, c, :], tmp[:, c % 2, :], c_hi[:, c, :], ALU.subtract).then_inc(ln_lo, 1)

            ln_scale(0)
            for c in range(1, CT):
                ln_scale(c)
                ln_low(c - 1)
            ln_low(CT - 1)
            branch(2, Z01_B2, 8)

            def norm_first(t):
                dve.wait_ge(n_std, 2 * t + 1)
                v.reciprocal(rstd[:, 10 + t:11 + t], std[:, 10 + t:11 + t]).then_inc(n_rstd, 1)
                dve.wait_ge(n_rstd, 2 * t + 1)
                v.scalar_tensor_tensor(x1[:, t, :], z[2 + t % 2][:], rstd[:, 10 + t:11 + t], post_gain[:], ALU.mult,
                                       ALU.mult).then_inc(z_free[2 + t % 2], 1)
                dve.wait_ge(z_free[2 + t % 2], Z23_N + t // 2 + 2)
                dve.wait_ge(x_again_t[t], 16)
                v.tensor_tensor(x1[:, t, :], x1[:, t, :], x_again[:, t, :], ALU.add).then_inc(n_x1, 1)

            def norm_second(t):
                dve.wait_ge(n_std, 2 * t + 2)
                v.reciprocal(rstd[:, 20 + t:21 + t], std[:, 20 + t:21 + t]).then_inc(n_rstd, 1)
                dve.wait_ge(n_rstd, 2 * t + 2)
                scaled(sg[:, t % 2, :], x1[:, t, :], rstd[:, 20 + t:21 + t]).then_inc(n_xs, 1)

            def norm_split(t):
                dve.wait_ge(n_xt, t + 1)
                gain = vcols[:, V_FFN:V_FFN + KD].unsqueeze(2).to_broadcast([P, KD, P])
                f = tmp[:, t % 2, :].rearrange("p (k n) -> p k n", k=KD)
                v.tensor_tensor(f, z[t % 2][:].rearrange("p (k n) -> p k n", k=KD), gain, ALU.mult)\
                    .then_inc(z_free[t % 2], 1)
                dve.wait_ge(n_hi, t + 1)
                at = slice(P * t, P * (t + 1))
                v.tensor_tensor(h_lo[:, :, at], f, h_hi[:, :, at], ALU.subtract).then_inc(n_lo, 1)

            dve.wait_ge(gain_in, 16)
            for t in range(NT):
                norm_first(t)
                norm_second(t)
                if t:
                    norm_split(t - 1)
            norm_split(NT - 1)

            def hidden(r, j, act_slot, n):
                dve.wait_ge(unit_done, r + 2 + CREDIT)
                dve.wait_ge(z_free[0], Z01_F[0] + n + 2)
                v.tensor_tensor(tmp[:, j, :], z[1][:], sg[:, j, :], ALU.mult).then_inc(z_free[1], 1)
                dve.wait_ge(ff_hi, n + 1)
                v.tensor_tensor(act_lo[:, act_slot, j, :], tmp[:, j, :], act_hi[:, act_slot, j, :], ALU.subtract)\
                    .then_inc(ff_lo, 1)

            def ffn_out(r, m, half):
                for q in range(4):
                    if q < 3:
                        dve.wait_ge(ff_y, 3 * m + q + 1)
                    else:
                        dve.wait_ge(unit_done, r + 1 + CREDIT)
                    y = y_t[:, 4 * half + q, :]
                    v.tensor_tensor(y, z[2 + q % 2][:], y, ALU.add).then_inc(z_free[2 + q % 2], 1)

            for j in range(2):
                hidden(U_FFN + 2 * j, j, 0, j)
            dve.wait_ge(y_zero, 1)
            with dve.Fori(0, (CHUNKS - 1) // 2) as i:
                for s in range(2):
                    c = 2 * i + 1 + s
                    for j in range(2):
                        r = U_FFN - 2 + 6 * c + 3 * j
                        hidden(r, j, (s + 1) % 2, 2 * c + j)
                        ffn_out(r + 2, 2 * (c - 1) + j, j)
            for half in range(2):
                ffn_out(N_UNITS - 2 + half, 2 * (CHUNKS - 1) + half, half)
            dve.wait_ge(gain_in, 32)
            for t in range(NT):
                dve.wait_ge(t_std, t + 1)
                v.reciprocal(rstd[:, 30 + t:31 + t], std[:, 30 + t:31 + t]).then_inc(t_rstd, 1)
                dve.wait_ge(t_rstd, t + 1)
                v.scalar_tensor_tensor(tmp[:, t % 2, :], z[2 + t % 2][:], rstd[:, 30 + t:31 + t], post_gain[:], ALU.mult,
                                       ALU.mult).then_inc(z_free[2 + t % 2], 1)
                dve.wait_ge(z_free[2 + t % 2], Z23_T + t // 2 + 2)
                v.tensor_tensor(x1[:, t, :], x1[:, t, :], tmp[:, t % 2, :], ALU.add).then_inc(t_out, 1)


INPUTS = ("x", "mem", "rel_bias", "norm_mix_pre", "w_in", "b_gate", "conv_dw", "conv_dw_bias", "conv_ln_g",
          "conv_ln_b", "w_conv_out", "w_att_out", "norm_mem", "w_mem_kv", "w_mem_out", "w_out", "norm_mix_post",
          "norm_ffn_pre", "w_ffn_in", "w_ffn_out", "norm_ffn_post")


def bucket_table():
    import numpy as np
    import math
    half, exact, largest = 16, 8, 1024
    table = np.zeros((3, 33, REL), np.float32)
    for g, dilation in enumerate(DILATIONS):
        for col in range(REL):
            off = col - REL // 2
            if abs(off) > RADIUS:
                table[g, 32, col] = NEG
                continue
            n = abs(off * dilation)
            bucket = n
            if n >= exact:
                bucket = min(exact + int(math.log(n / exact) / math.log(largest / exact) * (half - exact)), half - 1)
            table[g, bucket + (half if off > 0 else 0), col] = 1.0
    return table


def kernel(**inputs):
    import numpy as np
    import concourse.bacc as bacc
    from concourse.bass_utils import run_bass_kernel_spmd

    nc = bacc.Bacc("TRN2", target_bir_lowering=False, num_devices=1)
    arrays = {name: np.ascontiguousarray(inputs[name]) for name in INPUTS}
    arrays["identity"] = np.eye(P, dtype=np.float32)
    arrays["bucket_hot"] = bucket_table()
    args = [nc.dram_tensor(f"in_{name}", a.shape, mybir.dt.from_np(a.dtype), kind="ExternalInput").ap()
            for name, a in arrays.items()]
    result = nc.dram_tensor("result", (1, T, D), mybir.dt.float32, kind="ExternalOutput").ap()
    hybrid_layer(nc, *args, result)
    ran = run_bass_kernel_spmd(nc, [{f"in_{name}": a for name, a in arrays.items()}], core_ids=[0])
    return ran.results[0]["result"]
```

```python
import concourse.bass as bass
from concourse import mybir
from contextlib import ExitStack

P = 128
D = 1024
T = 1024
NT = T // P
KD = D // P
HALF = 512
N_MEM = 256
MEM_HEADS = 4
CONV_W = 512
CT = CONV_W // P
TAPS = 31
PAD = TAPS // 2
ATT_W = 768
ATT_E = 64
SLOTS_H = 4
HIDDEN = 2816
CHUNKS = HIDDEN // 256
DILATIONS = (1, 4, 16)
RADIUS = 64
REL = 512
NEG = -1e30
C_ATT = 2 * CONV_W
C_MEM = C_ATT + 3 * ATT_W
C_GATE = C_MEM + MEM_HEADS * P
ROW = ATT_E + 2

V_MIX, V_MEM, V_FFN, V_GATE, V_DWB, V_LNG, V_LNB = 0, 8, 16, 24, 48, 52, 56
N_VEC = 60

U_KV, U_MQ, U_CONV, U_QKV, U_BR, U_OUT, U_FFN = 0, 8, 12, 20, 56, 92, 100
N_UNITS = U_FFN + 6 * CHUNKS
CREDIT = 2


def window(g, t):
    if g == 0:
        start = min(max(P * t - RADIUS, 0), T - 2 * P)
        return start, P * t - start
    if g == 1:
        return 2 * P * (t // 2), P * (t % 2)
    return P * t, 0


V_CHUNKS = ([0, P] + [RADIUS + P * k for k in range(7)] + [T - 2 * P, T - P],
            [P * k for k in range(NT)], [P * k for k in range(NT)])
V_BATCHES = (3, 2, 2)


def v_batches_before(pair):
    return sum(2 * V_BATCHES[g] for g in range(pair // 2)) + (pair % 2) * V_BATCHES[pair // 2]


def hybrid_layer(nc, x, mem, rel_bias, norm_mix_pre, w_in, b_gate, conv_dw, conv_dw_bias, conv_ln_g,
                 conv_ln_b, w_conv_out, w_att_out, norm_mem, w_mem_kv, w_mem_out, w_out,
                 norm_mix_post, norm_ffn_pre, w_ffn_in, w_ffn_out, norm_ffn_post,
                 identity, bucket_hot, out):
    f32 = mybir.dt.float32
    f32r = mybir.dt.float32r
    u8 = mybir.dt.uint8
    ALU = mybir.AluOpType
    ACT = mybir.ActivationFunctionType
    X = mybir.AxisListType.X
    ctx = ExitStack()

    BASE = 16512

    def sb(name, shape, offset, dt=f32):
        return nc.alloc_sbuf_tensor_at(name, shape, dt, offset=BASE + offset)

    KB = 1024
    h_hi = sb("h_hi", [P, KD, T], 0, f32r)
    h_lo = sb("h_lo", [P, KD, T], 32 * KB, f32r)
    raw = sb("raw", [P, 2, 1024], 64 * KB)
    w_hi = sb("w_hi", [P, 2, 1024], 72 * KB, f32r)
    w_lo = sb("w_lo", [P, 2, 1024], 80 * KB, f32r)
    o = 88 * KB
    ident = sb("ident", [P, P], o)
    ones = sb("ones", [P, P], o + 512)
    zeros = sb("zeros", [P, P], o + 1024)
    vcols = sb("vcols", [P, N_VEC], o + 1536)
    taps = sb("taps", [P, TAPS, CT], o + 2048)
    sumsq = sb("sumsq", [P, 40], o + 2560)
    std = sb("std", [P, 40], o + 2720)
    rstd = sb("rstd", [P, 40], o + 2880)
    eps_rms = sb("eps_rms", [P, 8], o + 3040)
    eps_ln = sb("eps_ln", [P, 8], o + 3072)
    post_gain = sb("post_gain", [P, D], o + 3104)
    conv_sum = sb("conv_sum", [P, T], o + 3104)
    R = o + 3104 + 4096
    U_W = T + 2 * PAD
    u = sb("u", [P, CT, U_W], R)
    ATT = R + CT * U_W * 4
    MEM = ATT + 16 * KB
    ACC = MEM + 32 * KB
    SG = ACC + 32 * KB
    TMP = SG + 8 * KB
    x_tok = sb("x_tok", [P, NT, D], R)
    mem_hi_t = sb("mem_hi_t", [P, KD, N_MEM], MEM, f32r)
    mem_lo_t = sb("mem_lo_t", [P, KD, N_MEM], MEM + 8 * KB, f32r)
    mem_tok = sb("mem_tok", [P, 2, D], MEM + 16 * KB)
    xs0 = sb("xs0", [P, 2, D], MEM + 24 * KB)
    f0 = [sb("f0a", [P, D], o + 3104), sb("f0b", [P, D], ACC + 8 * KB)]
    bhot = sb("bhot", [33, 3, REL], ACC + 12 * KB)
    rel = sb("rel", [33, 12], ACC + 18 * KB)
    e_rows = sb("e_rows", [SLOTS_H, 3, REL], ACC + 20 * KB)
    junk0 = sb("junk0", [P, D], ACC + 28 * KB)
    vec_rows = sb("vec_rows", [N_VEC, P], ACC + 26 * KB)
    tap_rows = sb("tap_rows", [TAPS * CT, P], ACC + 26 * KB + 512)
    q_mem = sb("q_mem", [P, MEM_HEADS, T], ATT)
    kv_t = sb("kv_t", [P, 2 * MEM_HEADS, N_MEM], ACC)
    v_mem = sb("v_mem", [P, 2, MEM_HEADS, P], ACC + 8 * KB)
    q_cur = sb("q_cur", [P, T], ACC + 12 * KB)
    v_cur = sb("v_cur", [P, 2, P], ACC + 17 * KB)
    p_mem = sb("p_mem", [P, 2, N_MEM], ACC + 18 * KB)
    pt_mem = sb("pt_mem", [P, 2, 2, HALF], ACC + 20 * KB)
    sg_conv = sb("sg_conv", [P, T], ACC + 28 * KB)
    mstat = sb("mstat", [P, 2, 4], ACC + 46 * KB)
    m_hi = sb("m_hi", [P, MEM_HEADS, T], MEM, f32r)
    m_lo = sb("m_lo", [P, MEM_HEADS, T], MEM + 16 * KB, f32r)
    nxt = sb("nxt", [P, 3, T], ATT)
    prob = sb("prob", [P, 2, 2, 256], ATT + 12 * KB)
    cur = sb("cur", [P, 3, T], ACC)
    v_tok = sb("v_tok", [P, 12, P], ACC + 12 * KB)
    sbias = sb("sbias", [P, 2, 2, 256], ACC + 18 * KB)
    p_t = sb("p_t", [P, 2, 4, P], ACC + 22 * KB)
    heads_out = sb("heads_out", [P, NT, 2, ROW], ACC + 26 * KB)
    bias01 = sb("bias01", [P, 2 * SLOTS_H, 384], ACC + 32 * KB)
    bias2 = sb("bias2", [P, SLOTS_H, P], ACC + 44 * KB)
    parts = sb("parts", [P, 3, NT * SLOTS_H, ROW], ACC)
    a_tok = sb("a_tok", [P, NT, SLOTS_H * ATT_E], ATT)
    cmb = sb("cmb", [P, 10, NT * SLOTS_H], ACC + 26 * KB)
    wsum = sb("wsum", [P, NT * SLOTS_H, ATT_E], ATT + 8 * KB)
    a_hi = sb("a_hi", [P, 2, T], ATT, f32r)
    a_lo = sb("a_lo", [P, 2, T], ATT + 8 * KB, f32r)
    acc = sb("acc", [P, KD, T], ACC)
    sg = sb("sg", [P, 2, T], SG)
    tmp = sb("tmp", [P, 2, T], TMP)
    ln_sq4 = sb("ln_sq4", [P, CT, T], MEM)
    ln_dev = sb("ln_dev", [P, 2, T], MEM + 16 * KB)
    c_hi = sb("c_hi", [P, CT, T], ATT, f32r)
    c_lo = sb("c_lo", [P, CT, T], R, f32r)
    merged_hi = sb("merged_hi", [P, KD, T], MEM, f32r)
    merged_lo = sb("merged_lo", [P, KD, T], ACC, f32r)
    y_t = sb("y_t", [P, KD, T], R)
    x1 = sb("x1", [P, NT, D], MEM)
    x_again = sb("x_again", [P, NT, D], ACC)
    act_hi = sb("act_hi", [P, 2, 2, T], ACC, f32r)
    act_lo = sb("act_lo", [P, 2, 2, T], ACC + 16 * KB, f32r)

    rel_scratch = nc.dram_tensor("rel_scratch", (3 * SLOTS_H, P, REL), f32)
    att_scratch = nc.dram_tensor("att_scratch", (3, T, SLOTS_H * ROW), f32).ap()

    with ctx:
        z = [ctx.enter_context(nc.psum_tensor(f"z{k}", [P, 1024], f32)) for k in range(4)]
        s_bank = z[2][:].rearrange("p (b n) -> p b n", b=2)
        t_bank = z[3][:, 0:512]
        o_bank = z[3][:, 512:1024]

        def sem(name):
            return ctx.enter_context(nc.semaphore(name))

        raw_ready = [sem("raw_ready0"), sem("raw_ready1")]
        hi_done = sem("hi_done")
        split_done = sem("split_done")
        unit_done = sem("unit_done")
        z_free = [sem(f"z{k}_free") for k in range(4)]
        consts_in, ident_in, rel_in, tables_in = (sem(n) for n in ("consts_in", "ident_in", "rel_in", "tables_in"))
        mem_in = [sem("mem_in0"), sem("mem_in1")]
        x_in = [sem(f"x_in{t}") for t in range(NT // 2)]
        rel_ones, rel_mm, rel_rows, rel_out = (sem(n) for n in ("rel_ones", "rel_mm", "rel_rows", "rel_out"))
        consts_set, vec_mm, vec_set = (sem(n) for n in ("consts_set", "vec_mm", "vec_set"))
        sq_done, std_done, rstd_done, xs_done = (sem(n) for n in ("sq_done", "std_done", "rstd_done", "xs_done"))
        xt_mm, f_done, fhi_done, flo_done = (sem(n) for n in ("xt_mm", "f_done", "fhi_done", "flo_done"))
        vmem_mm, vmem_set = sem("vmem_mm"), sem("vmem_set")
        m_cur, m_qk, m_max, m_exp, m_rden, m_pn, m_t, m_pt, m_pv, m_ohi, m_olo = (sem(n) for n in (
            "m_cur", "m_qk", "m_max", "m_exp", "m_rden", "m_pn", "m_t", "m_pt", "m_pv", "m_ohi", "m_olo"))
        u_pad = sem("u_pad")
        c_cur, c_qk, c_add, c_max, c_exp, c_t, c_pt, c_pv, c_oev, c_vt, c_vset = (sem(n) for n in (
            "c_cur", "c_qk", "c_add", "c_max", "c_exp", "c_t", "c_pt", "c_pv", "c_oev", "c_vt",
            "c_vset"))
        heads_sent = [sem("heads_sent0"), sem("heads_sent1")]
        bias_cut = sem("bias_cut")
        parts_in, cmb_step, cmb_exp, a_tok_set, at_mm, ahi_set, a_set = (sem(n) for n in (
            "parts_in", "cmb_step", "cmb_exp", "a_tok_set", "at_mm", "ahi_set", "a_set"))
        br_tmp, br_f, br_hi, br_lo, tap_done = (sem(n) for n in ("br_tmp", "br_f", "br_hi", "br_lo", "tap_done"))
        proj_half, acc_kept = sem("proj_half"), sem("acc_kept")
        ln_mean, ln_xc, ln_sq, ln_var, ln_std, ln_rstd, ln_xn, ln_f, ln_hi, ln_lo = (sem(n) for n in (
            "ln_mean", "ln_xc", "ln_sq", "ln_var", "ln_std", "ln_rstd", "ln_xn", "ln_f", "ln_hi", "ln_lo"))
        y_set, n_yt, n_sq, n_std, n_rstd, n_t1, n_x1, n_xs, n_xt, n_f, n_hi, n_lo, x_again_in, gain_in = (
            sem(n) for n in ("y_set", "n_yt", "n_sq", "n_std", "n_rstd", "n_t1", "n_x1", "n_xs", "n_xt", "n_f",
                             "n_hi", "n_lo", "x_again_in", "gain_in"))
        x_again_t = [sem(f"x_again{t}") for t in range(NT)]
        y_zero, ff_f, ff_hi, ff_lo, ff_y = (sem(n) for n in ("y_zero", "ff_f", "ff_hi", "ff_lo", "ff_y"))
        t_sq, t_std, t_rstd, t_t1, t_out, t_yt, stored = (sem(n) for n in (
            "t_sq", "t_std", "t_rstd", "t_t1", "t_out", "t_yt", "stored"))

        Z0_QKV = Z1_QKV = 4 + 2 + MEM_HEADS
        Z01_BR = (Z0_QKV + 12, Z1_QKV + 6)
        Z01_B1 = tuple(n + 5 for n in Z01_BR)
        Z01_B2 = tuple(n + 4 for n in Z01_B1)
        Z01_OUT = tuple(n + 4 for n in Z01_B2)
        Z01_N = tuple(n + 4 for n in Z01_OUT)
        Z01_F = tuple(n + 4 for n in Z01_N)
        Z23_B2 = 4 + 4 + 1
        Z23_N = Z23_B2 + 4
        Z23_F = Z23_N + 4
        Z23_T = Z23_F + 4 * CHUNKS

        block = ctx.enter_context(nc.Block())

        def unit_ready(pe, r):
            pe.wait_ge(split_done, r + CREDIT + 1)

        kv_v = w_mem_kv.rearrange("o (k p) n -> p (o k) n", p=P)
        in_v = w_in.rearrange("o (k p) n -> p (o k) n", p=P)
        conv_v = w_conv_out.rearrange("o (k p) n -> p (o k) n", p=P)
        att_v = w_att_out.rearrange("o (k p) n -> p (o k) n", p=P)
        memo_v = w_mem_out.rearrange("o (k p) n -> p (o k) n", p=P)
        out_v = w_out.rearrange("o (k p) n -> p (o k) n", p=P)
        ffi_v = w_ffn_in.rearrange("o (k p) n -> p (o k) n", p=P)
        ffo_v = w_ffn_out.rearrange("o (k p) n -> p (o k) n", p=P)

        @block.sync
        def _(sp):
            def load(r, slot, src, row, k, col, n, free=True):
                src = src.bitcast(u8)
                (row_step, _), (tile_step, _), _ = src.ap
                at = tile_step * row + 4 * col
                src = bass.AP(src.tensor, at if isinstance(at, int) else sp.snap(sp.to_reg(at)),
                              [[row_step, P], [tile_step, k], [1, 4 * n]])
                if free:
                    sp.wait_ge(split_done, r + 1)
                sp.dma_start(raw[:, slot, 0:k * n].rearrange("p (k n) -> p k n", k=k).bitcast(u8), src)\
                    .then_inc(raw_ready[slot], 16)

            sp.dma_start(mem_tok[:, 0, :], mem[0, 0:P, :]).then_inc(mem_in[0], 16)
            sp.dma_start(ident[:], identity).then_inc(ident_in, 16)
            sp.dma_start(mem_tok[:, 1, :], mem[0, P:2 * P, :]).then_inc(mem_in[1], 16)
            load(0, 0, kv_v, 0, KD, 0, P, free=False)
            for row, v, n in ((V_MIX, norm_mix_pre, 8), (V_MEM, norm_mem, 8), (V_FFN, norm_ffn_pre, 8),
                              (V_GATE, b_gate, 24), (V_DWB, conv_dw_bias, 4), (V_LNG, conv_ln_g, 4),
                              (V_LNB, conv_ln_b, 4)):
                sp.dma_start(vec_rows[row:row + n, :], v.rearrange("o (k p) -> (o k) p", p=P))\
                    .then_inc(consts_in, 16)
            sp.dma_start(tap_rows[:], conv_dw.rearrange("o j (c p) -> (o j c) p", p=P)).then_inc(consts_in, 16)
            load(1, 1, kv_v, 0, KD, P, P, free=False)
            sp.dma_start(bhot[:], bucket_hot.rearrange("g b n -> b g n")).then_inc(rel_in, 16)
            with sp.Fori(1, 4) as i:
                for slot in range(2):
                    load(U_KV + 2 * i + slot, slot, kv_v, 0, KD, 2 * P * i + P * slot, P)
            with sp.Fori(0, 2) as i:
                for slot in range(2):
                    load(U_MQ + 2 * i + slot, slot, in_v, 0, KD, C_MEM + 2 * P * i + P * slot, P)
            with sp.Fori(0, CT) as i:
                load(U_CONV + 2 * i, 0, in_v, 0, KD, CONV_W + P * i, P)
                load(U_CONV + 2 * i + 1, 1, in_v, 0, KD, P * i, P)
            sp.wait_ge(rel_out, 48)
            with nc.allow_non_contiguous_dma(reason="Toeplitz rows"):
                sp.dma_start(bias01[:], bass.AP(rel_scratch, P, [[REL - 1, P], [P * REL, 8], [1, 384]]))\
                    .then_inc(tables_in, 16)
                sp.dma_start(bias2[:], bass.AP(rel_scratch, 8 * P * REL + 2 * P,
                                               [[REL - 1, P], [P * REL, 4], [1, P]])).then_inc(tables_in, 16)
            with sp.Fori(0, 6) as i:
                for j in range(6):
                    load(U_QKV + 6 * i + j, j % 2,
                         in_v, 4 * (j % 2), 4, C_ATT + ATT_W * (j // 2) + P * i, P)
            for b, (proj, k) in enumerate(((memo_v, 4), (att_v, 2), (conv_v, 4))):
                branch = (2, 1, 0)[b]
                with sp.Fori(0, 2) as i:
                    for j in range(2):
                        for q in range(2):
                            r = U_BR + 12 * b + 6 * i + 3 * j + q
                            load(r, (3 * j + q) % 2,
                                 in_v, 0, KD, C_GATE + D * branch + HALF * i + P * (2 * j + q), P)
                        load(U_BR + 12 * b + 6 * i + 3 * j + 2, (3 * j + 2) % 2,
                             proj, 0, k, HALF * i + 256 * j, 256)
            with sp.Fori(0, 4) as i:
                for slot in range(2):
                    load(U_OUT + 2 * i + slot, slot, out_v, 0, KD, 2 * P * i + P * slot, P)
            sp.dma_start(post_gain[:], norm_mix_post.to_broadcast([P, D])).then_inc(gain_in, 16)

            def load_ffn_in(r, slot, tile, gate):
                load(r, slot, ffi_v, 0, KD, (0 if gate else HIDDEN) + P * tile, P)

            def load_ffn_out(r, slot, chunk, half):
                load(r, slot, ffo_v, 2 * chunk, 2, HALF * half, HALF)

            load_ffn_in(U_FFN, 0, 0, True)
            load_ffn_in(U_FFN + 1, 1, 0, False)
            sp.wait_ge(unit_done, U_FFN + CREDIT)
            for t in range(NT):
                sp.dma_start(x_again[:, t, :], x[0, P * t:P * (t + 1), :]).then_inc(x_again_t[t], 16)
            load_ffn_in(U_FFN + 2, 0, 1, True)
            load_ffn_in(U_FFN + 3, 1, 1, False)
            sp.wait_ge(n_x1, NT)
            sp.dma_start(post_gain[:], norm_ffn_post.to_broadcast([P, D])).then_inc(gain_in, 16)
            with sp.Fori(1, CHUNKS) as c:
                r = U_FFN - 2 + 6 * c
                for j in range(2):
                    load_ffn_in(r + 3 * j, (3 * j) % 2, 2 * c + j, True)
                    load_ffn_in(r + 3 * j + 1, (3 * j + 1) % 2, 2 * c + j, False)
                    load_ffn_out(r + 3 * j + 2, (3 * j + 2) % 2, c - 1, j)
            for half in range(2):
                load_ffn_out(N_UNITS - 2 + half, half, CHUNKS - 1, half)
            for t in range(NT):
                sp.wait_ge(t_out, t + 1)
                sp.dma_start(out[0, P * t:P * (t + 1), :], x1[:, t, :]).then_inc(stored, 16)
            sp.wait_ge(stored, 16 * NT)

        @block.gpsimd
        def _(pool):
            pool.sem_inc(split_done, CREDIT)
            nc.gpsimd.memset(zeros[:], 0.0).then_inc(consts_set, 1)
            nc.gpsimd.memset(eps_rms[:], 1e-6).then_inc(consts_set, 1)
            nc.gpsimd.memset(eps_ln[:], 1e-5).then_inc(consts_set, 1)
            nc.gpsimd.memset(ones[:], 1.0 / CONV_W).then_inc(consts_set, 1)
            nc.gpsimd.memset(rel[:], 1.0).then_inc(rel_ones, 1)
            pool.wait_ge(consts_set, 4)

            def split(r, n, slot, width=1024, free=True):
                pool.wait_ge(raw_ready[slot], 16 * (n + 1))
                if free:
                    pool.wait_ge(unit_done, r + 1)
                a = width // P
                view = [w[:, slot, 0:width].rearrange("p (a b) -> p a b", a=a) for w in (raw, w_hi, w_lo)]
                nc.gpsimd.tensor_tensor(view[1], view[0], zeros[:].unsqueeze(1).to_broadcast([P, a, P]),
                                        ALU.add).then_inc(hi_done, 1)
                pool.wait_ge(hi_done, r + 1)
                nc.gpsimd.tensor_tensor(view[2], view[0], view[1], ALU.subtract).then_inc(split_done, 1)

            def split_run(first, last, widths=(1024, 1024)):
                per = len(widths)
                with pool.Fori(0, (last - first) // per) as i:
                    for j, width in enumerate(widths):
                        split(first + per * i + j, first // 2 + per // 2 * i + j // 2, j % 2, width)

            for slot in range(2):
                split(slot, 0, slot, free=False)
            split_run(2, U_QKV)
            split_run(U_QKV, U_BR, (512, 512))
            split_run(U_BR, U_BR + 12)
            split_run(U_BR + 12, U_BR + 24, (1024, 1024, 512, 1024, 1024, 512))
            split_run(U_BR + 24, U_FFN + 2)
            pool.wait_ge(n_yt, NT)
            nc.gpsimd.memset(y_t[:], 0.0).then_inc(y_zero, 1)
            split_run(U_FFN + 2, N_UNITS)

        SPLIT_PRODUCTS = ("hh", "hl", "lh")

        def products(slot, k_tiles, pick, cols, rhs_hi, rhs_lo, dst, rhs_n, first=0, last=None):
            todo = []
            halves = (rhs_n + HALF - 1) // HALF
            n = min(rhs_n, HALF)
            for h in range(halves):
                for k in range(k_tiles):
                    for what in SPLIT_PRODUCTS:
                        w = w_hi if what[0] == "h" else w_lo
                        m = rhs_hi if what[1] == "h" else rhs_lo
                        todo.append((dst[:, h * HALF:h * HALF + n], w[:, slot, pick(k) + cols:pick(k) + cols + P],
                                     m(k, h * HALF, n), first == 0 and k == 0 and what == "hh",
                                     last is None and k == k_tiles - 1 and what == "lh"))
            return todo

        def issue(todo):
            for dst, w, m, start, stop in todo:
                mm = nc.tensor.matmul(dst, w, m, start=start, stop=stop)
            return mm

        def h_rhs(t):
            return lambda k, at, n: t[:, k, at:at + n]

        def unit_todo(slot, dst):
            return products(slot, KD, lambda k: P * k, 0, h_rhs(h_hi), h_rhs(h_lo), dst, T)

        @block.tensor
        def _(pe):
            pe.sem_inc(unit_done, CREDIT)
            for s in (m_t, m_pv, c_t, c_pv):
                pe.sem_inc(s, 2)

            def transposes(dst, src, n, done):
                for k in range(n):
                    mm = nc.tensor.transpose(dst[:, P * k:P * (k + 1)], src[:, P * k:P * (k + 1)], ident[:])
                mm.then_inc(done, 1)

            pe.wait_ge(ident_in, 16)
            for t in range(2):
                pe.wait_ge(xs_done, t + 1)
                transposes(z[2 + t], xs0[:, t], KD, xt_mm)
            pe.wait_ge(consts_in, 16 * 8)
            nc.tensor.transpose(z[0][:, 0:N_VEC], vec_rows[:], ident[0:N_VEC, 0:N_VEC])
            nc.tensor.transpose(z[0][:, P:P + TAPS * CT], tap_rows[:], ident[0:TAPS * CT, 0:TAPS * CT])\
                .then_inc(vec_mm, 1)
            pe.wait_ge(rel_in, 32)
            for g in range(3):
                dst = z[1][0:SLOTS_H, HALF * g:HALF * (g + 1)] if g < 2 else z[0][0:SLOTS_H, HALF:2 * HALF]
                mm = nc.tensor.matmul(dst, rel[:, SLOTS_H * g:SLOTS_H * (g + 1)], bhot[:, g, :], start=True, stop=True)
            mm.then_inc(rel_mm, 1)
            pe.wait_ge(flo_done, 2)
            pe.wait_ge(rel_rows, 3)
            with pe.Fori(0, 4) as i:
                for s in range(2):
                    n = 2 * i + s
                    unit_ready(pe, U_KV + n)
                    pe.wait_ge(z_free[s], i + 1)
                    issue(products(s, KD, lambda k: P * k, 0, h_rhs(mem_hi_t), h_rhs(mem_lo_t), z[s], N_MEM))\
                        .then_inc(unit_done, 1)
                    pe.wait_ge(xs_done, n + 3)
                    pe.wait_ge(f_done, n + 1)
                    transposes(z[2 + s], xs0[:, s], KD, xt_mm)
            for k in range(2):
                pe.wait_ge(z_free[k], 4 + 1)
            pe.wait_ge(f_done, 9)
            for c in range(2):
                for h in range(MEM_HEADS):
                    mm = nc.tensor.transpose(z[2][:, P * (4 * c + h):P * (4 * c + h + 1)],
                                             kv_t[:, MEM_HEADS + h, P * c:P * (c + 1)], ident[:])
            mm.then_inc(vmem_mm, 1)
            pe.wait_ge(flo_done, 10)
            with pe.Fori(0, 2) as i:
                for s in range(2):
                    unit_ready(pe, U_MQ + 2 * i + s)
                    pe.wait_ge(z_free[s], 4 + i + 1)
                    issue(unit_todo(s, z[s])).then_inc(unit_done, 1)

            def conv_issue(conv, share, h):
                for j, n in share:
                    if n == 0:
                        unit_ready(pe, U_CONV + 2 * h + j)
                        pe.wait_ge(z_free[j], 6 + h + 1)
                    mm = issue([conv[j][n]])
                    if n == len(conv[j]) - 1:
                        mm.then_inc(unit_done, 1)

            pe.wait_ge(vmem_set, 1)
            pe.wait_ge(f_done, 10)
            with pe.Fori(0, MEM_HEADS) as h:
                conv = [unit_todo(0, z[0]), unit_todo(1, z[1])]
                flat = [(j, n) for j in range(2) for n in range(len(conv[j]))]
                share = 8
                conv_issue(conv, flat[:2 * share], h)
                for step in range(10):
                    if step in (5, 9):
                        half = (step - 5) // 4
                        pe.wait_ge(m_pt, 8 * h + 4 * half + 4 + 1)
                        pe.wait_ge(m_olo, 2 * h + half + 1)
                        for c in range(2):
                            mm = nc.tensor.matmul(o_bank, v_cur[:, c, :], pt_mem[:, half, c, :], start=c == 0, stop=c == 1)
                        mm.then_inc(m_pv, 1)
                    if 1 <= step <= 8:
                        t = step - 1
                        pe.wait_ge(m_pn, 8 * h + t + 1)
                        pe.wait_ge(m_pt, 8 * h + t + 1)
                        for c in range(2):
                            at = P * c
                            mm = nc.tensor.transpose(t_bank[:, at:at + P], p_mem[:, t % 2, P * c:P * (c + 1)], ident[:])
                        mm.then_inc(m_t, 1)
                    if step < 8:
                        t = step
                        if t == 0:
                            pe.wait_ge(m_cur, h + 1)
                        pe.wait_ge(m_exp, 8 * h + t + 1)
                        nc.tensor.matmul(s_bank[:, t % 2, 0:N_MEM], q_cur[:, P * t:P * (t + 1)],
                                         kv_t[:, bass.ds(h, 1), :].rearrange("p a n -> p (a n)"),
                                         start=True, stop=True).then_inc(m_qk, 1)
                    conv_issue(conv, flat[share * (step + 2):share * (step + 3)], h)

            def qkv_todo():
                todo = []
                for j in range(6):
                    dst = z[(j // 2) % 2]
                    half_k = j % 2
                    part = []
                    for hh in range(2):
                        for k in range(4):
                            for what in SPLIT_PRODUCTS:
                                w = w_hi if what[0] == "h" else w_lo
                                m = h_hi if what[1] == "h" else h_lo
                                part.append((dst[:, hh * HALF:(hh + 1) * HALF], w[:, j % 2, P * k:P * (k + 1)],
                                             m[:, 4 * half_k + k, hh * HALF:(hh + 1) * HALF],
                                             half_k == 0 and k == 0 and what == "hh",
                                             half_k == 1 and k == 3 and what == "lh"))
                    todo += [(j, n, len(part), mm) for n, mm in enumerate(part)]
                return todo


            def qkv_issue(share, pair):
                for j, n, size, mm in share:
                    if n == 0:
                        unit_ready(pe, U_QKV + 6 * pair + j)
                        if j == 0:
                            pe.wait_ge(z_free[0], Z0_QKV + 2 * pair + 1)
                        if j == 2:
                            pe.wait_ge(z_free[1], Z1_QKV + pair + 1)
                        if j == 4:
                            pe.wait_ge(z_free[0], Z0_QKV + 2 * pair + 2)
                    m = issue([mm])
                    if n == size - 1:
                        m.then_inc(unit_done, 1)

            def scores(g, pair, t):
                pe.wait_ge(c_add, 8 * pair + t + 1)
                start = window(g, t)[0]
                n = P if g == 2 else 2 * P
                for hd in range(2):
                    rows = slice(ATT_E * hd, ATT_E * (hd + 1))
                    mm = nc.tensor.matmul(s_bank[:, hd, 0:n], cur[rows, 0, P * t:P * (t + 1)],
                                          cur[rows, 1, start:start + n], start=True, stop=True)
                mm.then_inc(c_qk, 1)

            def gates_todo():
                todo = []
                for q in range(2):
                    part = unit_todo(q, z[q])
                    todo += [(q, n, len(part), mm) for n, mm in enumerate(part)]
                return todo

            def gates_issue(share):
                for q, n, size, mm in share:
                    if n == 0:
                        unit_ready(pe, U_BR + q)
                        pe.wait_ge(z_free[q], Z01_BR[q] + 1)
                    m = issue([mm])
                    if n == size - 1:
                        m.then_inc(unit_done, 1)

            def dilated_pair(g, pair, vb, more):
                todo = qkv_todo() if more else gates_todo()
                share = -(-len(todo) // 11)

                def fill(n):
                    if more:
                        qkv_issue(todo[share * n:share * (n + 1)], pair + 1)
                    else:
                        gates_issue(todo[share * n:share * (n + 1)])

                tile = 8 * pair
                chunks = V_CHUNKS[g]
                fill(0)
                for step in range(10):
                    if step == 0:
                        pe.wait_ge(c_cur, 3 * pair + 2)
                        scores(g, pair, 0)
                        pe.wait_ge(c_cur, 3 * pair + 3)
                        pe.wait_ge(c_oev, tile + 1)
                        pe.wait_ge(c_pt, tile + 1)
                    for b in ((0, 1) if step == 0 else (2,) if step == 1 and V_BATCHES[g] == 3 else ()):
                        if b == 2:
                            pe.wait_ge(c_vset, vb + 1)
                        dst = t_bank if b == 1 else o_bank
                        for j, start in enumerate(chunks[4 * b:4 * b + 4]):
                            mm = nc.tensor.transpose(dst[:, P * j:P * (j + 1)], cur[:, 2, start:start + P], ident[:])
                        mm.then_inc(c_vt, 1)
                    if step >= 2:
                        t = step - 2
                        if t == 0:
                            pe.wait_ge(c_vset, vb + V_BATCHES[g])
                        pe.wait_ge(c_pt, tile + t + 2)
                        pe.wait_ge(c_oev, tile + t + 1)
                        start = window(g, t)[0]
                        keys = 1 if g == 2 else 2
                        for hd in range(2):
                            for c in range(keys):
                                mm = nc.tensor.matmul(o_bank[:, ATT_E * hd:ATT_E * (hd + 1)], p_t[:, t % 2, 2 * hd + c, :],
                                                      v_tok[:, chunks.index(start + P * c), ATT_E * hd:ATT_E * (hd + 1)],
                                                      start=c == 0, stop=c == keys - 1)
                        mm.then_inc(c_pv, 1)
                    if 1 <= step <= 8:
                        t = step - 1
                        if t == 0:
                            pe.wait_ge(c_vset, vb + 2)
                        pe.wait_ge(c_exp, tile + t + 3)
                        pe.wait_ge(c_pt, tile + t + 1)
                        for hd in range(2):
                            for c in range(1 if g == 2 else 2):
                                mm = nc.tensor.transpose(t_bank[:, P * (2 * hd + c):P * (2 * hd + c + 1)],
                                                         prob[:, t % 2, hd, P * c:P * (c + 1)], ident[:])
                        mm.then_inc(c_t, 1)
                    if 1 <= step < 8:
                        scores(g, pair, step)
                    fill(step + 1)

            qkv_issue(qkv_todo(), 0)
            pe.wait_ge(m_exp, 8 * MEM_HEADS + 2)
            pe.wait_ge(m_pt, 8 * MEM_HEADS + 1)
            pe.wait_ge(m_olo, 2 * MEM_HEADS + 1)
            for g in range(2):
                with pe.Fori(0, 2) as i:
                    dilated_pair(g, 2 * g + i, v_batches_before(2 * g) + V_BATCHES[g] * i, True)
            dilated_pair(2, 4, v_batches_before(4), True)
            dilated_pair(2, 5, v_batches_before(5), False)
            pe.wait_ge(c_add, 8 * 6 + 1)
            pe.wait_ge(c_oev, 8 * 6 + 1)


            def gates(b, i, j, z01):
                for q in range(2):
                    unit_ready(pe, U_BR + 12 * b + 6 * i + 3 * j + q)
                    pe.wait_ge(z_free[q], z01[q] + 2 * i + j + 1)
                    issue(unit_todo((3 * j + q) % 2, z[q])).then_inc(unit_done, 1)

            def projection(b, i, j, k_tiles, rhs_hi, rhs_lo, z23):
                unit_ready(pe, U_BR + 12 * b + 6 * i + 3 * j + 2)
                for q in range(2):
                    pe.wait_ge(z_free[2 + q], z23 + 2 * i + j + 1)
                    issue(products((3 * j + 2) % 2, k_tiles, lambda k: 256 * k, P * q,
                                   rhs_hi, rhs_lo, z[2 + q], T)).then_inc((proj_half, unit_done)[q], 1)

            for n in range(4):
                if n:
                    gates(0, n // 2, n % 2, Z01_BR)
                projection(0, n // 2, n % 2, 4, h_rhs(m_hi), h_rhs(m_lo), 0)
            pe.wait_ge(a_tok_set, 1)
            for c in range(2):
                pe.wait_ge(z_free[c], Z01_BR[c] + 4 + 1)
                for t in range(NT):
                    mm = nc.tensor.transpose(z[c][:, P * t:P * (t + 1)], a_tok[:, t, P * c:P * (c + 1)], ident[:])
                mm.then_inc(at_mm, 1)
            for n in range(4):
                gates(1, n // 2, n % 2, Z01_B1)
                if n == 1:
                    pe.wait_ge(z_free[3], 4 + 1 + 1)
                    for c in range(CT):
                        pe.wait_ge(ln_sq, c + 1)
                        for hh in range(2):
                            mm = nc.tensor.matmul(z[3][:, HALF * hh:HALF * (hh + 1)], ones[:],
                                                  ln_sq4[:, c, HALF * hh:HALF * (hh + 1)], start=c == 0, stop=c == CT - 1)
                    mm.then_inc(ln_var, 1)
                projection(1, n // 2, n % 2, 2, h_rhs(a_hi), h_rhs(a_lo), 5 if n else 4)
                if n == 0:
                    pe.wait_ge(tap_done, (TAPS + 1) * CT + 1)
                    pe.wait_ge(z_free[2], 4 + 1 + 1)
                    for hh in range(2):
                        for c in range(CT):
                            mm = nc.tensor.matmul(z[2][:, HALF * hh:HALF * (hh + 1)], ones[:],
                                                  u[:, c, PAD + HALF * hh:PAD + HALF * (hh + 1)],
                                                  start=c == 0, stop=c == CT - 1)
                    mm.then_inc(ln_mean, 1)
            with pe.Fori(0, 2) as i:
                for j in range(2):
                    gates(2, i, j, Z01_B2)
                    pe.wait_ge(ln_lo, CT)
                    projection(2, i, j, 4, h_rhs(c_hi), h_rhs(c_lo), Z23_B2)

            def out_unit(s, i, first=False):
                unit_ready(pe, U_OUT + 2 * i + s)
                pe.wait_ge(z_free[s], Z01_OUT[s] + i + 1)
                todo = products(s, KD, lambda k: P * k, 0, h_rhs(merged_hi), h_rhs(merged_lo), z[s], T)
                for n in range(0, len(todo), 3):
                    if first and n < 3 * KD:
                        pe.wait_ge(br_lo, n // 3 + 1)
                    mm = issue(todo[n:n + 3])
                mm.then_inc(unit_done, 1)

            out_unit(0, 0, first=True)
            out_unit(1, 0)
            with pe.Fori(1, 4) as i:
                for s in range(2):
                    out_unit(s, i)
            for k in range(2):
                pe.wait_ge(z_free[k], Z01_N[k] + 1)

            def y_tile(t, slot, wait, done):
                pe.wait_ge(z_free[2 + slot], wait)
                for k in range(KD):
                    mm = nc.tensor.transpose(z[2 + slot][:, P * k:P * (k + 1)], y_t[:, k, P * t:P * (t + 1)], ident[:])
                mm.then_inc(done, 1)

            y_tile(0, 0, Z23_N + 1, n_yt)
            for t in range(NT):
                if t + 1 < NT:
                    y_tile(t + 1, (t + 1) % 2, Z23_N + (t + 1) // 2 + 1, n_yt)
                pe.wait_ge(n_xs, t + 1)
                pe.wait_ge(z_free[t % 2], Z01_N[t % 2] + t // 2 + 1)
                transposes(z[t % 2], sg[:, t % 2], KD, n_xt)

            pe.wait_ge(n_lo, NT)

            def hidden(r, slot0, z01):
                for s in range(2):
                    slot = (slot0 + s) % 2
                    unit_ready(pe, r + s)
                    pe.wait_ge(z_free[s], z01[s] + 1)
                    issue(unit_todo(slot, z[s])).then_inc(unit_done, 1)

            def ffn_out(r, slot, act_slot, z23):
                unit_ready(pe, r)
                for q in range(4):
                    pe.wait_ge(z_free[2 + q % 2], z23 + q // 2 + 1)
                    mm = issue(products(slot, 2, lambda k: HALF * k, P * q,
                                        lambda k, at, n: act_hi[:, act_slot, k, at:at + n],
                                        lambda k, at, n: act_lo[:, act_slot, k, at:at + n], z[2 + q % 2], T))
                    if q < 3:
                        mm.then_inc(ff_y, 1)
                mm.then_inc(unit_done, 1)

            def chunk(c, act_slot):
                for j in range(2):
                    r = U_FFN - 2 + 6 * c + 3 * j
                    hidden(r, (3 * j) % 2, (Z01_F[0] + 2 * c + j, Z01_F[1] + 2 * c + j))
                    if j == 0:
                        pe.wait_ge(ff_lo, 2 * c)
                    ffn_out(r + 2, (3 * j + 2) % 2, act_slot, Z23_F + 4 * (c - 1) + 2 * j)

            for j in range(2):
                hidden(U_FFN + 2 * j, 0, (Z01_F[0] + j, Z01_F[1] + j))
            with pe.Fori(0, (CHUNKS - 1) // 2) as i:
                for s in range(2):
                    chunk(2 * i + 1 + s, s)
            pe.wait_ge(ff_lo, 2 * CHUNKS)
            for half in range(2):
                ffn_out(N_UNITS - 2 + half, half, (CHUNKS - 1) % 2, Z23_F + 4 * (CHUNKS - 1) + 2 * half)
            for k in (0, 1):
                pe.wait_ge(z_free[2 + k], Z23_T + 1)
            for t in range(NT):
                y_tile(t, t % 2, Z23_T + t // 2 + 1, t_yt)

        @block.scalar
        def _(act):
            for s, credit in ((m_exp, 2), (m_pt, 1), (c_exp, 2), (c_pt, 1), (heads_sent[0], 16),
                              (heads_sent[1], 16), (z_free[0], 1)):
                act.sem_inc(s, credit)
            a = nc.scalar.activation
            act.wait_ge(rel_ones, 1)
            act.dma_start(rel[0:32, :], rel_bias).then_inc(rel_in, 16)
            for t in range(0, NT, 2):
                act.dma_start(x_tok[:, t:t + 2, :], x[0, P * t:P * (t + 2), :].rearrange("(t p) d -> p t d", p=P))\
                    .then_inc(x_in[t // 2], 16)
            act.wait_ge(consts_set, 4)

            def token_stats(j):
                act.wait_ge(mem_in[j] if j < 2 else x_in[(j - 2) // 2], 16)
                src = mem_tok[:, j, :] if j < 2 else x_tok[:, j - 2, :]
                if j:
                    act.wait_ge(sq_done, j)
                a(junk0[:], src, ACT.Square, accum_out=sumsq[:, j:j + 1]).then_inc(sq_done, 1)
                act.wait_ge(sq_done, j + 1)
                a(std[:, j:j + 1], sumsq[:, j:j + 1], ACT.Sqrt, bias=eps_rms[:, 0:1], scale=1.0 / D)\
                    .then_inc(std_done, 1)

            def token_hi(j):
                act.wait_ge(f_done, j + 1)
                dst = mem_hi_t[:, :, P * j:P * (j + 1)] if j < 2 else h_hi[:, :, P * (j - 2):P * (j - 1)]
                a(dst, f0[j % 2][:].rearrange("p (k n) -> p k n", k=KD), ACT.Copy).then_inc(fhi_done, 1)

            token_stats(0)
            token_stats(1)
            act.wait_ge(vec_mm, 1)
            a(vcols[:], z[0][:, 0:N_VEC], ACT.Copy).then_inc(vec_set, 1)
            a(taps[:].rearrange("p j c -> p (j c)"), z[0][:, P:P + TAPS * CT], ACT.Copy).then_inc(vec_set, 1)
            token_hi(0)
            token_hi(1)
            act.wait_ge(rel_mm, 1)
            a(e_rows[:, 0:2, :].rearrange("h g n -> h (g n)"), z[1][0:SLOTS_H, :], ACT.Copy).then_inc(rel_rows, 2)
            a(e_rows[:, 2, :], z[0][0:SLOTS_H, HALF:2 * HALF], ACT.Copy).then_inc(rel_rows, 1)
            act.wait_ge(rel_rows, 3)
            for g in range(3):
                src = e_rows[:, g, :].unsqueeze(1).to_broadcast([SLOTS_H, P, REL])
                act.dma_start(rel_scratch.ap()[SLOTS_H * g:SLOTS_H * (g + 1), :, :], src).then_inc(rel_out, 16)
            token_stats(2)
            for n in range(8):
                act.wait_ge(unit_done, U_KV + n + 1 + CREDIT)
                a(kv_t[:, n, :], z[n % 2][:, 0:N_MEM], ACT.Copy).then_inc(z_free[n % 2], 1)
                if n + 3 < 10:
                    token_stats(n + 3)
                token_hi(n + 2)
            act.wait_ge(vmem_mm, 1)
            act.wait_ge(flo_done, 10)
            a(v_mem[:].rearrange("p c h n -> p (c h n)"), z[2][:], ACT.Copy).then_inc(vmem_set, 1)
            for h in range(MEM_HEADS):
                act.wait_ge(unit_done, U_MQ + h + 1 + CREDIT)
                a(q_mem[:, h, :], z[h % 2][:], ACT.Copy, scale=P ** -0.5).then_inc(z_free[h % 2], 1)

            act.wait_ge(rel_out, 48)
            with act.Fori(0, MEM_HEADS) as h:
                for step in range(10):
                    if step < 8:
                        t = step
                        act.wait_ge(m_max, 8 * h + t + 1)
                        act.wait_ge(m_t, 8 * h + t + 1)
                        a(p_mem[:, t % 2, :], s_bank[:, t % 2, 0:N_MEM], ACT.Exp, bias=mstat[:, t % 2, 0:1],
                          accum_out=mstat[:, t % 2, 1:2]).then_inc(m_exp, 1)
                    if 1 <= step <= 8:
                        t = step - 1
                        act.wait_ge(m_t, 8 * h + t + 3)
                        act.wait_ge(m_pv, 2 * h + t // 4 + 1)
                        a(pt_mem[:, t // 4, :, P * (t % 4):P * (t % 4 + 1)],
                          t_bank[:, 0:256].rearrange("p (c n) -> p c n", c=2), ACT.Copy)\
                            .then_inc(m_pt, 1)
                    if step == 6:
                        act.wait_ge(unit_done, U_CONV + 2 * h + 1 + CREDIT)
                        act.wait_ge(z_free[1], 6 + h + 1)
                        a(sg_conv[:], z[0][:], ACT.Sigmoid).then_inc(z_free[0], 1)

            def next_evac(j, pair, first=False):
                act.wait_ge(unit_done, U_QKV + 6 * pair + 2 * j + 2 + CREDIT)
                if not first:
                    act.wait_ge(c_cur, 3 * pair)
                a(nxt[:, j, :], z[j % 2][:], ACT.Copy, scale=ATT_E ** -0.5 if j == 0 else 1.0)\
                    .then_inc(z_free[j % 2], 1)

            def dilated_pair(g, pair, vb, more):
                tile = 8 * pair
                n = P if g == 2 else 2 * P
                for step in range(10):
                    for b in ((0, 1) if step == 0 else (2,) if step == 1 and V_BATCHES[g] == 3 else ()):
                        act.wait_ge(c_vt, vb + b + 1)
                        m = len(V_CHUNKS[g][4 * b:4 * b + 4])
                        a(v_tok[:, 4 * b:4 * b + m, :].rearrange("p j n -> p (j n)"),
                          (t_bank if b == 1 else o_bank)[:, 0:P * m], ACT.Copy).then_inc(c_vset, 1)
                    if step < 8:
                        t = step
                        act.wait_ge(c_max, tile + t + 1)
                        act.wait_ge(c_t, tile + t + 1)
                        for hd in range(2):
                            i = a(prob[:, t % 2, hd, 0:n], sbias[:, t % 2, hd, 0:n], ACT.Exp,
                                  bias=heads_out[:, t, hd, ATT_E + 1:ATT_E + 2],
                                  accum_out=heads_out[:, t, hd, ATT_E:ATT_E + 1])
                        i.then_inc(c_exp, 1)
                    if 1 <= step <= 8:
                        t = step - 1
                        act.wait_ge(c_t, tile + t + 3)
                        act.wait_ge(c_pv, tile + t + 1)
                        if g == 2:
                            a(p_t[:, t % 2, 0:4:2, :], t_bank.rearrange("p (b n) -> p b n", b=4)[:, 0:4:2, :],
                              ACT.Copy).then_inc(c_pt, 1)
                        else:
                            a(p_t[:, t % 2, :, :].rearrange("p b n -> p (b n)"), t_bank, ACT.Copy).then_inc(c_pt, 1)
                    if more and step in (3, 6):
                        next_evac((step - 3) // 3, pair + 1)
                    if not more and step == 6:
                        gate(0, 0, 0)
                    if step in (6, 9):
                        half = (step - 6) // 3
                        act.wait_ge(c_oev, tile + 4 * half + 4 + 1)
                        send(g, pair, half)
                if more:
                    next_evac(2, pair + 1)
                else:
                    gate(0, 1, 1)

            def gate(b, q, d):
                r = U_BR + 12 * b + 6 * (d // 4) + 3 * (d % 4 // 2) + d % 2
                act.wait_ge(unit_done, r + 1 + CREDIT)
                act.wait_ge(z_free[2 + q], 4 * b + d // 2 + 1 + (b == 2 or b == 1 and d >= 4))
                col = V_GATE + KD * (2, 1, 0)[b] + d
                a(sg[:, q, :], z[q][:], ACT.Sigmoid, bias=vcols[:, col:col + 1]).then_inc(z_free[q], 1)

            def send(g, pair, half):
                col = 2 * ROW * (pair - 2 * g)
                rows = att_scratch[g, :, bass.ds(col, 2 * ROW)]
                ts = slice(4 * half, 4 * half + 4)
                src = heads_out[:, ts].rearrange("p t h n -> p t (h n)")
                if g == 0:
                    act.dma_start(rows.rearrange("(t p) n -> p t n", p=P)[:, ts], src).then_inc(heads_sent[half], 16)
                elif g == 1:
                    for r in range(2):
                        act.dma_start(rows.rearrange("(c p r) n -> r p c n", p=P, c=2)[2 * half + r],
                                      src[:, 2 * r:2 * r + 2]).then_inc(heads_sent[half], 16)
                else:
                    for b in range(2):
                        act.dma_start(rows.rearrange("(l t a) n -> a l t n", t=8, a=2)[b, :, ts],
                                      src[64 * b:64 * (b + 1)]).then_inc(heads_sent[half], 16)

            act.wait_ge(z_free[1], 6 + MEM_HEADS + 1)
            for j in range(3):
                next_evac(j, 0, first=True)
            for g in range(2):
                with act.Fori(0, 2) as i:
                    dilated_pair(g, 2 * g + i, v_batches_before(2 * g) + V_BATCHES[g] * i, True)
            dilated_pair(2, 4, v_batches_before(4), True)
            dilated_pair(2, 5, v_batches_before(5), False)
            for half in range(2):
                act.wait_ge(heads_sent[half], 16 * (1 + 2 + 4 + 4))
            for g in range(3):
                act.dma_start(parts[:, g].rearrange("p (t h) n -> p t (h n)", t=NT),
                              att_scratch[g].rearrange("(t p) n -> p t n", p=P)).then_inc(parts_in, 16)
            act.wait_ge(cmb_step, 5)
            a(cmb[:, 4:7, :], cmb[:, 1:4, :], ACT.Exp).then_inc(cmb_exp, 1)

            for d in range(2, KD):
                gate(0, d % 2, d)
                if d == 3:
                    act.wait_ge(a_tok_set, 1)
                    for c in range(2):
                        act.wait_ge(z_free[2 + c], 1 + 1)
                        a(acc[:, c, :], tmp[:, c, :], ACT.Copy).then_inc(acc_kept, 1)
            for c in range(2):
                act.wait_ge(at_mm, 2)
                a(a_hi[:, c, :], z[c][:], ACT.Copy).then_inc(ahi_set, 1)
            for d in range(KD):
                gate(1, d % 2, d)
                if d == 1:
                    for c in range(CT):
                        act.wait_ge(ln_xc, c + 1)
                        a(ln_sq4[:, c, :], u[:, c, PAD:PAD + T], ACT.Square).then_inc(ln_sq, 1)
                if d == 3:
                    act.wait_ge(ln_var, 1)
                    a(ln_dev[:, 0, :], z[3][:], ACT.Sqrt, bias=eps_ln[:, 0:1]).then_inc(z_free[3], 1)
                    for c in range(CT):
                        act.wait_ge(ln_xn, c + 1)
                        a(ln_sq4[:, c, :], u[:, c, PAD:PAD + T], ACT.Silu, bias=vcols[:, V_LNB + c:V_LNB + c + 1],
                          scale=vcols[:, V_LNG + c:V_LNG + c + 1]).then_inc(ln_f, 1)
            act.wait_ge(unit_done, U_BR + 24 + CREDIT)
            act.wait_ge(ln_f, CT)
            for c in range(CT):
                a(c_hi[:, c, :], ln_sq4[:, c, :], ACT.Copy).then_inc(ln_hi, 1)

            def merged_part(d):
                act.wait_ge(br_f, d + 1)
                a(merged_hi[:, d, :], tmp[:, d % 2, :], ACT.Copy).then_inc(br_hi, 1)

            for d in range(0, KD, 2):
                gate(2, 0, d)
                gate(2, 1, d + 1)
                if d == 0:
                    act.wait_ge(ln_lo, CT)
                merged_part(d)
                merged_part(d + 1)
            for d in range(KD):
                act.wait_ge(unit_done, U_OUT + d + 1 + CREDIT)
                a(y_t[:, d, :], z[d % 2][:], ACT.Copy).then_inc(z_free[d % 2], 1)
            def norm_first(t):
                act.wait_ge(n_yt, t + 1)
                if t >= 2:
                    act.wait_ge(n_xt, t - 1)
                a(sg[:, t % 2, :], z[2 + t % 2][:], ACT.Square, accum_out=sumsq[:, 10 + t:11 + t]).then_inc(n_sq, 1)
                act.wait_ge(n_sq, 2 * t + 1)
                a(std[:, 10 + t:11 + t], sumsq[:, 10 + t:11 + t], ACT.Sqrt, bias=eps_rms[:, 0:1], scale=1.0 / D)\
                    .then_inc(n_std, 1)

            def norm_second(t):
                act.wait_ge(n_x1, t + 1)
                a(sg[:, t % 2, :], x1[:, t, :], ACT.Square, accum_out=sumsq[:, 20 + t:21 + t]).then_inc(n_sq, 1)
                act.wait_ge(n_sq, 2 * t + 2)
                a(std[:, 20 + t:21 + t], sumsq[:, 20 + t:21 + t], ACT.Sqrt, bias=eps_rms[:, 0:1], scale=1.0 / D)\
                    .then_inc(n_std, 1)

            def norm_hi(t):
                act.wait_ge(z_free[t % 2], Z01_N[t % 2] + t // 2 + 2)
                a(h_hi[:, :, P * t:P * (t + 1)], tmp[:, t % 2, :].rearrange("p (k n) -> p k n", k=KD), ACT.Copy)\
                    .then_inc(n_hi, 1)

            for t in range(NT):
                norm_first(t)
                norm_second(t)
                if t:
                    norm_hi(t - 1)
            norm_hi(NT - 1)

            def hidden(r, j, act_slot, n):
                act.wait_ge(unit_done, r + 1 + CREDIT)
                act.wait_ge(z_free[1], Z01_F[1] + n)
                a(sg[:, j, :], z[0][:], ACT.Silu).then_inc(z_free[0], 1)
                act.wait_ge(z_free[1], Z01_F[1] + n + 2)
                a(act_hi[:, act_slot, j, :], tmp[:, j, :], ACT.Copy).then_inc(ff_hi, 1)

            act.wait_ge(n_lo, NT)
            for j in range(2):
                hidden(U_FFN + 2 * j, j, 0, j)
            with act.Fori(0, (CHUNKS - 1) // 2) as i:
                for s in range(2):
                    c = 2 * i + 1 + s
                    for j in range(2):
                        if j == 0:
                            act.wait_ge(unit_done, U_FFN - 2 + 6 * c + CREDIT)
                        hidden(U_FFN - 2 + 6 * c + 3 * j, j, (s + 1) % 2, 2 * c + j)
            for t in range(NT):
                act.wait_ge(t_yt, t + 1)
                a(sg[:, t % 2, :], z[2 + t % 2][:], ACT.Square, accum_out=sumsq[:, 30 + t:31 + t]).then_inc(t_sq, 1)
                act.wait_ge(t_sq, t + 1)
                a(std[:, 30 + t:31 + t], sumsq[:, 30 + t:31 + t], ACT.Sqrt, bias=eps_rms[:, 0:1], scale=1.0 / D)\
                    .then_inc(t_std, 1)

        @block.vector
        def _(dve):
            for s, credit in ((m_olo, 1), (c_add, 1), (c_oev, 1), (tap_done, 1), (z_free[1], 1), (z_free[2], 1), (z_free[3], 1)):
                dve.sem_inc(s, credit)
            v = nc.vector

            def scaled(dst, src, scalar):
                return v.tensor_scalar(dst, src, scalar, None, ALU.mult)

            def tokens_scaled(j):
                dve.wait_ge(std_done, j + 1)
                v.reciprocal(rstd[:, j:j + 1], std[:, j:j + 1]).then_inc(rstd_done, 1)
                dve.wait_ge(rstd_done, j + 1)
                if j >= 2:
                    dve.wait_ge(xt_mm, j - 1)
                src = mem_tok[:, j, :] if j < 2 else x_tok[:, j - 2, :]
                scaled(xs0[:, j % 2, :], src, rstd[:, j:j + 1]).then_inc(xs_done, 1)

            def tokens_gain(j):
                dve.wait_ge(xt_mm, j + 1)
                if j == 0:
                    dve.wait_ge(vec_set, 2)
                if j >= 2:
                    dve.wait_ge(flo_done, j - 1)
                col = V_MEM if j < 2 else V_MIX
                gain = vcols[:, col:col + KD].unsqueeze(2).to_broadcast([P, KD, P])
                v.tensor_tensor(f0[j % 2][:].rearrange("p (k n) -> p k n", k=KD),
                                z[2 + j % 2][:].rearrange("p (k n) -> p k n", k=KD), gain, ALU.mult).then_inc(f_done, 1)

            def tokens_lo(j):
                dve.wait_ge(fhi_done, j + 1)
                hi, lo = (mem_hi_t, mem_lo_t) if j < 2 else (h_hi, h_lo)
                at = slice(P * (j % 2 if j < 2 else j - 2), P * (j % 2 if j < 2 else j - 2) + P)
                v.tensor_tensor(lo[:, :, at], f0[j % 2][:].rearrange("p (k n) -> p k n", k=KD), hi[:, :, at],
                                ALU.subtract).then_inc(flo_done, 1)

            tokens_scaled(0)
            tokens_scaled(1)
            tokens_gain(0)
            tokens_gain(1)
            tokens_lo(0)
            tokens_lo(1)
            for j in range(2, 10):
                tokens_scaled(j)
                tokens_gain(j)
                if j > 2:
                    tokens_lo(j - 1)
            tokens_lo(9)
            v.memset(u[:, :, 0:PAD], 0.0).then_inc(u_pad, 1)
            v.memset(u[:, :, PAD + T:U_W], 0.0).then_inc(u_pad, 1)

            dve.wait_ge(vmem_set, 1)
            dve.wait_ge(z_free[0], 6 + 1)
            dve.wait_ge(z_free[1], 6 + 1)
            with dve.Fori(0, MEM_HEADS) as h:
                dve.wait_ge(m_pv, 2 * h + 2)
                scaled(q_cur[:], q_mem[:, bass.ds(h, 1), :].rearrange("p a t -> p (a t)"), 1.0)
                scaled(v_cur[:], v_mem[:, :, bass.ds(h, 1), :].rearrange("p c a n -> p c (a n)"), 1.0)\
                    .then_inc(m_cur, 1)
                for step in range(10):
                    if step < 8:
                        t = step
                        dve.wait_ge(m_qk, 8 * h + t + 1)
                        v.tensor_reduce(mstat[:, t % 2, 0:1], s_bank[:, t % 2, 0:N_MEM], X, ALU.max, negate=True)\
                            .then_inc(m_max, 1)
                        dve.wait_ge(m_exp, 8 * h + t + 3)
                        v.reciprocal(mstat[:, t % 2, 2:3], mstat[:, t % 2, 1:2]).then_inc(m_rden, 1)
                        dve.wait_ge(m_rden, 8 * h + t + 1)
                        scaled(p_mem[:, t % 2, :], p_mem[:, t % 2, :], mstat[:, t % 2, 2:3]).then_inc(m_pn, 1)
                    if step in (6, 9):
                        half = (step - 6) // 3
                        dve.wait_ge(m_pv, 2 * h + half + 3)
                        at = slice(HALF * half, HALF * (half + 1))
                        hi = m_hi[:, bass.ds(h, 1), at].rearrange("p a t -> p (a t)")
                        lo = m_lo[:, bass.ds(h, 1), at].rearrange("p a t -> p (a t)")
                        scaled(hi, o_bank, 1.0).then_inc(m_ohi, 1)
                        dve.wait_ge(m_ohi, 2 * h + half + 1)
                        v.tensor_tensor(lo, o_bank, hi, ALU.subtract).then_inc(m_olo, 1)
                dve.wait_ge(unit_done, U_CONV + 2 * h + 2 + CREDIT)
                dve.wait_ge(z_free[0], 6 + h + 2)
                v.tensor_tensor(u[:, bass.ds(h, 1), PAD:PAD + T].rearrange("p a t -> p (a t)"), z[1][:], sg_conv[:],
                                ALU.mult).then_inc(z_free[1], 1)

            dve.wait_ge(tables_in, 32)
            v.memset(bias2[0:64, :, 64:P], NEG).then_inc(bias_cut, 1)
            v.memset(bias2[64:P, :, 0:64], NEG).then_inc(bias_cut, 1)
            dve.wait_ge(bias_cut, 2)

            def conv_start(c):
                dve.wait_ge(tap_done, (TAPS + 1) * c + 1)
                v.tensor_copy(conv_sum[:], vcols[:, V_DWB + c:V_DWB + c + 1].to_broadcast([P, T])).then_inc(tap_done, 1)

            def conv_taps(c, first, tap, count):
                for n in range(count):
                    dve.wait_ge(tap_done, (TAPS + 1) * c + first + n + 1)
                    last = isinstance(first, int) and first + n == TAPS
                    v.scalar_tensor_tensor(u[:, c, PAD:PAD + T] if last else conv_sum[:],
                                           u[:, c, bass.ds(tap + n, T)], taps[:, bass.ds(tap + n, 1), c],
                                           conv_sum[:], ALU.mult, ALU.add).then_inc(tap_done, 1)

            def dilated_pair(g, pair, sent_before, conv_tile, conv_op, tap, per_step, op_count):
                tile = 8 * pair
                d = DILATIONS[g]
                n = P if g == 2 else 2 * P
                head = 2 * (pair - 2 * g)
                for j in range(3):
                    dve.wait_ge(z_free[j % 2], (Z0_QKV + 2 * pair + 2, Z1_QKV + pair + 2, Z0_QKV + 2 * pair + 3)[j])
                    if d == 1:
                        dst, src = cur[:, j, :], nxt[:, j, :]
                    else:
                        dst = cur[:, j, :].rearrange("p (r l) -> p r l", r=d)
                        src = nxt[:, j, :].rearrange("p (l r) -> p r l", r=d)
                    v.tensor_copy(dst, src).then_inc(c_cur, 1)
                for step in range(10):
                    if step < 8:
                        t = step
                        dve.wait_ge(c_qk, tile + t + 1)
                        dve.wait_ge(c_exp, tile + t + 1)
                        if g == 2:
                            bias = bias2[:, bass.ds(head, 2), :]
                        else:
                            col = P - window(g, t)[1]
                            bias = bias01[:, bass.ds(SLOTS_H * g + head, 2), col:col + n]
                        v.tensor_tensor(sbias[:, t % 2, :, 0:n], s_bank[:, :, 0:n], bias, ALU.add).then_inc(c_add, 1)
                        dve.wait_ge(c_add, tile + t + 2)
                        if t % 4 == 0:
                            dve.wait_ge(heads_sent[t // 4], 16 * (1 + sent_before))
                        v.tensor_reduce(heads_out[:, t, :, ATT_E + 1:ATT_E + 2], sbias[:, t % 2, :, 0:n], X, ALU.max,
                                        negate=True).then_inc(c_max, 1)
                    if step >= 2:
                        t = step - 2
                        dve.wait_ge(c_pv, tile + t + 3)
                        v.tensor_copy(heads_out[:, t, :, 0:ATT_E], o_bank[:, 0:2 * ATT_E].rearrange(
                            "p (h e) -> p h e", h=2)).then_inc(c_oev, 1)
                    conv_taps(conv_tile, conv_op + per_step * step, tap + per_step * step,
                              max(min(per_step, op_count - per_step * step), 0))

            for g in range(2):
                conv_start(g)
                with dve.Fori(0, 2) as i:
                    dilated_pair(g, 2 * g + i, 2 * g + (1 + g) * i, g, 1 + PAD * i, (PAD + 1) * i, 2, PAD)
                conv_taps(g, TAPS, PAD, 1)
            conv_start(2)
            dilated_pair(2, 4, 6, 2, 1, 0, 2, PAD)
            dilated_pair(2, 5, 8, 2, 1 + PAD, PAD + 1, 1, 8)

            def gated(b, i, j, q, dst, z01, z23):
                if q == 0:
                    dve.wait_ge(proj_half, 4 * b + 2 * i + j + 1)
                else:
                    dve.wait_ge(unit_done, U_BR + 12 * b + 6 * i + 3 * j + 3 + CREDIT)
                dve.wait_ge(z_free[q], z01[q] + 2 * i + j + 2)
                v.tensor_tensor(dst, z[2 + q][:], sg[:, q, :], ALU.mult).then_inc(z_free[2 + q], 1)

            steps = [0]

            def combine(op, *args):
                op(*args).then_inc(cmb_step, 1)
                steps[0] += 1
                dve.wait_ge(cmb_step, steps[0])

            def col(g, c):
                return parts[:, g, :, c]

            dve.wait_ge(parts_in, 48)
            combine(v.tensor_tensor, cmb[:, 0, :], col(0, ATT_E + 1), col(1, ATT_E + 1), ALU.min)
            combine(v.tensor_tensor, cmb[:, 0, :], cmb[:, 0, :], col(2, ATT_E + 1), ALU.min)
            for g in range(3):
                combine(v.tensor_tensor, cmb[:, 1 + g, :], cmb[:, 0, :], col(g, ATT_E + 1), ALU.subtract)
            for q in range(2):
                gated(0, 0, 0, q, tmp[:, q, :], Z01_BR, 0)
            dve.wait_ge(cmb_exp, 1)
            for g in range(3):
                combine(v.tensor_tensor, cmb[:, 1 + g, :], cmb[:, 4 + g, :], col(g, ATT_E), ALU.mult)
            combine(v.tensor_tensor, cmb[:, 7, :], cmb[:, 1, :], cmb[:, 2, :], ALU.add)
            combine(v.tensor_tensor, cmb[:, 7, :], cmb[:, 7, :], cmb[:, 3, :], ALU.add)
            combine(v.reciprocal, cmb[:, 8, :], cmb[:, 7, :])
            total = a_tok[:].rearrange("p t (h e) -> p (t h) e", h=SLOTS_H)
            for g in range(3):
                combine(v.tensor_tensor, cmb[:, 1 + g, :], cmb[:, 4 + g, :], cmb[:, 8, :], ALU.mult)
                share = cmb[:, 1 + g, :].unsqueeze(2).to_broadcast([P, NT * SLOTS_H, ATT_E])
                combine(v.tensor_tensor, total if g == 0 else wsum[:], parts[:, g, :, 0:ATT_E], share, ALU.mult)
                if g == 1:
                    combine(v.tensor_tensor, total, total, wsum[:], ALU.add)
            v.tensor_tensor(total, total, wsum[:], ALU.add).then_inc(a_tok_set, 1)

            ops = [(2, n) for n in range(PAD + 9, TAPS + 1)] + [(3, n) for n in range(TAPS + 1)]
            share = -(-len(ops) // 6)
            for n in range(2, KD):
                gated(0, n // 4, n % 4 // 2, n % 2, acc[:, n, :], Z01_BR, 0)
                for c, op in ops[share * (n - 2):share * (n - 1)]:
                    if op == 0:
                        conv_start(c)
                    else:
                        conv_taps(c, op, PAD if op == TAPS else op - (op <= PAD), 1)
            for c in range(2):
                dve.wait_ge(ahi_set, c + 1)
                v.tensor_tensor(a_lo[:, c, :], z[c][:], a_hi[:, c, :], ALU.subtract).then_inc(z_free[c], 1)
            dve.wait_ge(acc_kept, 2)

            def summed(b, i, j, q, dst, z01, z23, done):
                gated(b, i, j, q, tmp[:, q, :], z01, z23)
                dve.wait_ge(z_free[2 + q], z23 + 2 * i + j + 2)
                acc_d = acc[:, bass.ds(4 * i + 2 * j + q, 1), :].rearrange("p a t -> p (a t)")
                v.tensor_tensor(acc_d if dst is None else dst, acc_d, tmp[:, q, :], ALU.add).then_inc(done, 1)

            def ln_scale(c):
                v.tensor_tensor(u[:, c, PAD:PAD + T], u[:, c, PAD:PAD + T], ln_dev[:, 1, :], ALU.mult).then_inc(ln_xn, 1)

            def ln_low(c):
                dve.wait_ge(ln_hi, c + 1)
                v.tensor_tensor(c_lo[:, c, :], ln_sq4[:, c, :], c_hi[:, c, :], ALU.subtract).then_inc(ln_lo, 1)

            for n in range(KD):
                summed(1, n // 4, n % 4 // 2, n % 2, None, Z01_B1, 5 if n >= 2 else 4, br_tmp)
                if n == 1:
                    dve.wait_ge(ln_mean, 1)
                    for c in range(CT):
                        v.tensor_tensor(u[:, c, PAD:PAD + T], u[:, c, PAD:PAD + T], z[2][:], ALU.subtract)\
                            .then_inc(ln_xc, 1)
                    dve.wait_ge(ln_xc, CT)
                    dve.sem_inc(z_free[2], 1)
                    dve.wait_ge(z_free[3], 4 + 1 + 2)
                    v.reciprocal(ln_dev[:, 1, :], ln_dev[:, 0, :]).then_inc(ln_rstd, 1)
                    dve.wait_ge(ln_rstd, 1)
                    for c in range(CT):
                        ln_scale(c)
            for c in range(CT):
                ln_low(c)
            with dve.Fori(0, 2) as i:
                for j in range(2):
                    for q in range(2):
                        n = 4 * i + 2 * j + q
                        summed(2, i, j, q, tmp[:, q, :], Z01_B2, Z23_B2, br_f)
                        dve.wait_ge(br_hi, n + 1)
                        v.tensor_tensor(merged_lo[:, bass.ds(n, 1), :].rearrange("p a t -> p (a t)"), tmp[:, q, :],
                                        merged_hi[:, bass.ds(n, 1), :].rearrange("p a t -> p (a t)"),
                                        ALU.subtract).then_inc(br_lo, 1)

            def norm_first(t):
                dve.wait_ge(n_std, 2 * t + 1)
                v.reciprocal(rstd[:, 10 + t:11 + t], std[:, 10 + t:11 + t]).then_inc(n_rstd, 1)
                dve.wait_ge(n_rstd, 2 * t + 1)
                v.scalar_tensor_tensor(x1[:, t, :], z[2 + t % 2][:], rstd[:, 10 + t:11 + t], post_gain[:], ALU.mult,
                                       ALU.mult).then_inc(z_free[2 + t % 2], 1)
                dve.wait_ge(z_free[2 + t % 2], Z23_N + t // 2 + 2)
                dve.wait_ge(x_again_t[t], 16)
                v.tensor_tensor(x1[:, t, :], x1[:, t, :], x_again[:, t, :], ALU.add).then_inc(n_x1, 1)

            def norm_second(t):
                dve.wait_ge(n_std, 2 * t + 2)
                v.reciprocal(rstd[:, 20 + t:21 + t], std[:, 20 + t:21 + t]).then_inc(n_rstd, 1)
                dve.wait_ge(n_rstd, 2 * t + 2)
                scaled(sg[:, t % 2, :], x1[:, t, :], rstd[:, 20 + t:21 + t]).then_inc(n_xs, 1)

            def norm_split(t):
                dve.wait_ge(n_xt, t + 1)
                gain = vcols[:, V_FFN:V_FFN + KD].unsqueeze(2).to_broadcast([P, KD, P])
                f = tmp[:, t % 2, :].rearrange("p (k n) -> p k n", k=KD)
                v.tensor_tensor(f, z[t % 2][:].rearrange("p (k n) -> p k n", k=KD), gain, ALU.mult)\
                    .then_inc(z_free[t % 2], 1)
                dve.wait_ge(n_hi, t + 1)
                at = slice(P * t, P * (t + 1))
                v.tensor_tensor(h_lo[:, :, at], f, h_hi[:, :, at], ALU.subtract).then_inc(n_lo, 1)

            dve.wait_ge(gain_in, 16)
            for t in range(NT):
                norm_first(t)
                norm_second(t)
                if t:
                    norm_split(t - 1)
            norm_split(NT - 1)

            def hidden(r, j, act_slot, n):
                dve.wait_ge(unit_done, r + 2 + CREDIT)
                dve.wait_ge(z_free[0], Z01_F[0] + n + 2)
                v.tensor_tensor(tmp[:, j, :], z[1][:], sg[:, j, :], ALU.mult).then_inc(z_free[1], 1)
                dve.wait_ge(ff_hi, n + 1)
                v.tensor_tensor(act_lo[:, act_slot, j, :], tmp[:, j, :], act_hi[:, act_slot, j, :], ALU.subtract)\
                    .then_inc(ff_lo, 1)

            def ffn_out(r, m, half):
                for q in range(4):
                    if q < 3:
                        dve.wait_ge(ff_y, 3 * m + q + 1)
                    else:
                        dve.wait_ge(unit_done, r + 1 + CREDIT)
                    y = y_t[:, 4 * half + q, :]
                    v.tensor_tensor(y, z[2 + q % 2][:], y, ALU.add).then_inc(z_free[2 + q % 2], 1)

            for j in range(2):
                hidden(U_FFN + 2 * j, j, 0, j)
            dve.wait_ge(y_zero, 1)
            with dve.Fori(0, (CHUNKS - 1) // 2) as i:
                for s in range(2):
                    c = 2 * i + 1 + s
                    for j in range(2):
                        r = U_FFN - 2 + 6 * c + 3 * j
                        hidden(r, j, (s + 1) % 2, 2 * c + j)
                        ffn_out(r + 2, 2 * (c - 1) + j, j)
            for half in range(2):
                ffn_out(N_UNITS - 2 + half, 2 * (CHUNKS - 1) + half, half)
            dve.wait_ge(gain_in, 32)
            for t in range(NT):
                dve.wait_ge(t_std, t + 1)
                v.reciprocal(rstd[:, 30 + t:31 + t], std[:, 30 + t:31 + t]).then_inc(t_rstd, 1)
                dve.wait_ge(t_rstd, t + 1)
                v.scalar_tensor_tensor(tmp[:, t % 2, :], z[2 + t % 2][:], rstd[:, 30 + t:31 + t], post_gain[:], ALU.mult,
                                       ALU.mult).then_inc(z_free[2 + t % 2], 1)
                dve.wait_ge(z_free[2 + t % 2], Z23_T + t // 2 + 2)
                v.tensor_tensor(x1[:, t, :], x1[:, t, :], tmp[:, t % 2, :], ALU.add).then_inc(t_out, 1)


INPUTS = ("x", "mem", "rel_bias", "norm_mix_pre", "w_in", "b_gate", "conv_dw", "conv_dw_bias", "conv_ln_g",
          "conv_ln_b", "w_conv_out", "w_att_out", "norm_mem", "w_mem_kv", "w_mem_out", "w_out", "norm_mix_post",
          "norm_ffn_pre", "w_ffn_in", "w_ffn_out", "norm_ffn_post")


def bucket_table():
    import numpy as np
    import math
    half, exact, largest = 16, 8, 1024
    table = np.zeros((3, 33, REL), np.float32)
    for g, dilation in enumerate(DILATIONS):
        for col in range(REL):
            off = col - REL // 2
            if abs(off) > RADIUS:
                table[g, 32, col] = NEG
                continue
            n = abs(off * dilation)
            bucket = n
            if n >= exact:
                bucket = min(exact + int(math.log(n / exact) / math.log(largest / exact) * (half - exact)), half - 1)
            table[g, bucket + (half if off > 0 else 0), col] = 1.0
    return table


def kernel(**inputs):
    import numpy as np
    import concourse.bacc as bacc
    from concourse.bass_utils import run_bass_kernel_spmd

    nc = bacc.Bacc("TRN2", target_bir_lowering=False, num_devices=1)
    arrays = {name: np.ascontiguousarray(inputs[name]) for name in INPUTS}
    arrays["identity"] = np.eye(P, dtype=np.float32)
    arrays["bucket_hot"] = bucket_table()
    args = [nc.dram_tensor(f"in_{name}", a.shape, mybir.dt.from_np(a.dtype), kind="ExternalInput").ap()
            for name, a in arrays.items()]
    result = nc.dram_tensor("result", (1, T, D), mybir.dt.float32, kind="ExternalOutput").ap()
    hybrid_layer(nc, *args, result)
    ran = run_bass_kernel_spmd(nc, [{f"in_{name}": a for name, a in arrays.items()}], core_ids=[0])
    return ran.results[0]["result"]
```

```python
import concourse.bass as bass
from concourse import mybir
from contextlib import ExitStack

P = 128
D = 1024
T = 1024
NT = T // P
KD = D // P
HALF = 512
N_MEM = 256
MEM_HEADS = 4
CONV_W = 512
CT = CONV_W // P
TAPS = 31
PAD = TAPS // 2
ATT_W = 768
ATT_E = 64
SLOTS_H = 4
HIDDEN = 2816
CHUNKS = HIDDEN // 256
DILATIONS = (1, 4, 16)
RADIUS = 64
REL = 512
NEG = -1e30
C_ATT = 2 * CONV_W
C_MEM = C_ATT + 3 * ATT_W
C_GATE = C_MEM + MEM_HEADS * P
ROW = ATT_E + 2

V_MIX, V_MEM, V_FFN, V_GATE, V_DWB, V_LNG, V_LNB = 0, 8, 16, 24, 48, 52, 56
N_VEC = 60

U_KV, U_MQ, U_CONV, U_QKV, U_BR, U_OUT, U_FFN = 0, 8, 12, 20, 56, 92, 100
N_UNITS = U_FFN + 6 * CHUNKS
CREDIT = 2
S_POST, S_PRE, S_TAIL = 10, 20, 30
S_SPARE = (18, 19, 28, 29, 38)


def window(g, t):
    if g == 0:
        start = min(max(P * t - RADIUS, 0), T - 2 * P)
        return start, P * t - start
    if g == 1:
        return 2 * P * (t // 2), P * (t % 2)
    return P * t, 0


V_CHUNKS = ([0, P] + [RADIUS + P * k for k in range(7)] + [T - 2 * P, T - P],
            [P * k for k in range(NT)], [P * k for k in range(NT)])
V_BATCHES = (3, 2, 2)


def stat(n):
    return slice(n, n + 1)


def v_batches_before(pair):
    return sum(2 * V_BATCHES[g] for g in range(pair // 2)) + (pair % 2) * V_BATCHES[pair // 2]


def hybrid_layer(nc, x, mem, rel_bias, norm_mix_pre, w_in, b_gate, conv_dw, conv_dw_bias, conv_ln_g,
                 conv_ln_b, w_conv_out, w_att_out, norm_mem, w_mem_kv, w_mem_out, w_out,
                 norm_mix_post, norm_ffn_pre, w_ffn_in, w_ffn_out, norm_ffn_post,
                 identity, bucket_hot, out):
    f32 = mybir.dt.float32
    f32r = mybir.dt.float32r
    u8 = mybir.dt.uint8
    ALU = mybir.AluOpType
    ACT = mybir.ActivationFunctionType
    X = mybir.AxisListType.X
    ctx = ExitStack()

    BASE = 16512

    def sb(name, shape, offset, dt=f32):
        return nc.alloc_sbuf_tensor_at(name, shape, dt, offset=BASE + offset)

    KB = 1024
    h_hi = sb("h_hi", [P, KD, T], 0, f32r)
    h_lo = sb("h_lo", [P, KD, T], 32 * KB, f32r)
    raw = sb("raw", [P, 2, 1024], 64 * KB)
    w_hi = sb("w_hi", [P, 2, 1024], 72 * KB, f32r)
    w_lo = sb("w_lo", [P, 2, 1024], 80 * KB, f32r)
    o = 88 * KB
    ident = sb("ident", [P, P], o)
    ones = sb("ones", [P, P], o + 512)
    zeros = sb("zeros", [P, P], o + 1024)
    vcols = sb("vcols", [P, N_VEC], o + 1536)
    taps = sb("taps", [P, TAPS, CT], o + 2048)
    sumsq = sb("sumsq", [P, 40], o + 2560)
    std = sb("std", [P, 40], o + 2720)
    rstd = sb("rstd", [P, 40], o + 2880)
    eps_rms = sb("eps_rms", [P, 8], o + 3040)
    eps_ln = sb("eps_ln", [P, 8], o + 3072)
    post_gain = sb("post_gain", [P, D], o + 3104)
    conv_sum = sb("conv_sum", [P, T], o + 3104)
    R = o + 3104 + 4096
    U_W = T + 2 * PAD
    u = sb("u", [P, CT, U_W], R)
    ATT = R + CT * U_W * 4
    MEM = ATT + 16 * KB
    ACC = MEM + 32 * KB
    SG = ACC + 32 * KB
    TMP = SG + 8 * KB
    x_tok = sb("x_tok", [P, NT, D], R)
    mem_hi_t = sb("mem_hi_t", [P, KD, N_MEM], MEM, f32r)
    mem_lo_t = sb("mem_lo_t", [P, KD, N_MEM], MEM + 8 * KB, f32r)
    mem_tok = sb("mem_tok", [P, 2, D], MEM + 16 * KB)
    xs0 = sb("xs0", [P, 2, D], MEM + 24 * KB)
    f0 = [sb("f0a", [P, D], o + 3104), sb("f0b", [P, D], ACC + 8 * KB)]
    bhot = sb("bhot", [33, 3, REL], ACC + 12 * KB)
    rel = sb("rel", [33, 12], ACC + 18 * KB)
    e_rows = sb("e_rows", [SLOTS_H, 3, REL], ACC + 20 * KB)
    junk0 = sb("junk0", [P, D], ACC + 28 * KB)
    vec_rows = sb("vec_rows", [N_VEC, P], ACC + 26 * KB)
    tap_rows = sb("tap_rows", [TAPS * CT, P], ACC + 26 * KB + 512)
    q_mem = sb("q_mem", [P, MEM_HEADS, T], ATT)
    kv_t = sb("kv_t", [P, 2 * MEM_HEADS, N_MEM], ACC)
    v_mem = sb("v_mem", [P, 2, MEM_HEADS, P], ACC + 8 * KB)
    q_cur = sb("q_cur", [P, T], ACC + 12 * KB)
    v_cur = sb("v_cur", [P, 2, P], ACC + 17 * KB)
    p_mem = sb("p_mem", [P, 2, N_MEM], ACC + 18 * KB)
    pt_mem = sb("pt_mem", [P, 2, 2, HALF], ACC + 20 * KB)
    sg_conv = sb("sg_conv", [P, T], ACC + 28 * KB)
    mstat = sb("mstat", [P, 2, 4], ACC + 46 * KB)
    m_hi = sb("m_hi", [P, MEM_HEADS, T], MEM, f32r)
    m_lo = sb("m_lo", [P, MEM_HEADS, T], MEM + 16 * KB, f32r)
    nxt = sb("nxt", [P, 3, T], ATT)
    prob = sb("prob", [P, 2, 2, 256], ATT + 12 * KB)
    cur = sb("cur", [P, 3, T], ACC)
    v_tok = sb("v_tok", [P, 12, P], ACC + 12 * KB)
    sbias = sb("sbias", [P, 2, 2, 256], ACC + 18 * KB)
    p_t = sb("p_t", [P, 2, 4, P], ACC + 22 * KB)
    heads_out = sb("heads_out", [P, NT, 2, ROW], ACC + 26 * KB)
    bias01 = sb("bias01", [P, 2 * SLOTS_H, 384], ACC + 32 * KB)
    bias2 = sb("bias2", [P, SLOTS_H, P], ACC + 44 * KB)
    parts = sb("parts", [P, 3, NT * SLOTS_H, ROW], ACC)
    a_tok = sb("a_tok", [P, NT, SLOTS_H * ATT_E], ATT)
    cmb = sb("cmb", [P, 10, NT * SLOTS_H], ACC + 26 * KB)
    wsum = sb("wsum", [P, NT * SLOTS_H, ATT_E], ATT + 8 * KB)
    a_hi = sb("a_hi", [P, 2, T], ATT, f32r)
    a_lo = sb("a_lo", [P, 2, T], ATT + 8 * KB, f32r)
    acc = sb("acc", [P, KD, T], ACC)
    sg = sb("sg", [P, 2, T], SG)
    tmp = sb("tmp", [P, 2, T], TMP)
    ln_sq4 = sb("ln_sq4", [P, CT, T], MEM)
    ln_dev = sb("ln_dev", [P, 2, T], MEM + 16 * KB)
    ln_sum = sb("ln_sum", [P, 2, T], MEM + 24 * KB)
    c_hi = sb("c_hi", [P, CT, T], ATT, f32r)
    c_lo = sb("c_lo", [P, CT, T], R, f32r)
    merged_hi = sb("merged_hi", [P, KD, T], MEM, f32r)
    merged_lo = sb("merged_lo", [P, KD, T], ACC, f32r)
    y_t = sb("y_t", [P, KD, T], R)
    y_sum = sb("y_sum", [P, KD, T], MEM)
    f_ffn = sb("f_ffn", [P, 2, D], ACC)
    x_rest = sb("x_rest", [P, NT - 2, D], ACC + 8 * KB)
    act_hi = sb("act_hi", [P, 2, 2, T], ACC, f32r)
    act_lo = sb("act_lo", [P, 2, 2, T], ACC + 16 * KB, f32r)

    rel_scratch = nc.dram_tensor("rel_scratch", (3 * SLOTS_H, P, REL), f32)
    att_scratch = nc.dram_tensor("att_scratch", (3, T, SLOTS_H * ROW), f32).ap()

    with ctx:
        z = [ctx.enter_context(nc.psum_tensor(f"z{k}", [P, 1024], f32)) for k in range(4)]
        s_bank = z[2][:].rearrange("p (b n) -> p b n", b=2)
        t_bank = z[3][:, 0:512]
        o_bank = z[3][:, 512:1024]

        def sem(name):
            return ctx.enter_context(nc.semaphore(name))

        raw_ready = [sem("raw_ready0"), sem("raw_ready1")]
        hi_done = sem("hi_done")
        split_done = sem("split_done")
        unit_done = sem("unit_done")
        z_free = [sem(f"z{k}_free") for k in range(4)]
        consts_in, ident_in, rel_in, tables_in = (sem(n) for n in ("consts_in", "ident_in", "rel_in", "tables_in"))
        mem_in = [sem("mem_in0"), sem("mem_in1")]
        x_in = [sem(f"x_in{t}") for t in range(NT // 2)]
        rel_ones, rel_mm, rel_rows, rel_out = (sem(n) for n in ("rel_ones", "rel_mm", "rel_rows", "rel_out"))
        consts_set, vec_mm, vec_set = (sem(n) for n in ("consts_set", "vec_mm", "vec_set"))
        sq_done, std_done, rstd_done, xs_done = (sem(n) for n in ("sq_done", "std_done", "rstd_done", "xs_done"))
        xt_mm, f_done, fhi_done, flo_done = (sem(n) for n in ("xt_mm", "f_done", "fhi_done", "flo_done"))
        vmem_mm, vmem_set = sem("vmem_mm"), sem("vmem_set")
        m_cur, m_qk, m_max, m_exp, m_rden, m_pn, m_t, m_pt, m_pv, m_ohi, m_olo = (sem(n) for n in (
            "m_cur", "m_qk", "m_max", "m_exp", "m_rden", "m_pn", "m_t", "m_pt", "m_pv", "m_ohi", "m_olo"))
        u_pad = sem("u_pad")
        c_cur, c_qk, c_add, c_max, c_exp, c_t, c_pt, c_pv, c_oev, c_vt, c_vset = (sem(n) for n in (
            "c_cur", "c_qk", "c_add", "c_max", "c_exp", "c_t", "c_pt", "c_pv", "c_oev", "c_vt",
            "c_vset"))
        heads_sent = [sem("heads_sent0"), sem("heads_sent1")]
        bias_cut = sem("bias_cut")
        parts_in, cmb_step, cmb_exp, a_tok_set, at_mm, ahi_set = (sem(n) for n in (
            "parts_in", "cmb_step", "cmb_exp", "a_tok_set", "at_mm", "ahi_set"))
        br_tmp, br_f, br_hi, br_lo, tap_done = (sem(n) for n in ("br_tmp", "br_f", "br_hi", "br_lo", "tap_done"))
        v_half, v_copied = sem("v_half"), sem("v_copied")
        ln_add = sem("ln_add")
        proj_half, acc_kept = sem("proj_half"), sem("acc_kept")
        ln_mean, ln_xc, ln_sq, ln_var, ln_rstd, ln_xn, ln_f, ln_hi, ln_lo = (sem(n) for n in (
            "ln_mean", "ln_xc", "ln_sq", "ln_var", "ln_rstd", "ln_xn", "ln_f", "ln_hi", "ln_lo"))
        out_half, y_copied, n_yt, n_sq1, n_std1, n_rstd1, n_sq2, n_std2, n_rstd2 = (sem(n) for n in (
            "out_half", "y_copied", "n_yt", "n_sq1", "n_std1", "n_rstd1", "n_sq2", "n_std2", "n_rstd2"))
        n_post, n_x1, n_xs, n_xt, n_hi, n_lo, gain_in = (sem(n) for n in (
            "n_post", "n_x1", "n_xs", "n_xt", "n_hi", "n_lo", "gain_in"))
        x_again_t = [sem(f"x_again{t}") for t in range(NT)]
        y_zero, ff_hi, ff_lo, ff_y = (sem(n) for n in ("y_zero", "ff_hi", "ff_lo", "ff_y"))
        t_sq, t_std, t_rstd, t_t1, t_sum0, t_yt, stored = (sem(n) for n in (
            "t_sq", "t_std", "t_rstd", "t_t1", "t_sum0", "t_yt", "stored"))
        last_part, last_added = sem("last_part"), sem("last_added")
        t_sum = [t_sum0, sem("t_sum1")]

        Z0_QKV = Z1_QKV = 4 + 2 + MEM_HEADS
        Z01_BR = (Z0_QKV + 12, Z1_QKV + 6)
        Z01_B1 = tuple(n + 5 for n in Z01_BR)
        Z01_B2 = tuple(n + 4 for n in Z01_B1)
        Z01_OUT = tuple(n + 4 for n in Z01_B2)
        Z01_N = tuple(n + 4 for n in Z01_OUT)
        Z01_F = (Z01_N[0], Z01_N[1] + NT - 2)
        Z01_T = tuple(n + 2 * CHUNKS for n in Z01_F)
        Z23_B2 = 4 + 4 + 1
        Z23_N = Z23_B2 + 4
        Z23_F = Z23_N + 4 + 1
        Z23_T = Z23_F + 4 * (CHUNKS - 1)
        TAIL_TILES = (9, 11, 13, 15)

        block = ctx.enter_context(nc.Block())

        def rows3(t):
            return t.rearrange("p (k n) -> p k n", k=KD)

        def x1(t):
            return y_t[:, :, P * t:P * (t + 1)]

        def x_again(t):
            return tmp[:, t, :] if t < 2 else x_rest[:, t - 2, :]

        def last_bank(n):
            return z[2 + n % 4 // 2][:, HALF * (n % 2):HALF * (n % 2 + 1)]

        def tail_z(t):
            return (0, 1, 0, 1, 2, 3, 0, 1)[t]

        def unit_ready(pe, r):
            pe.wait_ge(split_done, r + CREDIT + 1)

        kv_v = w_mem_kv.rearrange("o (k p) n -> p (o k) n", p=P)
        in_v = w_in.rearrange("o (k p) n -> p (o k) n", p=P)
        conv_v = w_conv_out.rearrange("o (k p) n -> p (o k) n", p=P)
        att_v = w_att_out.rearrange("o (k p) n -> p (o k) n", p=P)
        memo_v = w_mem_out.rearrange("o (k p) n -> p (o k) n", p=P)
        out_v = w_out.rearrange("o (k p) n -> p (o k) n", p=P)
        ffi_v = w_ffn_in.rearrange("o (k p) n -> p (o k) n", p=P)
        ffo_v = w_ffn_out.rearrange("o (k p) n -> p (o k) n", p=P)

        @block.sync
        def _(sp):
            def load(r, slot, src, row, k, col, n, free=True):
                src = src.bitcast(u8)
                (row_step, _), (tile_step, _), _ = src.ap
                at = tile_step * row + 4 * col
                src = bass.AP(src.tensor, at if isinstance(at, int) else sp.snap(sp.to_reg(at)),
                              [[row_step, P], [tile_step, k], [1, 4 * n]])
                if free:
                    sp.wait_ge(split_done, r + 1)
                sp.dma_start(raw[:, slot, 0:k * n].rearrange("p (k n) -> p k n", k=k).bitcast(u8), src)\
                    .then_inc(raw_ready[slot], 16)

            sp.dma_start(mem_tok[:, 0, :], mem[0, 0:P, :]).then_inc(mem_in[0], 16)
            sp.dma_start(ident[:], identity).then_inc(ident_in, 16)
            sp.dma_start(mem_tok[:, 1, :], mem[0, P:2 * P, :]).then_inc(mem_in[1], 16)
            for row, v, n in ((V_MIX, norm_mix_pre, 8), (V_MEM, norm_mem, 8), (V_FFN, norm_ffn_pre, 8),
                              (V_GATE, b_gate, 24), (V_DWB, conv_dw_bias, 4), (V_LNG, conv_ln_g, 4),
                              (V_LNB, conv_ln_b, 4)):
                sp.dma_start(vec_rows[row:row + n, :], v.rearrange("o (k p) -> (o k) p", p=P))\
                    .then_inc(consts_in, 16)
            sp.dma_start(tap_rows[:], conv_dw.rearrange("o j (c p) -> (o j c) p", p=P)).then_inc(consts_in, 16)
            load(0, 0, kv_v, 0, KD, 0, P, free=False)
            sp.dma_start(bhot[:], bucket_hot.rearrange("g b n -> b g n")).then_inc(rel_in, 16)
            load(1, 1, kv_v, 0, KD, P, P, free=False)
            for t in range(0, NT, 2):
                if t == 4:
                    for slot in range(2):
                        load(U_KV + 2 + slot, slot, kv_v, 0, KD, P * (2 + slot), P)
                sp.dma_start(x_tok[:, t:t + 2, :], x[0, P * t:P * (t + 2), :].rearrange("(t p) d -> p t d", p=P))\
                    .then_inc(x_in[t // 2], 16)
            with sp.Fori(2, 4) as i:
                for slot in range(2):
                    load(U_KV + 2 * i + slot, slot, kv_v, 0, KD, 2 * P * i + P * slot, P)
            with sp.Fori(0, 2) as i:
                for slot in range(2):
                    load(U_MQ + 2 * i + slot, slot, in_v, 0, KD, C_MEM + 2 * P * i + P * slot, P)
            with sp.Fori(0, CT) as i:
                load(U_CONV + 2 * i, 0, in_v, 0, KD, CONV_W + P * i, P)
                load(U_CONV + 2 * i + 1, 1, in_v, 0, KD, P * i, P)
            sp.wait_ge(rel_out, 48)
            with nc.allow_non_contiguous_dma(reason="Toeplitz rows"):
                sp.dma_start(bias01[:], bass.AP(rel_scratch, P, [[REL - 1, P], [P * REL, 8], [1, 384]]))\
                    .then_inc(tables_in, 16)
                sp.dma_start(bias2[:], bass.AP(rel_scratch, 8 * P * REL + 2 * P,
                                               [[REL - 1, P], [P * REL, 4], [1, P]])).then_inc(tables_in, 16)
            with sp.Fori(0, 6) as i:
                for j in range(6):
                    load(U_QKV + 6 * i + j, j % 2,
                         in_v, 4 * (j % 2), 4, C_ATT + ATT_W * (j // 2) + P * i, P)
            for b, (proj, k) in enumerate(((memo_v, 4), (att_v, 2), (conv_v, 4))):
                branch = (2, 1, 0)[b]
                with sp.Fori(0, 2) as i:
                    for j in range(2):
                        for q in range(2):
                            r = U_BR + 12 * b + 6 * i + 3 * j + q
                            load(r, (3 * j + q) % 2,
                                 in_v, 0, KD, C_GATE + D * branch + HALF * i + P * (2 * j + q), P)
                        load(U_BR + 12 * b + 6 * i + 3 * j + 2, (3 * j + 2) % 2,
                             proj, 0, k, HALF * i + 256 * j, 256)
            with sp.Fori(0, 4) as i:
                for slot in range(2):
                    load(U_OUT + 2 * i + slot, slot, out_v, 0, KD, 2 * P * i + P * slot, P)
            sp.dma_start(post_gain[:], norm_mix_post.to_broadcast([P, D])).then_inc(gain_in, 16)
            sp.wait_ge(br_lo, KD)
            for t in range(2):
                sp.dma_start(x_again(t), x[0, P * t:P * (t + 1), :]).then_inc(x_again_t[t], 16)

            def load_ffn_in(r, slot, tile, gate):
                load(r, slot, ffi_v, 0, KD, (0 if gate else HIDDEN) + P * tile, P)

            def load_ffn_out(r, slot, chunk, half):
                load(r, slot, ffo_v, 2 * chunk, 2, HALF * half, HALF)

            load_ffn_in(U_FFN, 0, 0, True)
            load_ffn_in(U_FFN + 1, 1, 0, False)
            sp.wait_ge(unit_done, U_FFN + CREDIT)
            for t in range(2, NT):
                sp.dma_start(x_again(t), x[0, P * t:P * (t + 1), :]).then_inc(x_again_t[t], 16)
            load_ffn_in(U_FFN + 2, 0, 1, True)
            load_ffn_in(U_FFN + 3, 1, 1, False)
            sp.wait_ge(n_post, NT)
            sp.dma_start(post_gain[:], norm_ffn_post.to_broadcast([P, D])).then_inc(gain_in, 16)
            with sp.Fori(1, CHUNKS) as c:
                r = U_FFN - 2 + 6 * c
                for j in range(2):
                    load_ffn_in(r + 3 * j, (3 * j) % 2, 2 * c + j, True)
                    load_ffn_in(r + 3 * j + 1, (3 * j + 1) % 2, 2 * c + j, False)
                    load_ffn_out(r + 3 * j + 2, (3 * j + 2) % 2, c - 1, j)
            for half in range(2):
                load_ffn_out(N_UNITS - 2 + half, half, CHUNKS - 1, half)
            for t in range(NT):
                sp.wait_ge(t_sum[t % 2], t // 2 + 1)
                sp.dma_start(out[0, P * t:P * (t + 1), :].rearrange("p (k n) -> p k n", k=KD), x1(t)).then_inc(stored, 16)
            sp.wait_ge(stored, 16 * NT)

        @block.gpsimd
        def _(pool):
            pool.sem_inc(split_done, CREDIT)
            nc.gpsimd.memset(zeros[:], 0.0).then_inc(consts_set, 1)
            nc.gpsimd.memset(eps_rms[:], 1e-6).then_inc(consts_set, 1)
            nc.gpsimd.memset(eps_ln[:], 1e-5).then_inc(consts_set, 1)
            nc.gpsimd.memset(ones[:], 1.0 / CONV_W).then_inc(consts_set, 1)
            nc.gpsimd.memset(rel[:], 1.0).then_inc(rel_ones, 1)
            pool.wait_ge(consts_set, 4)

            def split(r, n, slot, width=1024, free=True):
                pool.wait_ge(raw_ready[slot], 16 * (n + 1))
                if free:
                    pool.wait_ge(unit_done, r + 1)
                a = width // P
                view = [w[:, slot, 0:width].rearrange("p (a b) -> p a b", a=a) for w in (raw, w_hi, w_lo)]
                nc.gpsimd.tensor_tensor(view[1], view[0], zeros[:].unsqueeze(1).to_broadcast([P, a, P]),
                                        ALU.add).then_inc(hi_done, 1)
                pool.wait_ge(hi_done, r + 1)
                nc.gpsimd.tensor_tensor(view[2], view[0], view[1], ALU.subtract).then_inc(split_done, 1)

            def split_run(first, last, widths=(1024, 1024)):
                per = len(widths)
                with pool.Fori(0, (last - first) // per) as i:
                    for j, width in enumerate(widths):
                        split(first + per * i + j, first // 2 + per // 2 * i + j // 2, j % 2, width)

            for slot in range(2):
                split(slot, 0, slot, free=False)
            for r in range(2, U_MQ):
                pool.wait_ge(hi_done, r + 1)
                nc.gpsimd.tensor_tensor(w_lo[:, r % 2, :], raw[:, r % 2, :], w_hi[:, r % 2, :], ALU.subtract)\
                    .then_inc(split_done, 1)
            split_run(U_MQ, U_QKV)
            split_run(U_QKV, U_BR, (512, 512))
            split_run(U_BR, U_BR + 12)
            split_run(U_BR + 12, U_BR + 24, (1024, 1024, 512, 1024, 1024, 512))
            split_run(U_BR + 24, U_FFN)
            split(U_FFN, U_FFN // 2, 0)
            for t in range(NT):
                if t == 3:
                    split(U_FFN + 1, U_FFN // 2, 1)
                pool.wait_ge(x_again_t[t], 16)
                pool.wait_ge(n_post, t + 1)
                nc.gpsimd.tensor_tensor(x1(t), x1(t), rows3(x_again(t)), ALU.add).then_inc(n_x1, 1)
            pool.wait_ge(unit_done, U_FFN + CREDIT)
            nc.gpsimd.memset(y_sum[:], 0.0).then_inc(y_zero, 1)
            split_run(U_FFN + 2, N_UNITS)
            for t in range(0, NT, 2):
                pool.wait_ge(t_t1, t + 1)
                nc.gpsimd.tensor_tensor(x1(t), x1(t), rows3(tmp[:, 0, :]), ALU.add).then_inc(t_sum[0], 1)

        SPLIT_PRODUCTS = ("hh", "hl", "lh")

        def products(slot, k_tiles, pick, cols, rhs_hi, rhs_lo, dst, rhs_n, first=0, last=None):
            todo = []
            halves = (rhs_n + HALF - 1) // HALF
            n = min(rhs_n, HALF)
            for h in range(halves):
                for k in range(k_tiles):
                    for what in SPLIT_PRODUCTS:
                        w = w_hi if what[0] == "h" else w_lo
                        m = rhs_hi if what[1] == "h" else rhs_lo
                        todo.append((dst[:, h * HALF:h * HALF + n], w[:, slot, pick(k) + cols:pick(k) + cols + P],
                                     m(k, h * HALF, n), first == 0 and k == 0 and what == "hh",
                                     last is None and k == k_tiles - 1 and what == "lh"))
            return todo

        def issue(todo):
            for dst, w, m, start, stop in todo:
                mm = nc.tensor.matmul(dst, w, m, start=start, stop=stop)
            return mm

        def h_rhs(t):
            return lambda k, at, n: t[:, k, at:at + n]

        def unit_todo(slot, dst):
            return products(slot, KD, lambda k: P * k, 0, h_rhs(h_hi), h_rhs(h_lo), dst, T)

        @block.tensor
        def _(pe):
            pe.sem_inc(unit_done, CREDIT)
            for s in (m_t, m_pv, c_t, c_pv):
                pe.sem_inc(s, 2)

            def transposes(dst, src, n, done):
                for k in range(n):
                    mm = nc.tensor.transpose(dst[:, P * k:P * (k + 1)], src[:, P * k:P * (k + 1)], ident[:])
                mm.then_inc(done, 1)

            pe.wait_ge(ident_in, 16)
            for t in range(2):
                pe.wait_ge(xs_done, t + 1)
                transposes(z[2 + t], xs0[:, t], KD, xt_mm)
            pe.wait_ge(consts_in, 16 * 8)
            nc.tensor.transpose(z[0][:, 0:N_VEC], vec_rows[:], ident[0:N_VEC, 0:N_VEC])
            nc.tensor.transpose(z[0][:, P:P + TAPS * CT], tap_rows[:], ident[0:TAPS * CT, 0:TAPS * CT])\
                .then_inc(vec_mm, 1)
            pe.wait_ge(rel_in, 32)
            for g in range(3):
                dst = z[1][0:SLOTS_H, HALF * g:HALF * (g + 1)] if g < 2 else z[0][0:SLOTS_H, HALF:2 * HALF]
                mm = nc.tensor.matmul(dst, rel[:, SLOTS_H * g:SLOTS_H * (g + 1)], bhot[:, g, :], start=True, stop=True)
            mm.then_inc(rel_mm, 1)
            pe.wait_ge(flo_done, 2)
            pe.wait_ge(rel_rows, 3)
            with pe.Fori(0, 4) as i:
                for s in range(2):
                    n = 2 * i + s
                    unit_ready(pe, U_KV + n)
                    pe.wait_ge(z_free[s], i + 1)
                    issue(products(s, KD, lambda k: P * k, 0, h_rhs(mem_hi_t), h_rhs(mem_lo_t), z[s], N_MEM))\
                        .then_inc(unit_done, 1)
                    pe.wait_ge(xs_done, n + 3)
                    pe.wait_ge(f_done, n + 1)
                    transposes(z[2 + s], xs0[:, s], KD, xt_mm)
            def part(slot, rhs_hi, rhs_lo, dst, at, n):
                return issue(products(slot, KD, lambda k: P * k, 0, lambda k, _, m: rhs_hi[:, k, at:at + m],
                                      lambda k, _, m: rhs_lo[:, k, at:at + m], dst[:, at:at + n], n))

            def first_queries(half):
                for s in range(2):
                    if half == 0:
                        unit_ready(pe, U_MQ + s)
                        pe.wait_ge(z_free[s], 4 + 1)
                    mm = part(s, h_hi, h_lo, z[s], HALF * half, HALF)
                    if half == 1:
                        mm.then_inc(unit_done, 1)

            pe.wait_ge(flo_done, 2 + NT // 2)
            first_queries(0)
            for k in range(2):
                pe.wait_ge(z_free[k], 4 + 1)
            pe.wait_ge(f_done, 9)
            for c in range(2):
                for h in range(MEM_HEADS):
                    mm = nc.tensor.transpose(z[2][:, P * (4 * c + h):P * (4 * c + h + 1)],
                                             kv_t[:, MEM_HEADS + h, P * c:P * (c + 1)], ident[:])
            mm.then_inc(vmem_mm, 1)
            pe.wait_ge(flo_done, 10)
            first_queries(1)
            for s in range(2):
                unit_ready(pe, U_MQ + 2 + s)
                pe.wait_ge(z_free[s], 5 + 1)
                issue(unit_todo(s, z[s])).then_inc(unit_done, 1)

            def conv_issue(conv, share, h):
                for j, n in share:
                    if n == 0:
                        unit_ready(pe, U_CONV + 2 * h + j)
                        pe.wait_ge(z_free[j], 6 + h + 1)
                    mm = issue([conv[j][n]])
                    if n == len(conv[j]) - 1:
                        mm.then_inc(unit_done, 1)

            pe.wait_ge(vmem_set, 1)
            pe.wait_ge(f_done, 10)
            with pe.Fori(0, MEM_HEADS) as h:
                conv = [unit_todo(0, z[0]), unit_todo(1, z[1])]
                flat = [(j, n) for j in range(2) for n in range(len(conv[j]))]
                share = 8
                conv_issue(conv, flat[:2 * share], h)
                for step in range(10):
                    if step in (5, 9):
                        half = (step - 5) // 4
                        pe.wait_ge(m_pt, 8 * h + 4 * half + 4 + 1)
                        pe.wait_ge(m_olo, 2 * h + half + 1)
                        for c in range(2):
                            mm = nc.tensor.matmul(o_bank, v_cur[:, c, :], pt_mem[:, half, c, :], start=c == 0, stop=c == 1)
                        mm.then_inc(m_pv, 1)
                    if 1 <= step <= 8:
                        t = step - 1
                        pe.wait_ge(m_pn, 8 * h + t + 1)
                        pe.wait_ge(m_pt, 8 * h + t + 1)
                        for c in range(2):
                            at = P * c
                            mm = nc.tensor.transpose(t_bank[:, at:at + P], p_mem[:, t % 2, P * c:P * (c + 1)], ident[:])
                        mm.then_inc(m_t, 1)
                    if step < 8:
                        t = step
                        if t == 0:
                            pe.wait_ge(m_cur, h + 1)
                        pe.wait_ge(m_exp, 8 * h + t + 1)
                        nc.tensor.matmul(s_bank[:, t % 2, 0:N_MEM], q_cur[:, P * t:P * (t + 1)],
                                         kv_t[:, bass.ds(h, 1), :].rearrange("p a n -> p (a n)"),
                                         start=True, stop=True).then_inc(m_qk, 1)
                    conv_issue(conv, flat[share * (step + 2):share * (step + 3)], h)

            def qkv_todo():
                todo = []
                for j in range(6):
                    dst = z[(j // 2) % 2]
                    half_k = j % 2
                    part = []
                    for hh in range(2):
                        for k in range(4):
                            for what in SPLIT_PRODUCTS:
                                w = w_hi if what[0] == "h" else w_lo
                                m = h_hi if what[1] == "h" else h_lo
                                part.append((dst[:, hh * HALF:(hh + 1) * HALF], w[:, j % 2, P * k:P * (k + 1)],
                                             m[:, 4 * half_k + k, hh * HALF:(hh + 1) * HALF],
                                             half_k == 0 and k == 0 and what == "hh",
                                             half_k == 1 and k == 3 and what == "lh"))
                    todo += [(j, n, len(part), mm) for n, mm in enumerate(part)]
                return todo


            def qkv_issue(share, pair):
                for j, n, size, mm in share:
                    if n == 0:
                        unit_ready(pe, U_QKV + 6 * pair + j)
                        if j == 0:
                            pe.wait_ge(v_copied, pair + 1)
                        if j == 2:
                            pe.wait_ge(z_free[1], Z1_QKV + pair + 1)
                        if j == 4:
                            pe.wait_ge(z_free[0], Z0_QKV + 2 * pair + 2)
                    if j == 0 and n == size // 2:
                        pe.wait_ge(z_free[0], Z0_QKV + 2 * pair + 1)
                    m = issue([mm])
                    if n == size - 1:
                        m.then_inc(unit_done, 1)
                    elif j == 5 and n == size // 2 - 1:
                        m.then_inc(v_half, 1)

            def scores(g, pair, t):
                pe.wait_ge(c_add, 8 * pair + t + 1)
                start = window(g, t)[0]
                n = P if g == 2 else 2 * P
                for hd in range(2):
                    rows = slice(ATT_E * hd, ATT_E * (hd + 1))
                    mm = nc.tensor.matmul(s_bank[:, hd, 0:n], cur[rows, 0, P * t:P * (t + 1)],
                                          cur[rows, 1, start:start + n], start=True, stop=True)
                mm.then_inc(c_qk, 1)

            def gates_todo():
                todo = []
                for q in range(2):
                    part = unit_todo(q, z[q])
                    todo += [(q, n, len(part), mm) for n, mm in enumerate(part)]
                return todo

            def gates_issue(share):
                for q, n, size, mm in share:
                    if n == 0:
                        unit_ready(pe, U_BR + q)
                        pe.wait_ge(z_free[q], Z01_BR[q] + 1)
                    m = issue([mm])
                    if n == size - 1:
                        m.then_inc(unit_done, 1)

            def dilated_pair(g, pair, vb, more):
                todo = qkv_todo() if more else gates_todo()
                share = -(-len(todo) // 11)

                def fill(n):
                    if more:
                        qkv_issue(todo[share * n:share * (n + 1)], pair + 1)
                    else:
                        gates_issue(todo[share * n:share * (n + 1)])

                tile = 8 * pair
                chunks = V_CHUNKS[g]
                fill(0)
                for step in range(10):
                    if step == 0:
                        pe.wait_ge(c_cur, 3 * pair + 2)
                        scores(g, pair, 0)
                        pe.wait_ge(c_cur, 3 * pair + 3)
                        pe.wait_ge(c_oev, tile + 1)
                        pe.wait_ge(c_pt, tile + 1)
                    for b in ((0, 1) if step == 0 else (2,) if step == 1 and V_BATCHES[g] == 3 else ()):
                        if b == 2:
                            pe.wait_ge(c_vset, vb + 1)
                        dst = t_bank if b == 1 else o_bank
                        for j, start in enumerate(chunks[4 * b:4 * b + 4]):
                            mm = nc.tensor.transpose(dst[:, P * j:P * (j + 1)], cur[:, 2, start:start + P], ident[:])
                        mm.then_inc(c_vt, 1)
                    if step >= 2:
                        t = step - 2
                        if t == 0:
                            pe.wait_ge(c_vset, vb + V_BATCHES[g])
                        pe.wait_ge(c_pt, tile + t + 2)
                        pe.wait_ge(c_oev, tile + t + 1)
                        start = window(g, t)[0]
                        keys = 1 if g == 2 else 2
                        for hd in range(2):
                            for c in range(keys):
                                mm = nc.tensor.matmul(o_bank[:, ATT_E * hd:ATT_E * (hd + 1)], p_t[:, t % 2, 2 * hd + c, :],
                                                      v_tok[:, chunks.index(start + P * c), ATT_E * hd:ATT_E * (hd + 1)],
                                                      start=c == 0, stop=c == keys - 1)
                        mm.then_inc(c_pv, 1)
                    if 1 <= step <= 8:
                        t = step - 1
                        if t == 0:
                            pe.wait_ge(c_vset, vb + 2)
                        pe.wait_ge(c_exp, tile + t + 3)
                        pe.wait_ge(c_pt, tile + t + 1)
                        for hd in range(2):
                            for c in range(1 if g == 2 else 2):
                                mm = nc.tensor.transpose(t_bank[:, P * (2 * hd + c):P * (2 * hd + c + 1)],
                                                         prob[:, t % 2, hd, P * c:P * (c + 1)], ident[:])
                        mm.then_inc(c_t, 1)
                    if 1 <= step < 8:
                        scores(g, pair, step)
                    fill(step + 1)

            pe.wait_ge(z_free[0], Z0_QKV + 1)
            qkv_issue(qkv_todo(), 0)
            pe.wait_ge(m_exp, 8 * MEM_HEADS + 2)
            pe.wait_ge(m_pt, 8 * MEM_HEADS + 1)
            pe.wait_ge(m_olo, 2 * MEM_HEADS + 1)
            for g in range(2):
                with pe.Fori(0, 2) as i:
                    dilated_pair(g, 2 * g + i, v_batches_before(2 * g) + V_BATCHES[g] * i, True)
            dilated_pair(2, 4, v_batches_before(4), True)
            dilated_pair(2, 5, v_batches_before(5), False)
            pe.wait_ge(c_add, 8 * 6 + 1)
            pe.wait_ge(c_oev, 8 * 6 + 1)


            def gates(b, i, j, z01):
                for q in range(2):
                    unit_ready(pe, U_BR + 12 * b + 6 * i + 3 * j + q)
                    pe.wait_ge(z_free[q], z01[q] + 2 * i + j + 1)
                    issue(unit_todo((3 * j + q) % 2, z[q])).then_inc(unit_done, 1)

            def projection(b, i, j, k_tiles, rhs_hi, rhs_lo, z23, tiles=(0, 1)):
                unit_ready(pe, U_BR + 12 * b + 6 * i + 3 * j + 2)
                for q in tiles:
                    pe.wait_ge(z_free[2 + q], z23 + 2 * i + j + 1)
                    issue(products((3 * j + 2) % 2, k_tiles, lambda k: 256 * k, P * q,
                                   rhs_hi, rhs_lo, z[2 + q], T)).then_inc((proj_half, unit_done)[q], 1)

            for n in range(4):
                if n:
                    gates(0, n // 2, n % 2, Z01_BR)
                projection(0, n // 2, n % 2, 4, h_rhs(m_hi), h_rhs(m_lo), 0, (0, 1) if n < 3 else (0,))
            pe.wait_ge(a_tok_set, 1)
            for c in range(2):
                pe.wait_ge(z_free[c], Z01_BR[c] + 4 + 1)
                for t in range(NT):
                    mm = nc.tensor.transpose(z[c][:, P * t:P * (t + 1)], a_tok[:, t, P * c:P * (c + 1)], ident[:])
                mm.then_inc(at_mm, 1)
            projection(0, 1, 1, 4, h_rhs(m_hi), h_rhs(m_lo), 0, (1,))
            for n in range(4):
                gates(1, n // 2, n % 2, Z01_B1)
                if n == 1:
                    pe.wait_ge(z_free[3], 4 + 1 + 1)
                    pe.wait_ge(ln_add, 6)
                    for hh in range(2):
                        mm = nc.tensor.matmul(z[3][:, HALF * hh:HALF * (hh + 1)], ones[:],
                                              ln_sum[:, 1, HALF * hh:HALF * (hh + 1)], start=True, stop=True)
                    mm.then_inc(ln_var, 1)
                projection(1, n // 2, n % 2, 2, h_rhs(a_hi), h_rhs(a_lo), 5 if n else 4)
                if n == 0:
                    pe.wait_ge(ln_add, 3)
                    pe.wait_ge(z_free[2], 4 + 1 + 1)
                    for hh in range(2):
                        mm = nc.tensor.matmul(z[2][:, HALF * hh:HALF * (hh + 1)], ones[:],
                                              ln_sum[:, 0, HALF * hh:HALF * (hh + 1)], start=True, stop=True)
                    mm.then_inc(ln_mean, 1)
            with pe.Fori(0, 2) as i:
                for j in range(2):
                    gates(2, i, j, Z01_B2)
                    pe.wait_ge(ln_lo, CT)
                    projection(2, i, j, 4, h_rhs(c_hi), h_rhs(c_lo), Z23_B2)

            def out_unit(s, i, first=False):
                unit_ready(pe, U_OUT + 2 * i + s)
                pe.wait_ge(z_free[s], Z01_OUT[s] + i + 1)
                todo = products(s, KD, lambda k: P * k, 0, h_rhs(merged_hi), h_rhs(merged_lo), z[s], T)
                for n in range(0, len(todo), 3):
                    if first and n < 3 * KD:
                        pe.wait_ge(br_lo, n // 3 + 1)
                    mm = issue(todo[n:n + 3])
                mm.then_inc(unit_done, 1)

            out_unit(0, 0, first=True)
            out_unit(1, 0)
            with pe.Fori(1, 3) as i:
                for s in range(2):
                    out_unit(s, i)

            def y_tile(src, t, k, z23, done):
                pe.wait_ge(z_free[k], z23 + 1)
                for c in range(KD):
                    mm = nc.tensor.transpose(z[k][:, P * c:P * (c + 1)], src[:, c, P * t:P * (t + 1)], ident[:])
                mm.then_inc(done, 1)

            for s in range(2):
                unit_ready(pe, U_OUT + 6 + s)
                pe.wait_ge(z_free[s], Z01_OUT[s] + 3 + 1)
                part(s, merged_hi, merged_lo, z[s], 0, HALF).then_inc(out_half, 1)
            part(0, merged_hi, merged_lo, z[0], HALF, HALF).then_inc(unit_done, 1)
            pe.wait_ge(y_copied, 2)
            for t in range(2):
                y_tile(y_t, t, 2 + t, Z23_N, n_yt)
            part(1, merged_hi, merged_lo, z[1], HALF, HALF).then_inc(unit_done, 1)

            def first_hidden(s, quarter):
                if quarter == 0:
                    unit_ready(pe, U_FFN + s)
                    pe.wait_ge(z_free[s], Z01_F[s] + 1)
                pe.wait_ge(n_lo, 2 * quarter + 2)
                mm = part(s, h_hi, h_lo, z[s], 256 * quarter, 256)
                if quarter == 3:
                    mm.then_inc(unit_done, 1)

            y_tile(y_t, 2, 2, Z23_N + 1, n_yt)
            for t in range(NT):
                pe.wait_ge(n_xs, t + 1)
                k = 1 if t < NT - 2 else t - 4
                pe.wait_ge(z_free[k], Z01_N[1] + t + 1 if k == 1 else Z23_N + 4 + 1)
                transposes(z[k], sg[:, t % 2], KD, n_xt)
                if t + 3 < NT:
                    if t + 3 == 4:
                        pe.wait_ge(y_copied, 4)
                    y_tile(y_t, t + 3, 2 + (t + 3) % 2, Z23_N + (t + 3) // 2, n_yt)
                for s, quarter in {2: [(0, 0)], 4: [(0, 1)], 5: [(1, 0)], 6: [(1, 1)],
                                   7: [(0, 2), (0, 3), (1, 2), (1, 3)]}.get(t, []):
                    first_hidden(s, quarter)

            def hidden(r, slot0, z01):
                for s in range(2):
                    slot = (slot0 + s) % 2
                    unit_ready(pe, r + s)
                    pe.wait_ge(z_free[s], z01[s] + 1)
                    issue(unit_todo(slot, z[s])).then_inc(unit_done, 1)

            def ffn_out(r, slot, act_slot, z23):
                unit_ready(pe, r)
                for q in range(4):
                    pe.wait_ge(z_free[2 + q % 2], z23 + q // 2 + 1)
                    mm = issue(products(slot, 2, lambda k: HALF * k, P * q,
                                        lambda k, at, n: act_hi[:, act_slot, k, at:at + n],
                                        lambda k, at, n: act_lo[:, act_slot, k, at:at + n], z[2 + q % 2], T))
                    if q < 3:
                        mm.then_inc(ff_y, 1)
                mm.then_inc(unit_done, 1)

            def chunk(c, act_slot):
                for j in range(2):
                    r = U_FFN - 2 + 6 * c + 3 * j
                    hidden(r, (3 * j) % 2, (Z01_F[0] + 2 * c + j, Z01_F[1] + 2 * c + j))
                    if j == 0:
                        pe.wait_ge(ff_lo, 2 * c)
                    ffn_out(r + 2, (3 * j + 2) % 2, act_slot, Z23_F + 4 * (c - 1) + 2 * j)

            hidden(U_FFN + 2, 0, (Z01_F[0] + 1, Z01_F[1] + 1))
            with pe.Fori(0, (CHUNKS - 1) // 2) as i:
                for s in range(2):
                    chunk(2 * i + 1 + s, s)
            pe.wait_ge(ff_lo, 2 * CHUNKS)
            a_slot = (CHUNKS - 1) % 2
            for n in range(2 * KD):
                half, d = n // KD, n % KD
                at = slice(HALF * half, HALF * half + HALF)
                if n in (0, 2):
                    pe.wait_ge(z_free[2 + n // 2], Z23_T + 1)
                if n in (0, 4):
                    unit_ready(pe, N_UNITS - 2 + n // 4)
                if n >= 4:
                    pe.wait_ge(last_added, n - 3)
                issue(products(d // 4, 2, lambda k: HALF * k, P * (d % 4), lambda k, _, m: act_hi[:, a_slot, k, at],
                               lambda k, _, m: act_lo[:, a_slot, k, at], last_bank(n), HALF)).then_inc(last_part, 1)
                if n in TAIL_TILES:
                    t = TAIL_TILES.index(n)
                    pe.wait_ge(last_added, KD)
                    y_tile(y_sum, t, t % 2, Z01_T[t % 2] + t // 2, t_yt)
            pe.wait_ge(last_added, 2 * KD)
            for t in range(4, NT):
                y_tile(y_sum, t, tail_z(t), Z23_T if t < 6 else Z01_T[t % 2] + 2, t_yt)

        @block.scalar
        def _(act):
            for s, credit in ((m_exp, 2), (m_pt, 1), (c_exp, 2), (c_pt, 1), (heads_sent[0], 16), (v_copied, 1),
                              (heads_sent[1], 16), (z_free[0], 1)):
                act.sem_inc(s, credit)
            a = nc.scalar.activation

            def load_table(func, col):
                a(std[:, col:col + 1], eps_rms[:, 0:1], func)

            act.wait_ge(rel_ones, 1)
            act.dma_start(rel[0:32, :], rel_bias).then_inc(rel_in, 16)
            act.wait_ge(consts_set, 4)
            load_table(ACT.Sqrt, S_SPARE[0])

            def token_stats(j):
                act.wait_ge(mem_in[j] if j < 2 else x_in[(j - 2) // 2], 16)
                src = mem_tok[:, j, :] if j < 2 else x_tok[:, j - 2, :]
                if j:
                    act.wait_ge(sq_done, j)
                a(junk0[:], src, ACT.Square, accum_out=sumsq[:, stat(j)]).then_inc(sq_done, 1)
                act.wait_ge(sq_done, j + 1)
                a(std[:, stat(j)], sumsq[:, stat(j)], ACT.Sqrt, bias=eps_rms[:, 0:1], scale=1.0 / D)\
                    .then_inc(std_done, 1)

            def token_hi(j):
                act.wait_ge(f_done, j + 1)
                dst = mem_hi_t[:, :, P * j:P * (j + 1)] if j < 2 else h_hi[:, :, P * (j - 2):P * (j - 1)]
                a(dst, f0[j % 2][:].rearrange("p (k n) -> p k n", k=KD), ACT.Copy).then_inc(fhi_done, 1)

            token_stats(0)
            token_stats(1)
            act.wait_ge(vec_mm, 1)
            a(vcols[:], z[0][:, 0:N_VEC], ACT.Copy).then_inc(vec_set, 1)
            a(taps[:].rearrange("p j c -> p (j c)"), z[0][:, P:P + TAPS * CT], ACT.Copy).then_inc(vec_set, 1)
            token_hi(0)
            token_hi(1)
            act.wait_ge(rel_mm, 1)
            a(e_rows[:, 0:2, :].rearrange("h g n -> h (g n)"), z[1][0:SLOTS_H, :], ACT.Copy).then_inc(rel_rows, 2)
            a(e_rows[:, 2, :], z[0][0:SLOTS_H, HALF:2 * HALF], ACT.Copy).then_inc(rel_rows, 1)
            token_stats(2)
            for n in range(8):
                if n + 3 < 10:
                    token_stats(n + 3)
                act.wait_ge(unit_done, U_KV + n + 1 + CREDIT)
                if n + 2 < U_MQ:
                    act.wait_ge(raw_ready[n % 2], 16 * (n // 2 + 2))
                    act.wait_ge(hi_done, n + 2)
                    a(w_hi[:, n % 2, :], raw[:, n % 2, :], ACT.Copy).then_inc(hi_done, 1)
                a(kv_t[:, n, :], z[n % 2][:, 0:N_MEM], ACT.Copy).then_inc(z_free[n % 2], 1)
                token_hi(n + 2)
            act.wait_ge(rel_rows, 3)
            for g in range(3):
                src = e_rows[:, g, :].unsqueeze(1).to_broadcast([SLOTS_H, P, REL])
                act.dma_start(rel_scratch.ap()[SLOTS_H * g:SLOTS_H * (g + 1), :, :], src).then_inc(rel_out, 16)
            act.wait_ge(vmem_mm, 1)
            act.wait_ge(flo_done, 10)
            a(v_mem[:].rearrange("p c h n -> p (c h n)"), z[2][:], ACT.Copy).then_inc(vmem_set, 1)
            for h in range(MEM_HEADS):
                act.wait_ge(unit_done, U_MQ + h + 1 + CREDIT)
                a(q_mem[:, h, :], z[h % 2][:], ACT.Copy, scale=P ** -0.5).then_inc(z_free[h % 2], 1)

            act.wait_ge(rel_out, 48)
            with act.Fori(0, MEM_HEADS) as h:
                for step in range(10):
                    if 1 <= step <= 8:
                        t = step - 1
                        act.wait_ge(m_t, 8 * h + t + 3)
                        act.wait_ge(m_pv, 2 * h + t // 4 + 1)
                        a(pt_mem[:, t // 4, :, P * (t % 4):P * (t % 4 + 1)],
                          t_bank[:, 0:256].rearrange("p (c n) -> p c n", c=2), ACT.Copy)\
                            .then_inc(m_pt, 1)
                    if step < 8:
                        t = step
                        act.wait_ge(m_max, 8 * h + t + 1)
                        act.wait_ge(m_t, 8 * h + t + 1)
                        a(p_mem[:, t % 2, :], s_bank[:, t % 2, 0:N_MEM], ACT.Exp, bias=mstat[:, t % 2, 0:1],
                          accum_out=mstat[:, t % 2, 1:2]).then_inc(m_exp, 1)
                act.wait_ge(unit_done, U_CONV + 2 * h + 1 + CREDIT)
                act.wait_ge(z_free[1], 6 + h + 1)
                a(sg_conv[:], z[0][:], ACT.Sigmoid).then_inc(z_free[0], 1)
                load_table(ACT.Exp, S_SPARE[1])

            def next_evac(j, pair, first=False):
                act.wait_ge(unit_done, U_QKV + 6 * pair + 2 * j + 2 + CREDIT)
                if not first:
                    act.wait_ge(c_cur, 3 * pair)
                a(nxt[:, j, :], z[j % 2][:], ACT.Copy, scale=ATT_E ** -0.5 if j == 0 else 1.0)\
                    .then_inc(z_free[j % 2], 1)

            def next_values(pair, first=False):
                act.wait_ge(v_half, pair + 1)
                if not first:
                    act.wait_ge(c_cur, 3 * pair)
                a(nxt[:, 2, 0:HALF], z[0][:, 0:HALF], ACT.Copy).then_inc(v_copied, 1)
                act.wait_ge(unit_done, U_QKV + 6 * pair + 6 + CREDIT)
                a(nxt[:, 2, HALF:T], z[0][:, HALF:T], ACT.Copy).then_inc(z_free[0], 1)

            def dilated_pair(g, pair, vb, more):
                tile = 8 * pair
                n = P if g == 2 else 2 * P
                for step in range(10):
                    for b in ((0, 1) if step == 0 else (2,) if step == 1 and V_BATCHES[g] == 3 else ()):
                        act.wait_ge(c_vt, vb + b + 1)
                        m = len(V_CHUNKS[g][4 * b:4 * b + 4])
                        a(v_tok[:, 4 * b:4 * b + m, :].rearrange("p j n -> p (j n)"),
                          (t_bank if b == 1 else o_bank)[:, 0:P * m], ACT.Copy).then_inc(c_vset, 1)
                    if 1 <= step <= 8:
                        t = step - 1
                        act.wait_ge(c_t, tile + t + 3)
                        act.wait_ge(c_pv, tile + t + 1)
                        if g == 2:
                            a(p_t[:, t % 2, 0:4:2, :], t_bank.rearrange("p (b n) -> p b n", b=4)[:, 0:4:2, :],
                              ACT.Copy).then_inc(c_pt, 1)
                        else:
                            a(p_t[:, t % 2, :, :].rearrange("p b n -> p (b n)"), t_bank, ACT.Copy).then_inc(c_pt, 1)
                    if step < 8:
                        t = step
                        act.wait_ge(c_max, tile + t + 1)
                        act.wait_ge(c_t, tile + t + 1)
                        for hd in range(2):
                            i = a(prob[:, t % 2, hd, 0:n], sbias[:, t % 2, hd, 0:n], ACT.Exp,
                                  bias=heads_out[:, t, hd, ATT_E + 1:ATT_E + 2],
                                  accum_out=heads_out[:, t, hd, ATT_E:ATT_E + 1])
                        i.then_inc(c_exp, 1)
                    if more and step in (3, 6):
                        next_evac((step - 3) // 3, pair + 1)
                    if step == 6:
                        act.wait_ge(c_oev, tile + 4 + 1)
                        send(g, pair, 0)
                if more:
                    next_values(pair + 1)
                act.wait_ge(c_oev, tile + 8 + 1)
                send(g, pair, 1)
                if not more:
                    gate(0, 0, 0)
                    gate(0, 1, 1)

            def gate(b, q, d):
                r = U_BR + 12 * b + 6 * (d // 4) + 3 * (d % 4 // 2) + d % 2
                act.wait_ge(unit_done, r + 1 + CREDIT)
                act.wait_ge(z_free[2 + q], 4 * b + d // 2 + 1 + (b == 2 or b == 1 and d >= 4))
                col = V_GATE + KD * (2, 1, 0)[b] + d
                a(sg[:, q, :], z[q][:], ACT.Sigmoid, bias=vcols[:, col:col + 1]).then_inc(z_free[q], 1)

            def send(g, pair, half):
                col = 2 * ROW * (pair - 2 * g)
                rows = att_scratch[g, :, bass.ds(col, 2 * ROW)]
                ts = slice(4 * half, 4 * half + 4)
                src = heads_out[:, ts].rearrange("p t h n -> p t (h n)")
                if g == 0:
                    act.dma_start(rows.rearrange("(t p) n -> p t n", p=P)[:, ts], src).then_inc(heads_sent[half], 16)
                elif g == 1:
                    for r in range(2):
                        act.dma_start(rows.rearrange("(c p r) n -> r p c n", p=P, c=2)[2 * half + r],
                                      src[:, 2 * r:2 * r + 2]).then_inc(heads_sent[half], 16)
                else:
                    for b in range(2):
                        act.dma_start(rows.rearrange("(l t a) n -> a l t n", t=8, a=2)[b, :, ts],
                                      src[64 * b:64 * (b + 1)]).then_inc(heads_sent[half], 16)

            act.wait_ge(z_free[1], 6 + MEM_HEADS + 1)
            for j in range(2):
                next_evac(j, 0, first=True)
            next_values(0, first=True)
            for g in range(2):
                with act.Fori(0, 2) as i:
                    dilated_pair(g, 2 * g + i, v_batches_before(2 * g) + V_BATCHES[g] * i, True)
            dilated_pair(2, 4, v_batches_before(4), True)
            dilated_pair(2, 5, v_batches_before(5), False)
            for half in range(2):
                act.wait_ge(heads_sent[half], 16 * (1 + 2 + 4 + 4))
            for g in range(3):
                act.dma_start(parts[:, g].rearrange("p (t h) n -> p t (h n)", t=NT),
                              att_scratch[g].rearrange("(t p) n -> p t n", p=P)).then_inc(parts_in, 16)
            act.wait_ge(cmb_step, 5)
            a(cmb[:, 4:7, :], cmb[:, 1:4, :], ACT.Exp).then_inc(cmb_exp, 1)

            for d in range(2, KD):
                gate(0, d % 2, d)
                if d == 3:
                    act.wait_ge(a_tok_set, 1)
                    for c in range(2):
                        act.wait_ge(z_free[2 + c], 1 + 1)
                        a(acc[:, c, :], tmp[:, c, :], ACT.Copy).then_inc(acc_kept, 1)
            for c in range(2):
                act.wait_ge(at_mm, 2)
                a(a_hi[:, c, :], z[c][:], ACT.Copy).then_inc(ahi_set, 1)
            for d in range(KD):
                gate(1, d % 2, d)
                if d == 1:
                    for c in range(CT):
                        act.wait_ge(ln_xc, c + 1)
                        a(ln_sq4[:, c, :], u[:, c, PAD:PAD + T], ACT.Square).then_inc(ln_sq, 1)
                if d == 3:
                    act.wait_ge(ln_var, 1)
                    a(ln_dev[:, 0, :], z[3][:], ACT.Sqrt, bias=eps_ln[:, 0:1]).then_inc(z_free[3], 1)
                    for c in range(CT):
                        act.wait_ge(ln_xn, c + 1)
                        a(ln_sq4[:, c, :], u[:, c, PAD:PAD + T], ACT.Silu, bias=vcols[:, V_LNB + c:V_LNB + c + 1],
                          scale=vcols[:, V_LNG + c:V_LNG + c + 1]).then_inc(ln_f, 1)
            act.wait_ge(unit_done, U_BR + 24 + CREDIT)
            act.wait_ge(ln_f, CT)
            for c in range(CT):
                a(c_hi[:, c, :], ln_sq4[:, c, :], ACT.Copy).then_inc(ln_hi, 1)

            def merged_part(d):
                act.wait_ge(br_f, d + 1)
                a(merged_hi[:, d, :], tmp[:, d % 2, :], ACT.Copy).then_inc(br_hi, 1)

            for d in range(0, KD, 2):
                gate(2, 0, d)
                gate(2, 1, d + 1)
                if d == 0:
                    act.wait_ge(ln_lo, CT)
                merged_part(d)
                merged_part(d + 1)
            for d in range(KD - 2):
                act.wait_ge(unit_done, U_OUT + d + 1 + CREDIT)
                a(y_t[:, d, :], z[d % 2][:], ACT.Copy).then_inc(z_free[d % 2], 1)

            def last_y(s, half):
                if half == 0:
                    act.wait_ge(out_half, s + 1)
                else:
                    act.wait_ge(unit_done, U_OUT + 6 + s + 1 + CREDIT)
                at = slice(HALF * half, HALF * (half + 1))
                a(y_t[:, 6 + s, at], z[s][:, at], ACT.Copy).then_inc(y_copied, 1)

            def rms_post(t):
                act.wait_ge(n_yt, t + 1)
                unread = (sg if t < 2 else y_sum)[:, t % 2, :]
                a(rows3(unread), rows3(z[2 + t % 2][:]), ACT.Square, accum_out=sumsq[:, stat(S_POST + t)])\
                    .then_inc(n_sq1, 1)
                act.wait_ge(n_sq1, t + 1)
                a(std[:, stat(S_POST + t)], sumsq[:, stat(S_POST + t)], ACT.Sqrt, bias=eps_rms[:, 0:1], scale=1.0 / D)\
                    .then_inc(n_std1, 1)

            def rms_pre(t):
                act.wait_ge(n_x1, t + 1)
                if t >= 2:
                    act.wait_ge(n_xt, t - 1)
                a(rows3(sg[:, t % 2, :]), x1(t), ACT.Square, accum_out=sumsq[:, stat(S_PRE + t)]).then_inc(n_sq2, 1)
                act.wait_ge(n_sq2, t + 1)
                a(std[:, stat(S_PRE + t)], sumsq[:, stat(S_PRE + t)], ACT.Sqrt, bias=eps_rms[:, 0:1], scale=1.0 / D)\
                    .then_inc(n_std2, 1)

            def norm_hi(t):
                if t < NT - 2:
                    act.wait_ge(z_free[1], Z01_N[1] + t + 2)
                else:
                    act.wait_ge(z_free[t - 4], Z23_N + 4 + 2)
                a(h_hi[:, :, P * t:P * (t + 1)], rows3(f_ffn[:, t % 2, :]), ACT.Copy).then_inc(n_hi, 1)

            load_table(ACT.Sqrt, S_SPARE[2])
            last_y(0, 0)
            last_y(1, 0)
            last_y(0, 1)
            act.wait_ge(y_copied, 3)
            act.sem_inc(z_free[0], 1)
            rms_post(0)
            rms_post(1)
            last_y(1, 1)
            act.wait_ge(y_copied, 4)
            act.sem_inc(z_free[1], 1)
            for t in range(NT):
                rms_pre(t)
                if t:
                    norm_hi(t - 1)
                if t + 2 < NT:
                    rms_post(t + 2)
            norm_hi(NT - 1)
            load_table(ACT.Silu, S_SPARE[3])

            def hidden(r, j, act_slot, n):
                act.wait_ge(unit_done, r + 1 + CREDIT)
                act.wait_ge(z_free[1], Z01_F[1] + n)
                a(sg[:, j, :], z[0][:], ACT.Silu).then_inc(z_free[0], 1)
                act.wait_ge(z_free[1], Z01_F[1] + n + 2)
                a(act_hi[:, act_slot, j, :], tmp[:, j, :], ACT.Copy).then_inc(ff_hi, 1)

            act.wait_ge(n_lo, NT)
            for j in range(2):
                hidden(U_FFN + 2 * j, j, 0, j)
            with act.Fori(0, (CHUNKS - 1) // 2) as i:
                for s in range(2):
                    c = 2 * i + 1 + s
                    for j in range(2):
                        if j == 0:
                            act.wait_ge(unit_done, U_FFN - 2 + 6 * c + CREDIT)
                        hidden(U_FFN - 2 + 6 * c + 3 * j, j, (s + 1) % 2, 2 * c + j)
            load_table(ACT.Sqrt, S_SPARE[4])
            for t in range(NT):
                act.wait_ge(t_yt, t + 1)
                a(sg[:, t % 2, :], z[tail_z(t)][:], ACT.Square, accum_out=sumsq[:, stat(S_TAIL + t)]).then_inc(t_sq, 1)
                act.wait_ge(t_sq, t + 1)
                a(std[:, stat(S_TAIL + t)], sumsq[:, stat(S_TAIL + t)], ACT.Sqrt, bias=eps_rms[:, 0:1], scale=1.0 / D)\
                    .then_inc(t_std, 1)

        @block.vector
        def _(dve):
            for s, credit in ((m_olo, 1), (c_add, 1), (c_oev, 1), (tap_done, 1), (z_free[1], 1), (z_free[2], 1), (z_free[3], 1)):
                dve.sem_inc(s, credit)
            v = nc.vector

            def scaled(dst, src, scalar):
                return v.tensor_scalar(dst, src, scalar, None, ALU.mult)

            def tokens_scaled(j):
                dve.wait_ge(std_done, j + 1)
                v.reciprocal(rstd[:, stat(j)], std[:, stat(j)]).then_inc(rstd_done, 1)
                dve.wait_ge(rstd_done, j + 1)
                if j >= 2:
                    dve.wait_ge(xt_mm, j - 1)
                src = mem_tok[:, j, :] if j < 2 else x_tok[:, j - 2, :]
                scaled(xs0[:, j % 2, :], src, rstd[:, stat(j)]).then_inc(xs_done, 1)

            def tokens_gain(j):
                dve.wait_ge(xt_mm, j + 1)
                if j == 0:
                    dve.wait_ge(vec_set, 2)
                if j >= 2:
                    dve.wait_ge(flo_done, j - 1)
                col = V_MEM if j < 2 else V_MIX
                gain = vcols[:, col:col + KD].unsqueeze(2).to_broadcast([P, KD, P])
                v.tensor_tensor(f0[j % 2][:].rearrange("p (k n) -> p k n", k=KD),
                                z[2 + j % 2][:].rearrange("p (k n) -> p k n", k=KD), gain, ALU.mult).then_inc(f_done, 1)

            def tokens_lo(j):
                dve.wait_ge(fhi_done, j + 1)
                hi, lo = (mem_hi_t, mem_lo_t) if j < 2 else (h_hi, h_lo)
                at = slice(P * (j % 2 if j < 2 else j - 2), P * (j % 2 if j < 2 else j - 2) + P)
                v.tensor_tensor(lo[:, :, at], f0[j % 2][:].rearrange("p (k n) -> p k n", k=KD), hi[:, :, at],
                                ALU.subtract).then_inc(flo_done, 1)

            tokens_scaled(0)
            tokens_scaled(1)
            tokens_gain(0)
            tokens_gain(1)
            tokens_lo(0)
            tokens_lo(1)
            for j in range(2, 10):
                tokens_scaled(j)
                tokens_gain(j)
                if j > 2:
                    tokens_lo(j - 1)
            tokens_lo(9)
            v.memset(u[:, :, 0:PAD], 0.0).then_inc(u_pad, 1)
            v.memset(u[:, :, PAD + T:U_W], 0.0).then_inc(u_pad, 1)

            dve.wait_ge(vmem_set, 1)
            dve.wait_ge(z_free[0], 6 + 1)
            dve.wait_ge(z_free[1], 6 + 1)
            with dve.Fori(0, MEM_HEADS) as h:
                dve.wait_ge(m_pv, 2 * h + 2)
                scaled(q_cur[:], q_mem[:, bass.ds(h, 1), :].rearrange("p a t -> p (a t)"), 1.0)
                scaled(v_cur[:], v_mem[:, :, bass.ds(h, 1), :].rearrange("p c a n -> p c (a n)"), 1.0)\
                    .then_inc(m_cur, 1)
                for step in range(10):
                    if step < 8:
                        t = step
                        dve.wait_ge(m_qk, 8 * h + t + 1)
                        v.tensor_reduce(mstat[:, t % 2, 0:1], s_bank[:, t % 2, 0:N_MEM], X, ALU.max, negate=True)\
                            .then_inc(m_max, 1)
                        dve.wait_ge(m_exp, 8 * h + t + 3)
                        v.reciprocal(mstat[:, t % 2, 2:3], mstat[:, t % 2, 1:2]).then_inc(m_rden, 1)
                        dve.wait_ge(m_rden, 8 * h + t + 1)
                        scaled(p_mem[:, t % 2, :], p_mem[:, t % 2, :], mstat[:, t % 2, 2:3]).then_inc(m_pn, 1)
                    if step in (6, 9):
                        half = (step - 6) // 3
                        dve.wait_ge(m_pv, 2 * h + half + 3)
                        at = slice(HALF * half, HALF * (half + 1))
                        hi = m_hi[:, bass.ds(h, 1), at].rearrange("p a t -> p (a t)")
                        lo = m_lo[:, bass.ds(h, 1), at].rearrange("p a t -> p (a t)")
                        scaled(hi, o_bank, 1.0).then_inc(m_ohi, 1)
                        dve.wait_ge(m_ohi, 2 * h + half + 1)
                        v.tensor_tensor(lo, o_bank, hi, ALU.subtract).then_inc(m_olo, 1)
                dve.wait_ge(unit_done, U_CONV + 2 * h + 2 + CREDIT)
                dve.wait_ge(z_free[0], 6 + h + 2)
                v.tensor_tensor(u[:, bass.ds(h, 1), PAD:PAD + T].rearrange("p a t -> p (a t)"), z[1][:], sg_conv[:],
                                ALU.mult).then_inc(z_free[1], 1)

            dve.wait_ge(tables_in, 32)
            v.memset(bias2[0:64, :, 64:P], NEG).then_inc(bias_cut, 1)
            v.memset(bias2[64:P, :, 0:64], NEG).then_inc(bias_cut, 1)
            dve.wait_ge(bias_cut, 2)

            def conv_start(c):
                dve.wait_ge(tap_done, (TAPS + 1) * c + 1)
                v.tensor_copy(conv_sum[:], vcols[:, V_DWB + c:V_DWB + c + 1].to_broadcast([P, T])).then_inc(tap_done, 1)

            def conv_taps(c, first, tap, count):
                for n in range(count):
                    dve.wait_ge(tap_done, (TAPS + 1) * c + first + n + 1)
                    last = isinstance(first, int) and first + n == TAPS
                    v.scalar_tensor_tensor(u[:, c, PAD:PAD + T] if last else conv_sum[:],
                                           u[:, c, bass.ds(tap + n, T)], taps[:, bass.ds(tap + n, 1), c],
                                           conv_sum[:], ALU.mult, ALU.add).then_inc(tap_done, 1)

            def dilated_pair(g, pair, sent_before, conv_tile, conv_op, tap, per_step, op_count):
                tile = 8 * pair
                d = DILATIONS[g]
                n = P if g == 2 else 2 * P
                head = 2 * (pair - 2 * g)
                for j in range(3):
                    dve.wait_ge(z_free[j % 2], (Z0_QKV + 2 * pair + 2, Z1_QKV + pair + 2, Z0_QKV + 2 * pair + 3)[j])
                    if d == 1:
                        dst, src = cur[:, j, :], nxt[:, j, :]
                    else:
                        dst = cur[:, j, :].rearrange("p (r l) -> p r l", r=d)
                        src = nxt[:, j, :].rearrange("p (l r) -> p r l", r=d)
                    v.tensor_copy(dst, src).then_inc(c_cur, 1)
                for step in range(10):
                    if step < 8:
                        t = step
                        dve.wait_ge(c_qk, tile + t + 1)
                        dve.wait_ge(c_exp, tile + t + 1)
                        if g == 2:
                            bias = bias2[:, bass.ds(head, 2), :]
                        else:
                            col = P - window(g, t)[1]
                            bias = bias01[:, bass.ds(SLOTS_H * g + head, 2), col:col + n]
                        v.tensor_tensor(sbias[:, t % 2, :, 0:n], s_bank[:, :, 0:n], bias, ALU.add).then_inc(c_add, 1)
                        dve.wait_ge(c_add, tile + t + 2)
                        if t % 4 == 0:
                            dve.wait_ge(heads_sent[t // 4], 16 * (1 + sent_before))
                        v.tensor_reduce(heads_out[:, t, :, ATT_E + 1:ATT_E + 2], sbias[:, t % 2, :, 0:n], X, ALU.max,
                                        negate=True).then_inc(c_max, 1)
                    if step >= 2:
                        t = step - 2
                        dve.wait_ge(c_pv, tile + t + 3)
                        v.tensor_copy(heads_out[:, t, :, 0:ATT_E], o_bank[:, 0:2 * ATT_E].rearrange(
                            "p (h e) -> p h e", h=2)).then_inc(c_oev, 1)
                    conv_taps(conv_tile, conv_op + per_step * step, tap + per_step * step,
                              max(min(per_step, op_count - per_step * step), 0))

            for g in range(2):
                conv_start(g)
                with dve.Fori(0, 2) as i:
                    dilated_pair(g, 2 * g + i, 2 * g + (1 + g) * i, g, 1 + PAD * i, (PAD + 1) * i, 2, PAD)
                conv_taps(g, TAPS, PAD, 1)
            conv_start(2)
            dilated_pair(2, 4, 6, 2, 1, 0, 2, PAD)
            dilated_pair(2, 5, 8, 2, 1 + PAD, PAD + 1, 1, 8)

            def gated(b, i, j, q, dst, z01, z23):
                if q == 0:
                    dve.wait_ge(proj_half, 4 * b + 2 * i + j + 1)
                else:
                    dve.wait_ge(unit_done, U_BR + 12 * b + 6 * i + 3 * j + 3 + CREDIT)
                dve.wait_ge(z_free[q], z01[q] + 2 * i + j + 2)
                v.tensor_tensor(dst, z[2 + q][:], sg[:, q, :], ALU.mult).then_inc(z_free[2 + q], 1)

            steps = [0]

            def combine(op, *args):
                op(*args).then_inc(cmb_step, 1)
                steps[0] += 1
                dve.wait_ge(cmb_step, steps[0])

            def col(g, c):
                return parts[:, g, :, c]

            dve.wait_ge(parts_in, 48)
            combine(v.tensor_tensor, cmb[:, 0, :], col(0, ATT_E + 1), col(1, ATT_E + 1), ALU.min)
            combine(v.tensor_tensor, cmb[:, 0, :], cmb[:, 0, :], col(2, ATT_E + 1), ALU.min)
            for g in range(3):
                combine(v.tensor_tensor, cmb[:, 1 + g, :], cmb[:, 0, :], col(g, ATT_E + 1), ALU.subtract)
            for q in range(2):
                gated(0, 0, 0, q, tmp[:, q, :], Z01_BR, 0)
            dve.wait_ge(cmb_exp, 1)
            for g in range(3):
                combine(v.tensor_tensor, cmb[:, 1 + g, :], cmb[:, 4 + g, :], col(g, ATT_E), ALU.mult)
            combine(v.tensor_tensor, cmb[:, 7, :], cmb[:, 1, :], cmb[:, 2, :], ALU.add)
            combine(v.tensor_tensor, cmb[:, 7, :], cmb[:, 7, :], cmb[:, 3, :], ALU.add)
            combine(v.reciprocal, cmb[:, 8, :], cmb[:, 7, :])
            total = a_tok[:].rearrange("p t (h e) -> p (t h) e", h=SLOTS_H)
            for g in range(3):
                combine(v.tensor_tensor, cmb[:, 1 + g, :], cmb[:, 4 + g, :], cmb[:, 8, :], ALU.mult)
                share = cmb[:, 1 + g, :].unsqueeze(2).to_broadcast([P, NT * SLOTS_H, ATT_E])
                combine(v.tensor_tensor, total if g == 0 else wsum[:], parts[:, g, :, 0:ATT_E], share, ALU.mult)
                if g == 1:
                    combine(v.tensor_tensor, total, total, wsum[:], ALU.add)
            v.tensor_tensor(total, total, wsum[:], ALU.add).then_inc(a_tok_set, 1)

            ops = [(2, n) for n in range(PAD + 9, TAPS + 1)] + [(3, n) for n in range(TAPS + 1)]
            share = -(-len(ops) // 5)
            for n in range(2, KD):
                gated(0, n // 4, n % 4 // 2, n % 2, acc[:, n, :], Z01_BR, 0)
                if n == 6:
                    for c in range(2):
                        dve.wait_ge(ahi_set, c + 1)
                        v.tensor_tensor(a_lo[:, c, :], z[c][:], a_hi[:, c, :], ALU.subtract).then_inc(z_free[c], 1)
                for c, op in () if n == 6 else ops[share * (n - 2 - n // 7):share * (n - 1 - n // 7)]:
                    if op == 0:
                        conv_start(c)
                    else:
                        conv_taps(c, op, PAD if op == TAPS else op - (op <= PAD), 1)
            dve.wait_ge(acc_kept, 2)

            def summed(b, i, j, q, dst, z01, z23, done):
                gated(b, i, j, q, tmp[:, q, :], z01, z23)
                dve.wait_ge(z_free[2 + q], z23 + 2 * i + j + 2)
                acc_d = acc[:, bass.ds(4 * i + 2 * j + q, 1), :].rearrange("p a t -> p (a t)")
                v.tensor_tensor(acc_d if dst is None else dst, acc_d, tmp[:, q, :], ALU.add).then_inc(done, 1)

            def ln_scale(c):
                v.tensor_tensor(u[:, c, PAD:PAD + T], u[:, c, PAD:PAD + T], ln_dev[:, 1, :], ALU.mult).then_inc(ln_xn, 1)

            def ln_low(c):
                dve.wait_ge(ln_hi, c + 1)
                v.tensor_tensor(c_lo[:, c, :], ln_sq4[:, c, :], c_hi[:, c, :], ALU.subtract).then_inc(ln_lo, 1)

            def ln_total(k, parts, scratch):
                total = ln_sum[:, k, :]
                v.tensor_tensor(total, parts[0], parts[1], ALU.add).then_inc(ln_add, 1)
                v.tensor_tensor(scratch, parts[2], parts[3], ALU.add).then_inc(ln_add, 1)
                dve.wait_ge(ln_add, 3 * k + 2)
                v.tensor_tensor(total, total, scratch, ALU.add).then_inc(ln_add, 1)

            dve.wait_ge(unit_done, U_BR + 12 + CREDIT)
            dve.wait_ge(tap_done, (TAPS + 1) * CT + 1)
            ln_total(0, [u[:, c, PAD:PAD + T] for c in range(CT)], ln_sum[:, 1, :])
            for n in range(KD):
                summed(1, n // 4, n % 4 // 2, n % 2, None, Z01_B1, 5 if n >= 2 else 4, br_tmp)
                if n == 1:
                    dve.wait_ge(ln_mean, 1)
                    for c in range(CT):
                        v.tensor_tensor(u[:, c, PAD:PAD + T], u[:, c, PAD:PAD + T], z[2][:], ALU.subtract)\
                            .then_inc(ln_xc, 1)
                    dve.wait_ge(ln_xc, CT)
                    dve.sem_inc(z_free[2], 1)
                    dve.wait_ge(ln_sq, CT)
                    ln_total(1, [ln_sq4[:, c, :] for c in range(CT)], ln_sq4[:, 2, :])
                    dve.wait_ge(z_free[3], 4 + 1 + 2)
                    v.reciprocal(ln_dev[:, 1, :], ln_dev[:, 0, :]).then_inc(ln_rstd, 1)
                    dve.wait_ge(ln_rstd, 1)
                    for c in range(CT):
                        ln_scale(c)
            for c in range(CT):
                ln_low(c)
            with dve.Fori(0, 2) as i:
                for j in range(2):
                    for q in range(2):
                        n = 4 * i + 2 * j + q
                        summed(2, i, j, q, tmp[:, q, :], Z01_B2, Z23_B2, br_f)
                        dve.wait_ge(br_hi, n + 1)
                        v.tensor_tensor(merged_lo[:, bass.ds(n, 1), :].rearrange("p a t -> p (a t)"), tmp[:, q, :],
                                        merged_hi[:, bass.ds(n, 1), :].rearrange("p a t -> p (a t)"),
                                        ALU.subtract).then_inc(br_lo, 1)

            def norm_post(t):
                dve.wait_ge(n_std1, t + 1)
                v.reciprocal(rstd[:, stat(S_POST + t)], std[:, stat(S_POST + t)]).then_inc(n_rstd1, 1)
                dve.wait_ge(n_rstd1, t + 1)
                if t == 4:
                    dve.wait_ge(y_copied, 4)
                v.scalar_tensor_tensor(x1(t), rows3(z[2 + t % 2][:]), rstd[:, stat(S_POST + t)], rows3(post_gain[:]),
                                       ALU.mult, ALU.mult).then_inc(n_post, 1)
                dve.wait_ge(n_post, t + 1)
                dve.sem_inc(z_free[2 + t % 2], 1)

            def norm_pre(t):
                dve.wait_ge(n_std2, t + 1)
                v.reciprocal(rstd[:, stat(S_PRE + t)], std[:, stat(S_PRE + t)]).then_inc(n_rstd2, 1)
                dve.wait_ge(n_rstd2, t + 1)
                scaled(rows3(sg[:, t % 2, :]), x1(t), rstd[:, stat(S_PRE + t)]).then_inc(n_xs, 1)

            def norm_gain(t):
                dve.wait_ge(n_xt, t + 1)
                if t == 0:
                    dve.wait_ge(unit_done, U_FFN + CREDIT)
                k = 1 if t < NT - 2 else t - 4
                gain = vcols[:, V_FFN:V_FFN + KD].unsqueeze(2).to_broadcast([P, KD, P])
                v.tensor_tensor(rows3(f_ffn[:, t % 2, :]), rows3(z[k][:]), gain, ALU.mult).then_inc(z_free[k], 1)

            def norm_lo(t):
                dve.wait_ge(n_hi, t + 1)
                at = slice(P * t, P * (t + 1))
                v.tensor_tensor(h_lo[:, :, at], rows3(f_ffn[:, t % 2, :]), h_hi[:, :, at], ALU.subtract).then_inc(n_lo, 1)

            dve.wait_ge(gain_in, 16)
            norm_post(0)
            for t in range(NT):
                if t + 1 < NT:
                    norm_post(t + 1)
                norm_pre(t)
                if t:
                    norm_lo(t - 1)
                norm_gain(t)
            norm_lo(NT - 1)

            def hidden(r, j, act_slot, n):
                dve.wait_ge(unit_done, r + 2 + CREDIT)
                dve.wait_ge(z_free[0], Z01_F[0] + n + 2)
                v.tensor_tensor(tmp[:, j, :], z[1][:], sg[:, j, :], ALU.mult).then_inc(z_free[1], 1)
                dve.wait_ge(ff_hi, n + 1)
                v.tensor_tensor(act_lo[:, act_slot, j, :], tmp[:, j, :], act_hi[:, act_slot, j, :], ALU.subtract)\
                    .then_inc(ff_lo, 1)

            def ffn_out(r, m, half):
                for q in range(4):
                    if q < 3:
                        dve.wait_ge(ff_y, 3 * m + q + 1)
                    else:
                        dve.wait_ge(unit_done, r + 1 + CREDIT)
                    y = y_sum[:, 4 * half + q, :]
                    v.tensor_tensor(y, z[2 + q % 2][:], y, ALU.add).then_inc(z_free[2 + q % 2], 1)

            for j in range(2):
                hidden(U_FFN + 2 * j, j, 0, j)
            dve.wait_ge(y_zero, 1)
            with dve.Fori(0, (CHUNKS - 1) // 2) as i:
                for s in range(2):
                    c = 2 * i + 1 + s
                    for j in range(2):
                        r = U_FFN - 2 + 6 * c + 3 * j
                        hidden(r, j, (s + 1) % 2, 2 * c + j)
                        ffn_out(r + 2, 2 * (c - 1) + j, j)
            dve.wait_ge(gain_in, 32)

            def tail(t):
                dve.wait_ge(t_std, t + 1)
                v.reciprocal(rstd[:, stat(S_TAIL + t)], std[:, stat(S_TAIL + t)]).then_inc(t_rstd, 1)
                dve.wait_ge(t_rstd, t + 1)
                if t >= 2:
                    dve.wait_ge(t_sum[t % 2], t // 2)
                v.scalar_tensor_tensor(rows3(tmp[:, t % 2, :]), rows3(z[tail_z(t)][:]), rstd[:, stat(S_TAIL + t)],
                                       rows3(post_gain[:]), ALU.mult, ALU.mult).then_inc(t_t1, 1)
                dve.wait_ge(t_t1, t + 1)
                dve.sem_inc(z_free[tail_z(t)], 1)
                if t % 2:
                    v.tensor_tensor(x1(t), x1(t), rows3(tmp[:, t % 2, :]), ALU.add).then_inc(t_sum[1], 1)

            for n in range(2 * KD):
                half, d = n // KD, n % KD
                dve.wait_ge(last_part, n + 1)
                y = y_sum[:, d, HALF * half:HALF * (half + 1)]
                v.tensor_tensor(y, last_bank(n), y, ALU.add).then_inc(last_added, 1)
                if n - 2 in TAIL_TILES:
                    tail(TAIL_TILES.index(n - 2))
            for t in range(NT):
                if t >= 4 or TAIL_TILES[t] + 2 >= 2 * KD:
                    tail(t)


INPUTS = ("x", "mem", "rel_bias", "norm_mix_pre", "w_in", "b_gate", "conv_dw", "conv_dw_bias", "conv_ln_g",
          "conv_ln_b", "w_conv_out", "w_att_out", "norm_mem", "w_mem_kv", "w_mem_out", "w_out", "norm_mix_post",
          "norm_ffn_pre", "w_ffn_in", "w_ffn_out", "norm_ffn_post")


def bucket_table():
    import numpy as np
    import math
    half, exact, largest = 16, 8, 1024
    table = np.zeros((3, 33, REL), np.float32)
    for g, dilation in enumerate(DILATIONS):
        for col in range(REL):
            off = col - REL // 2
            if abs(off) > RADIUS:
                table[g, 32, col] = NEG
                continue
            n = abs(off * dilation)
            bucket = n
            if n >= exact:
                bucket = min(exact + int(math.log(n / exact) / math.log(largest / exact) * (half - exact)), half - 1)
            table[g, bucket + (half if off > 0 else 0), col] = 1.0
    return table


def kernel(**inputs):
    import numpy as np
    import concourse.bacc as bacc
    from concourse.bass_utils import run_bass_kernel_spmd

    nc = bacc.Bacc("TRN2", target_bir_lowering=False, num_devices=1)
    arrays = {name: np.ascontiguousarray(inputs[name]) for name in INPUTS}
    arrays["identity"] = np.eye(P, dtype=np.float32)
    arrays["bucket_hot"] = bucket_table()
    args = [nc.dram_tensor(f"in_{name}", a.shape, mybir.dt.from_np(a.dtype), kind="ExternalInput").ap()
            for name, a in arrays.items()]
    result = nc.dram_tensor("result", (1, T, D), mybir.dt.float32, kind="ExternalOutput").ap()
    hybrid_layer(nc, *args, result)
    ran = run_bass_kernel_spmd(nc, [{f"in_{name}": a for name, a in arrays.items()}], core_ids=[0])
    return ran.results[0]["result"]
```
